# Optimizing a Trainium2 kernel written in Bass

```python
import math
import jax, jax.numpy as jnp
from jax import lax
import numpy as np

D_MODEL = 1024
BATCH = 1
SEQ = 256
DEPTH = 1

HEAD_DIM = 64
N_HEADS_MOBA = 8
N_HEADS_SB = 8
MOBA_WIDTH = N_HEADS_MOBA * HEAD_DIM
SB_WIDTH = N_HEADS_SB * HEAD_DIM
N_BRANCHES = 2
IN_WIDTH = 3 * MOBA_WIDTH + 3 * SB_WIDTH + N_BRANCHES * D_MODEL
MOBA_BLOCK = 256
MOBA_TOPK = 3
MOBA_Q_CHUNK = 16
SB_Q_BLOCK = 128
D_FF = 2816
CONV_WIDTH = 3
REL_BUCKETS = 32
REL_MAX_DIST = 128
NORM_EPS = 1e-6
NEG_INF = -1e30


def rms_norm(x, g):
    xf = x.astype(jnp.float32)
    y = xf * lax.rsqrt(jnp.mean(xf * xf, axis=-1, keepdims=True) + NORM_EPS)
    return (y * g.astype(jnp.float32)).astype(x.dtype)

def modulate(h, shift, scale):
    return h * (1.0 + scale[:, None, :]) + shift[:, None, :]

def to_heads(t, n_heads):
    b, s, _ = t.shape
    return t.reshape(b, s, n_heads, HEAD_DIM).transpose(0, 2, 1, 3)

def merge_heads(t):
    b, h, s, hd = t.shape
    return t.transpose(0, 2, 1, 3).reshape(b, s, h * hd)

def t5_bucket(rel):
    n = jnp.maximum(rel, 0)
    max_exact = REL_BUCKETS // 2
    n_f = jnp.maximum(n, max_exact).astype(jnp.float32)
    large = max_exact + (jnp.log(n_f / max_exact) / math.log(REL_MAX_DIST / max_exact)
                         * (REL_BUCKETS - max_exact)).astype(jnp.int32)
    large = jnp.minimum(large, REL_BUCKETS - 1)
    return jnp.where(n < max_exact, n, large)

def moba_attention(q, k, v, rel_table):
    b, h, s, hd = q.shape
    n_blk = -(-s // MOBA_BLOCK)
    s_pad = n_blk * MOBA_BLOCK
    pad = ((0, 0), (0, 0), (0, s_pad - s), (0, 0))
    q = jnp.pad(q, pad)
    k = jnp.pad(k, pad)
    v = jnp.pad(v, pad)
    k_blk = k.reshape(b, h, n_blk, MOBA_BLOCK, hd)
    v_blk = v.reshape(b, h, n_blk, MOBA_BLOCK, hd)
    k_mean = jnp.mean(k_blk.astype(jnp.float32), axis=3).astype(q.dtype)
    n_sel = min(MOBA_TOPK, n_blk)
    scale = hd ** -0.5
    n_chunks = s_pad // MOBA_Q_CHUNK
    q_chunks = jnp.moveaxis(q.reshape(b, h, n_chunks, MOBA_Q_CHUNK, hd), 2, 0)
    b_idx = jnp.arange(b)[:, None, None, None]
    h_idx = jnp.arange(h)[None, :, None, None]
    offs = jnp.arange(MOBA_BLOCK)
    blk_ids = jnp.arange(n_blk)

    def chunk(args):
        qc, ci = args
        q_start = ci * MOBA_Q_CHUNK
        q_pos = q_start + jnp.arange(MOBA_Q_CHUNK)
        own = q_start // MOBA_BLOCK
        gate = jnp.einsum('bhqd,bhnd->bhqn', qc, k_mean).astype(jnp.float32)
        gate = jnp.where(blk_ids < own, gate, NEG_INF)
        _, sel = lax.top_k(gate, n_sel)
        sel_ok = sel < own
        k_sel = k_blk[b_idx, h_idx, sel]
        v_sel = v_blk[b_idx, h_idx, sel]
        s_sel = jnp.einsum('bhqd,bhqnkd->bhqnk', qc, k_sel).astype(jnp.float32) * scale
        rel_sel = q_pos[:, None, None] - (sel[..., None] * MOBA_BLOCK + offs)
        bias_sel = rel_table[h_idx[..., None], t5_bucket(rel_sel)]
        s_sel = jnp.where(sel_ok[..., None], s_sel + bias_sel, NEG_INF)
        k_own = lax.dynamic_slice_in_dim(k, own * MOBA_BLOCK, MOBA_BLOCK, axis=2)
        v_own = lax.dynamic_slice_in_dim(v, own * MOBA_BLOCK, MOBA_BLOCK, axis=2)
        s_own = jnp.einsum('bhqd,bhkd->bhqk', qc, k_own).astype(jnp.float32) * scale
        rel_own = q_pos[:, None] - (own * MOBA_BLOCK + offs)[None, :]
        bias_own = rel_table[:, t5_bucket(rel_own)]
        s_own = jnp.where(rel_own >= 0, s_own + bias_own, NEG_INF)
        logits = jnp.concatenate(
            [s_sel.reshape(b, h, MOBA_Q_CHUNK, n_sel * MOBA_BLOCK), s_own], axis=-1)
        p = jax.nn.softmax(logits, axis=-1).astype(v.dtype)
        p_sel = p[..., :n_sel * MOBA_BLOCK].reshape(b, h, MOBA_Q_CHUNK, n_sel, MOBA_BLOCK)
        p_own = p[..., n_sel * MOBA_BLOCK:]
        return (jnp.einsum('bhqnk,bhqnkd->bhqd', p_sel, v_sel)
                + jnp.einsum('bhqk,bhkd->bhqd', p_own, v_own))

    out = lax.map(chunk, (q_chunks, jnp.arange(n_chunks)))
    return jnp.moveaxis(out, 0, 2).reshape(b, h, s_pad, hd)[:, :, :s]

def stick_breaking_attention(q, k, v):
    b, h, s, hd = q.shape
    n_qb = s // SB_Q_BLOCK
    scale = hd ** -0.5
    k_pos = jnp.arange(s)
    q_blocks = jnp.moveaxis(q.reshape(b, h, n_qb, SB_Q_BLOCK, hd), 2, 0)

    def block(args):
        qb, bi = args
        q_pos = bi * SB_Q_BLOCK + jnp.arange(SB_Q_BLOCK)
        z = jnp.einsum('bhqd,bhkd->bhqk', qb, k).astype(jnp.float32) * scale
        past = k_pos[None, :] < q_pos[:, None]
        log_beta = jax.nn.log_sigmoid(z)
        log_keep = jnp.where(past, jax.nn.log_sigmoid(-z), 0.0)
        log_later = lax.cumsum(log_keep, axis=3, reverse=True) - log_keep
        a = jnp.where(past, jnp.exp(log_beta + log_later), 0.0)
        return jnp.einsum('bhqk,bhkd->bhqd', a.astype(v.dtype), v)

    out = lax.map(block, (q_blocks, jnp.arange(n_qb)))
    return jnp.moveaxis(out, 0, 2).reshape(b, h, s, hd)

def causal_depthwise_conv(u, w, bias):
    ch = u.shape[-1]
    out = lax.conv_general_dilated(
        u, w[:, None, :], window_strides=(1,), padding=[(CONV_WIDTH - 1, 0)],
        dimension_numbers=('NWC', 'WIO', 'NWC'), feature_group_count=ch)
    return out + bias

def first_inputs(seed: int = 0) -> dict:
    key = jax.random.key(seed)
    ks = jax.random.split(key, 16)
    f32 = jnp.float32
    nrm = lambda k, shp, sc: jax.random.normal(k, shp, f32) * sc
    return {
        'x': nrm(ks[0], (BATCH, SEQ, D_MODEL), 1.0),
        'c': nrm(ks[1], (BATCH, D_MODEL), 1.0),
        'w_ada': nrm(ks[2], (DEPTH, D_MODEL, 6 * D_MODEL), D_MODEL ** -0.5),
        'b_ada': nrm(ks[3], (DEPTH, 6 * D_MODEL), 0.02),
        'g_mix': 1.0 + nrm(ks[4], (DEPTH, D_MODEL), 0.05),
        'w_in': nrm(ks[5], (DEPTH, D_MODEL, IN_WIDTH), D_MODEL ** -0.5),
        'w_br_moba': nrm(ks[6], (DEPTH, MOBA_WIDTH, D_MODEL), MOBA_WIDTH ** -0.5),
        'w_br_sb': nrm(ks[7], (DEPTH, SB_WIDTH, D_MODEL), SB_WIDTH ** -0.5),
        'w_out': nrm(ks[8], (DEPTH, D_MODEL, D_MODEL), D_MODEL ** -0.5),
        'rel_bias': nrm(ks[9], (N_HEADS_MOBA, REL_BUCKETS), 0.5),
        'g_ffn': 1.0 + nrm(ks[10], (DEPTH, D_MODEL), 0.05),
        'w_up': nrm(ks[11], (DEPTH, D_MODEL, 2 * D_FF), D_MODEL ** -0.5),
        'w_conv': nrm(ks[12], (DEPTH, CONV_WIDTH, 2 * D_FF), CONV_WIDTH ** -0.5),
        'b_conv': nrm(ks[13], (DEPTH, 2 * D_FF), 0.02),
        'w_down': nrm(ks[14], (DEPTH, D_FF, D_MODEL), D_FF ** -0.5),
        'g_final': 1.0 + nrm(ks[15], (D_MODEL,), 0.05),
    }

def first_block(x, c, w_ada, b_ada, g_mix, w_in, w_br_moba, w_br_sb, w_out, rel_bias,
              g_ffn, w_up, w_conv, b_conv, w_down, g_final):
    splits = list(np.cumsum([MOBA_WIDTH, MOBA_WIDTH, MOBA_WIDTH, SB_WIDTH, SB_WIDTH, SB_WIDTH]))
    c_act = jax.nn.silu(c)
    for l in range(DEPTH):
        mod = c_act @ w_ada[l] + b_ada[l]
        sh_m, sc_m, gt_m, sh_f, sc_f, gt_f = jnp.split(mod, 6, axis=-1)
        h = modulate(rms_norm(x, g_mix[l]), sh_m, sc_m)
        proj = jnp.einsum('bsd,de->bse', h, w_in[l])
        qa, ka, va, qb, kb, vb, gate_logits = jnp.split(proj, splits, axis=-1)
        oa = moba_attention(to_heads(qa, N_HEADS_MOBA), to_heads(ka, N_HEADS_MOBA),
                            to_heads(va, N_HEADS_MOBA), rel_bias)
        ob = stick_breaking_attention(to_heads(qb, N_HEADS_SB), to_heads(kb, N_HEADS_SB),
                                      to_heads(vb, N_HEADS_SB))
        ya = jnp.einsum('bse,ed->bsd', merge_heads(oa), w_br_moba[l])
        yb = jnp.einsum('bse,ed->bsd', merge_heads(ob), w_br_sb[l])
        gates = jax.nn.sigmoid(gate_logits.astype(jnp.float32)).astype(x.dtype)
        g_a, g_b = jnp.split(gates, 2, axis=-1)
        mixed = jnp.einsum('bsd,de->bse', g_a * ya + g_b * yb, w_out[l])
        x = x + gt_m[:, None, :] * mixed
        h2 = modulate(rms_norm(x, g_ffn[l]), sh_f, sc_f)
        u = jnp.einsum('bsd,df->bsf', h2, w_up[l])
        u = causal_depthwise_conv(u, w_conv[l], b_conv[l])
        u_val, u_gate = jnp.split(u, 2, axis=-1)
        y = jnp.einsum('bsf,fd->bsd', jax.nn.gelu(u_gate) * u_val, w_down[l])
        x = x + gt_f[:, None, :] * y
    return rms_norm(x, g_final)


DEPTH_2 = 2

CHUNK = 64
ROPE_THETA = 10000.0
EPS = 1e-6
Q_BLOCK = 128
DSA_Q_BLOCK = 32
A_HEADS = D_MODEL // (4 * HEAD_DIM)
A_VDIM = 2 * HEAD_DIM
B_HEADS = D_MODEL // (2 * HEAD_DIM)
IDX_HEADS = 8
IDX_DIM = 32
TOPK_MAX = 256
C_HEADS = D_MODEL // HEAD_DIM
C_LEFT_CHUNKS = 8
MAX_REL = 256
REL_TABLE = MAX_REL + CHUNK

MIX_WIDTH = A_HEADS * A_VDIM + B_HEADS * HEAD_DIM
EVEN_SIZES = (2 * A_HEADS * HEAD_DIM, 2 * A_HEADS * HEAD_DIM, A_HEADS * A_VDIM,
              B_HEADS * HEAD_DIM, B_HEADS * HEAD_DIM, B_HEADS * HEAD_DIM,
              IDX_HEADS * IDX_DIM, IDX_DIM, IDX_HEADS)
EVEN_PROJ = sum(EVEN_SIZES)
EVEN_SPLITS = [sum(EVEN_SIZES[:i + 1]) for i in range(len(EVEN_SIZES) - 1)]


def rmsnorm(x, g):
    xf = x.astype(jnp.float32)
    y = xf * lax.rsqrt(jnp.mean(xf * xf, axis=-1, keepdims=True) + EPS)
    return (y * g.astype(jnp.float32)).astype(x.dtype)

def rope_tables(seq, dim):
    inv = ROPE_THETA ** (-jnp.arange(0, dim, 2, dtype=jnp.float32) / dim)
    ang = jnp.arange(seq, dtype=jnp.float32)[:, None] * inv[None, :]
    return jnp.cos(ang), jnp.sin(ang)

def apply_rope(x, cos, sin):
    xf = x.astype(jnp.float32)
    x1, x2 = jnp.split(xf, 2, axis=-1)
    c = cos[:, None, :]
    s = sin[:, None, :]
    return jnp.concatenate([x1 * c - x2 * s, x2 * c + x1 * s], axis=-1).astype(x.dtype)

def masked_softmax(s, mask):
    return jax.nn.softmax(jnp.where(mask, s, -jnp.inf), axis=-1)

def swiglu(h, wg, wu, wd):
    return (jax.nn.silu(h @ wg) * (h @ wu)) @ wd

def diff_attention(q, k, v, lam, subln, lambda_init):
    B_, S_ = q.shape[0], q.shape[1]
    nb = S_ // Q_BLOCK
    qb = q.reshape(B_, nb, Q_BLOCK, A_HEADS, 2, HEAD_DIM).swapaxes(0, 1)
    kf = k.astype(jnp.float32)
    vf = v.astype(jnp.float32)
    kchunk = jnp.arange(S_) // CHUNK
    scale = HEAD_DIM ** -0.5

    def one_block(args):
        bi, qblk = args
        qpos = bi * Q_BLOCK + jnp.arange(Q_BLOCK)
        mask = kchunk[None, :] <= (qpos // CHUNK)[:, None]
        s = jnp.einsum('bqhcd,bkhcd->bhcqk', qblk.astype(jnp.float32), kf) * scale
        p = masked_softmax(s, mask)
        w = p[:, :, 0] - lam * p[:, :, 1]
        return jnp.einsum('bhqk,bkhe->bqhe', w, vf)

    o = lax.map(one_block, (jnp.arange(nb), qb))
    o = o.swapaxes(0, 1).reshape(B_, S_, A_HEADS, A_VDIM)
    o = rmsnorm(o, subln) * (1.0 - lambda_init)
    return o.reshape(B_, S_, A_HEADS * A_VDIM).astype(v.dtype)

def dsa_attention(q, k, v, qi, ki, wi, topk):
    B_, S_ = q.shape[0], q.shape[1]
    nb = S_ // DSA_Q_BLOCK
    qb = q.reshape(B_, nb, DSA_Q_BLOCK, B_HEADS, HEAD_DIM).swapaxes(0, 1)
    qib = qi.reshape(B_, nb, DSA_Q_BLOCK, IDX_HEADS, IDX_DIM).swapaxes(0, 1)
    wib = wi.reshape(B_, nb, DSA_Q_BLOCK, IDX_HEADS).swapaxes(0, 1)
    kf = k.astype(jnp.float32)
    vf = v.astype(jnp.float32)
    kif = ki.astype(jnp.float32)
    kchunk = jnp.arange(S_) // CHUNK
    scale = HEAD_DIM ** -0.5
    gather = jax.vmap(lambda kk, ii: kk[ii])

    def one_block(args):
        bi, qblk, qiblk, wiblk = args
        qpos = bi * DSA_Q_BLOCK + jnp.arange(DSA_Q_BLOCK)
        qchunk = qpos // CHUNK
        rel = jax.nn.relu(jnp.einsum('bqhd,bkd->bqhk', qiblk.astype(jnp.float32), kif))
        score = jnp.einsum('bqhk,bqh->bqk', rel, wiblk.astype(jnp.float32))
        mask = kchunk[None, :] <= qchunk[:, None]
        score = jnp.where(mask[None], score, -jnp.inf)
        _, idx = lax.top_k(score, topk)
        valid = (idx // CHUNK) <= qchunk[None, :, None]
        kg = gather(kf, idx)
        vg = gather(vf, idx)
        s = jnp.einsum('bqhd,bqkhd->bhqk', qblk.astype(jnp.float32), kg) * scale
        p = masked_softmax(s, valid[:, None])
        return jnp.einsum('bhqk,bqkhd->bqhd', p, vg)

    o = lax.map(one_block, (jnp.arange(nb), qb, qib, wib))
    return o.swapaxes(0, 1).reshape(B_, S_, B_HEADS * HEAD_DIM).astype(v.dtype)

def chunk_band_attention(q, k, v, rel_bias):
    B_, S_ = q.shape[0], q.shape[1]
    nc = S_ // CHUNK
    left = C_LEFT_CHUNKS * CHUNK
    band = left + CHUNK
    kp = jnp.pad(k.astype(jnp.float32), ((0, 0), (left, 0), (0, 0), (0, 0)))
    vp = jnp.pad(v.astype(jnp.float32), ((0, 0), (left, 0), (0, 0), (0, 0)))
    dist = left + jnp.arange(CHUNK)[:, None] - jnp.arange(band)[None, :]
    bias_idx = jnp.clip(dist, -(CHUNK - 1), MAX_REL) + (CHUNK - 1)
    bias = rel_bias.astype(jnp.float32)[:, bias_idx]
    qc = q.reshape(B_, nc, CHUNK, C_HEADS, HEAD_DIM).swapaxes(0, 1)
    scale = HEAD_DIM ** -0.5

    def one_chunk(args):
        ci, qblk = args
        kb = lax.dynamic_slice_in_dim(kp, ci * CHUNK, band, axis=1)
        vb = lax.dynamic_slice_in_dim(vp, ci * CHUNK, band, axis=1)
        valid = (ci * CHUNK - left + jnp.arange(band)) >= 0
        s = jnp.einsum('bqhd,bkhd->bhqk', qblk.astype(jnp.float32), kb) * scale + bias[None]
        p = masked_softmax(s, valid[None, None, None, :])
        return jnp.einsum('bhqk,bkhd->bqhd', p, vb)

    o = lax.map(one_chunk, (jnp.arange(nc), qc))
    return o.swapaxes(0, 1).reshape(B_, S_, C_HEADS * HEAD_DIM).astype(v.dtype)

def even_mixer(h, w_in, w_out, lam_p, subln, rope64, rope32, lambda_init, topk):
    B_, S_ = h.shape[0], h.shape[1]
    cos64, sin64 = rope64
    cos32, sin32 = rope32
    a_q, a_k, a_v, b_q, b_k, b_v, i_q, i_k, i_w = jnp.split(h @ w_in, EVEN_SPLITS, axis=-1)
    a_q = apply_rope(a_q.reshape(B_, S_, 2 * A_HEADS, HEAD_DIM), cos64, sin64).reshape(B_, S_, A_HEADS, 2, HEAD_DIM)
    a_k = apply_rope(a_k.reshape(B_, S_, 2 * A_HEADS, HEAD_DIM), cos64, sin64).reshape(B_, S_, A_HEADS, 2, HEAD_DIM)
    a_v = a_v.reshape(B_, S_, A_HEADS, A_VDIM)
    lp = lam_p.astype(jnp.float32)
    lam = jnp.exp(jnp.sum(lp[0] * lp[1])) - jnp.exp(jnp.sum(lp[2] * lp[3])) + lambda_init
    o_a = diff_attention(a_q, a_k, a_v, lam, subln, lambda_init)
    b_q = apply_rope(b_q.reshape(B_, S_, B_HEADS, HEAD_DIM), cos64, sin64)
    b_k = apply_rope(b_k.reshape(B_, S_, B_HEADS, HEAD_DIM), cos64, sin64)
    b_v = b_v.reshape(B_, S_, B_HEADS, HEAD_DIM)
    i_q = apply_rope(i_q.reshape(B_, S_, IDX_HEADS, IDX_DIM), cos32, sin32)
    i_k = apply_rope(i_k.reshape(B_, S_, 1, IDX_DIM), cos32, sin32)[:, :, 0]
    i_w = i_w * (IDX_HEADS ** -0.5 * IDX_DIM ** -0.5)
    o_b = dsa_attention(b_q, b_k, b_v, i_q, i_k, i_w, topk)
    return jnp.concatenate([o_a, o_b], axis=-1) @ w_out

def odd_mixer(h, w_in, w_out, rel_bias):
    B_, S_ = h.shape[0], h.shape[1]
    q, k, v = jnp.split(h @ w_in, 3, axis=-1)
    q = q.reshape(B_, S_, C_HEADS, HEAD_DIM)
    k = k.reshape(B_, S_, C_HEADS, HEAD_DIM)
    v = v.reshape(B_, S_, C_HEADS, HEAD_DIM)
    return chunk_band_attention(q, k, v, rel_bias) @ w_out

def second_inputs(seed: int = 0) -> dict:
    key = jax.random.key(seed)
    ks = jax.random.split(key, 12)
    n_even = (DEPTH_2 + 1) // 2
    n_odd = DEPTH_2 // 2
    nrm = jax.random.normal
    f32 = jnp.float32
    return {
        "x": nrm(ks[0], (BATCH, SEQ, D_MODEL), f32),
        "norm_g": 1.0 + 0.01 * nrm(ks[1], (DEPTH_2, 6, D_MODEL), f32),
        "ffn_wg": nrm(ks[2], (DEPTH_2, 2, D_MODEL, D_FF), f32) * D_MODEL ** -0.5,
        "ffn_wu": nrm(ks[3], (DEPTH_2, 2, D_MODEL, D_FF), f32) * D_MODEL ** -0.5,
        "ffn_wd": nrm(ks[4], (DEPTH_2, 2, D_FF, D_MODEL), f32) * D_FF ** -0.5,
        "even_w_in": nrm(ks[5], (n_even, D_MODEL, EVEN_PROJ), f32) * D_MODEL ** -0.5,
        "even_w_out": nrm(ks[6], (n_even, MIX_WIDTH, D_MODEL), f32) * MIX_WIDTH ** -0.5,
        "even_lambda": 0.1 * nrm(ks[7], (n_even, 4, HEAD_DIM), f32),
        "even_subln": 1.0 + 0.01 * nrm(ks[8], (n_even, A_VDIM), f32),
        "odd_w_in": nrm(ks[9], (n_odd, D_MODEL, 3 * D_MODEL), f32) * D_MODEL ** -0.5,
        "odd_w_out": nrm(ks[10], (n_odd, D_MODEL, D_MODEL), f32) * D_MODEL ** -0.5,
        "odd_rel_bias": 0.1 * nrm(ks[11], (n_odd, C_HEADS, REL_TABLE), f32),
    }

def second_block(x, norm_g, ffn_wg, ffn_wu, ffn_wd, even_w_in, even_w_out, even_lambda, even_subln,
              odd_w_in, odd_w_out, odd_rel_bias):
    S_ = x.shape[1]
    topk = min(TOPK_MAX, S_ // 4)
    rope64 = rope_tables(S_, HEAD_DIM)
    rope32 = rope_tables(S_, IDX_DIM)
    for l in range(DEPTH_2):
        g = norm_g[l]
        h = rmsnorm(x, g[0])
        x = x + 0.5 * rmsnorm(swiglu(h, ffn_wg[l, 0], ffn_wu[l, 0], ffn_wd[l, 0]), g[1])
        h = rmsnorm(x, g[2])
        if l % 2 == 0:
            e = l // 2
            lambda_init = 0.8 - 0.6 * math.exp(-0.3 * l)
            m = even_mixer(h, even_w_in[e], even_w_out[e], even_lambda[e], even_subln[e],
                           rope64, rope32, lambda_init, topk)
        else:
            o = l // 2
            m = odd_mixer(h, odd_w_in[o], odd_w_out[o], odd_rel_bias[o])
        x = x + rmsnorm(m.astype(x.dtype), g[3])
        h = rmsnorm(x, g[4])
        x = x + 0.5 * rmsnorm(swiglu(h, ffn_wg[l, 1], ffn_wu[l, 1], ffn_wd[l, 1]), g[5])
    return x


def setup_inputs(seed=0):
    out = dict(first_inputs(seed))
    for name, value in second_inputs(seed + 1).items():
        if name != "x":
            out[name + "_2"] = value
    return out


def reference(
    x, c, w_ada, b_ada, g_mix, w_in, w_br_moba, w_br_sb, w_out, rel_bias, g_ffn, w_up, w_conv,
    b_conv, w_down, g_final, norm_g_2, ffn_wg_2, ffn_wu_2, ffn_wd_2, even_w_in_2, even_w_out_2,
    even_lambda_2, even_subln_2, odd_w_in_2, odd_w_out_2, odd_rel_bias_2,
):
    x = first_block(
        x, c, w_ada, b_ada, g_mix, w_in, w_br_moba, w_br_sb, w_out, rel_bias, g_ffn, w_up,
        w_conv, b_conv, w_down, g_final,
    )
    return second_block(
        x, norm_g_2, ffn_wg_2, ffn_wu_2, ffn_wd_2, even_w_in_2, even_w_out_2, even_lambda_2,
        even_subln_2, odd_w_in_2, odd_w_out_2, odd_rel_bias_2,
    )


_drawn_inputs = setup_inputs


def setup_inputs(seed=0):
    import zlib

    import numpy as np

    out = dict(_drawn_inputs(seed))
    spreads = {}
    factors = {'even_subln_2': 52.358, 'odd_rel_bias_2': 6.353, 'b_conv': 2.82, 'norm_g_2': 3.088}
    for name, (base, spread) in spreads.items():
        noise = np.random.default_rng([zlib.crc32(name.encode()), seed]).standard_normal(out[name].shape)
        drawn = base * np.exp(spread * noise) if base else spread * noise
        out[name] = __import__('jax').numpy.asarray(drawn.astype(out[name].dtype))
    for name, factor in factors.items():
        out[name] = (out[name] * factor).astype(out[name].dtype)
    return out
```

```python
from contextlib import ExitStack

import numpy as np

import concourse.bass as bass
from concourse import mybir

F32 = mybir.dt.float32
F32R = mybir.dt.float32r
BF16 = mybir.dt.bfloat16
ACT = mybir.ActivationFunctionType
ALU = mybir.AluOpType
AX = mybir.AxisListType

P = 128
S = 256
TT = S // P
D = 1024
KT = D // P
HD = 64
D_FF = 2816
FC = 256
NFC = D_FF // FC
CONV = 2 * D_FF // P
BANK = 512
UNIT = 2048
RAW, SPLIT = 3, 3
LOOK = SPLIT - 1
EPS = 1e-6
NEG = -1e30
SCALE = HD ** -0.5
REL_BUCKETS = 32
REL_MAX_DIST = 128
CHUNK = 64
IDX_HEADS, IDX_DIM, TOPK = 8, 32, 64
LAMBDA_INIT = 0.2
EVEN_W = 3368
SC = P + S
BIAS_T = S + P - 1


def t5_bounds():
    exact = REL_BUCKETS // 2
    n = np.arange(S)
    large = exact + (np.log(np.maximum(n, exact).astype(np.float32) / exact)
                     / np.log(REL_MAX_DIST / exact) * (REL_BUCKETS - exact)).astype(np.int32)
    b = np.where(n < exact, n, np.minimum(large, REL_BUCKETS - 1))
    return [int(np.argmax(b >= i)) for i in range(REL_BUCKETS)] + [S]


def constants():
    p = np.arange(P)[:, None]
    k = np.arange(P)[None, :]
    ident = np.eye(P, dtype=np.float32)
    later = (p >= k).astype(np.float32)
    q_of = np.concatenate([p + 0 * k, p + P + 0 * k, p + P + 0 * k], 1)
    k_of = np.concatenate([k + 0 * p, k + 0 * p, k + P + 0 * p], 1)
    chunk_mask = np.where(k_of // CHUNK <= q_of // CHUNK, 0.0, NEG).astype(np.float32)
    past = np.concatenate([p < k, p < k + P, p < k], 1)
    minus_past = -past.astype(np.float32)

    def rope(dim):
        inv = (np.float32(10000.0) ** (-np.arange(0, dim, 2, dtype=np.float32) / np.float32(dim))).astype(np.float32)
        ang = (np.arange(S, dtype=np.float32)[:, None] * inv[None, :]).astype(np.float32)
        c, s = np.cos(ang), np.sin(ang)
        both = np.concatenate([c, c, -s, s], 1).astype(np.float32)
        return both.reshape(TT, P, 2 * dim).transpose(1, 0, 2).reshape(P, TT * 2 * dim)

    return np.ascontiguousarray(np.concatenate(
        [ident, later, chunk_mask, minus_past, rope(HD), rope(IDX_DIM)], 1).astype(np.float32))


class Use:

    def __init__(self, bank, prev, unit, ready, evacuated):
        self.bank, self.prev, self.unit, self.ready = bank, prev, unit, ready
        self.read_by = ("psum_read", evacuated)


class Plan:

    def __init__(self):
        self.steps, self.units = [], []
        self.tenant, self.announced, self.evacuated = [None] * 8, [0] * 8, [0] * 8
        self.ropes = 0
        self.turned, self.turned_groups, self.squares = 0, [], 0
        self.splits = 0
        self.stats = 0
        self.stat_cols = 0

    def add(self, kind, **kw):
        self.steps.append((kind, kw))

    def unit(self, nk, w, parts):
        self.units.append((nk, w, parts))
        return len(self.units) - 1

    def use(self, bank, unit=None, read_by=None, by_unit=False):
        if unit is None and not by_unit:
            self.announced[bank] += 1
        if read_by is None:
            self.evacuated[bank] += 1
        use = Use(bank, self.tenant[bank], unit, self.announced[bank], self.evacuated[bank])
        if read_by is not None:
            use.read_by = read_by
        self.tenant[bank] = use
        return use

    def turned_use(self, bank):
        self.turned += 1
        return self.use(bank, read_by=("turned_ready", self.turned))

    def turn(self):
        self.splits += 1
        return self.splits - 1

    def new_stat(self, width):
        c, i = self.stat_cols, self.stats
        self.stat_cols += 5 * width
        self.stats += 1
        return dict(i=i, w=width, ss=(c, c + width), v=(c + width, c + 2 * width), y=(c + 2 * width, c + 3 * width),
                    t=(c + 3 * width, c + 4 * width), r=(c + 4 * width, c + 5 * width))



def build_plan(W):
    pl = Plan()
    n_attn, n_sb, n_turned_heads, n_x, n_scr = [0], [0], [0], [0], [0]
    last_hT_unit = [None]

    def rows(w, k0, nk, c0, n):
        return w[k0 * P:(k0 + nk) * P, c0:c0 + n].rearrange("(k p) n -> p k n", p=P)

    def column_units(w, k_tiles, c0, n):
        made = []
        for k0 in range(0, k_tiles, 4):
            u = pl.unit(4, n, [(0, n, rows(w, k0, 4, c0, n))])
            made.append((u, k0))
        return made

    free_pair = [0]

    def pair():
        free_pair[0] ^= 1
        return (4, 5) if free_pair[0] else (6, 7)

    def proj(w, c0, n, dst, mode, banks=None, stat=None, k_tiles=KT, k_base=0, g0=0):
        us = column_units(w, k_tiles, c0, n)
        banks = banks or pair()
        uses = [pl.use(b, us[-1][0]) for b in banks]
        last_hT_unit[0] = us[-1][0]
        pl.add("proj", units=us, n=n, dst=dst, mode=mode, uses=uses, stat=stat, k_base=k_base, g0=g0)
        return uses

    row_uses, col_uses = [], []

    def ada(n, bank):
        us = column_units(W["w_ada"], KT, n * BANK, BANK)
        gate = {4: 0, 5: 0, 10: 1, 11: 1}.get(n)
        use = pl.use(bank, us[-1][0])
        row = None
        if gate is None:
            row = len(row_uses)
            row_uses.append(use)
        pl.add("ada", n=n, units=us, use=use, gate=gate, row=row,
               slot_free=col_uses[row - 2] if row is not None and row >= 2 else None)

    def adacol(n, row, bank):
        use = pl.use(bank)
        col_uses.append(use)
        pl.add("adacol", n=n, row=row, row_use=row_uses[row], use=use, vec={0: 0, 1: 1, 3: 2, 4: 3}[n // 2])

    def group():
        g = pl.turn()
        pl.turned_groups.append(g)
        return g

    def turn(src, after, scale, bias, k0=0, nk=KT, banks=(4, 5, 6, 7)):
        first = pl.splits
        for j in range(nk // 2):
            pl.add("turn", src=src, after=after if j == 0 else None, scale=scale, bias=bias,
                   kt=k0 + 2 * j, use=pl.turned_use(banks[j % len(banks)]), ti=pl.turned - 1, g=group(),
                   read_before=last_hT_unit[0])
        return first

    def stats(kind, after, width=TT, uses=None):
        st = pl.new_stat(width)
        pl.squares += 1
        pl.add("stats", src=kind, si=pl.squares, after=after, st=st, uses=uses)
        return st

    def head_turn(col, block, banks, after):
        use = pl.use(banks)
        pl.add("headturn", col=col, block=block, use=use, after=after)
        return use

    def softmax_heads(name, fillers, bias, v_col, v_w, q_ready, v_ready, diff=False, base=0):
        n0 = n_attn[0]
        n_attn[0] += 8
        pend_v = []
        fill = list(fillers)

        def t_of(h):
            k = n_turned_heads[0]
            n_turned_heads[0] += 1
            use = pl.use(2 + k % 2)
            pl.add("probturn", n=n0 + h, k=k, use=use, diff=diff)
            return k, use

        state = dict(o=None)

        def pv(h, kt):
            first = state["o"] is None
            if first:
                state["o"] = [pl.use(0), pl.use(1)]
            nv = (h // 2) if diff else h
            last = h == 7
            pl.add("pv", n=n0 + h, k=kt[0], turned=kt[1], slot=nv, v=v_col + nv * v_w, w=v_w, uses=state["o"], first=first, last=last,
                   v_ready=v_ready)

        for i in range(8 + 2):
            if i >= 2 and pend_v:
                pv(*pend_v.pop(0))
            if i < 8:
                h = i
                pl.add("qk", name=name, n=n0 + h, h=h, base=base, use=pl.use(4 + (n0 + h) % 2), bias=bias,
                       ready=q_ready(h))
            if fill:
                for f in fill.pop(0):
                    f()
            if 1 <= i <= 8:
                if not diff:
                    pend_v.append((i - 1, t_of(i - 1)))
                elif (i - 1) % 2 == 1:
                    pl.add("mix", n=n0 + i - 1)
                    pend_v.append((i - 1, t_of(i - 1)))
        while pend_v:
            pv(*pend_v.pop(0))
        while fill:
            for f in fill.pop(0):
                f()
        return n0, state["o"]

    def sb_heads(fillers, v_col, q_ready, v_ready):
        fill = list(fillers)
        o = [pl.use(0), pl.use(1)]
        for i in range(8 + 2):
            if i >= 2:
                m = i - 2
                pl.add("sb_pv", m=m, v=v_col + m * HD, uses=o, v_ready=v_ready)
            if i < 8:
                pl.add("sb_z", m=i, use=pl.use(4 + i % 2), ready=q_ready(i))
            if fill:
                for f in fill.pop(0):
                    f()
            if 1 <= i <= 8:
                k = n_turned_heads[0]
                n_turned_heads[0] += 1
                pl.add("sb_cum", m=i - 1, use=pl.use(2 + k % 2))
        while fill:
            for f in fill.pop(0):
                f()
        return o

    def ffn(up_units, stat, conv, g0, w_down):
        y = [None] * 4
        ups = {}

        def up(c):
            us = up_units(c)
            banks = (4, 5) if c % 2 == 0 else (6, 7)
            uses = [pl.use(b, us[-1][0]) for b in banks]
            ups[c] = uses
            last_hT_unit[0] = us[-1][0]
            pl.add("up", c=c, units=us, uses=uses, stat=stat, conv=conv, g0=g0, ci=chunk_no[0] + c)

        def turn_hidden(c):
            banks = (4, 5) if c % 2 == 0 else (6, 7)
            uses = [pl.use(b) for b in banks] if conv else [pl.turned_use(banks[0])]
            g = pl.turn() if conv else group()
            before = downs[c - 2] if c >= 2 else None
            pl.add("hturn", c=c, ci=chunk_no[0] + c, uses=uses, ups=ups[c], conv=conv, g=g, down_before=before,
                   cc=conv_no[0] + c, ti=pl.turned - 1)
            gs[c] = g

        def down(c):
            u = pl.unit(2, D, [(0, D, rows(w_down, 2 * c, 2, 0, D))])
            downs[c] = u
            if c == 0:
                for b in range(4):
                    y[b] = pl.use(b, by_unit=True)
            pl.add("down", c=c, unit=u, uses=y, g=gs[c])

        downs, gs = {}, {}
        up(0)
        turn_hidden(0)
        for c in range(1, NFC):
            up(c)
            down(c - 1)
            turn_hidden(c)
        down(NFC - 1)
        for b in range(4):
            y[b].unit = downs[NFC - 1]
        if not conv:
            chunk_no[0] += NFC
        else:
            conv_no[0] += NFC
        return y

    chunk_no, conv_no = [0], [0]

    def post(mode, y, **kw):
        pl.add("post", mode=mode, uses=y, row=rows_used[0], **kw)
        if mode == "norm":
            rows_used[0] += 1
        n_x[0] += 1
    rows_used = [0]

    def o_evac(o, dst, final, n0=None):
        if final:
            o[1].read_by = ("scr_ready", n_scr[0])
            pl.evacuated[o[1].bank] -= 1
        pl.add("oevac", mode="plain" if n0 is None else "norm", uses=o, n0=n0, dst=dst, final=final)

    def scr_version():
        n_scr[0] += 1
        return n_scr[0]

    pl.add("vectors", uses=[pl.use(b) for b in (4, 5, 6, 7)])
    st = stats("X", ("x_loaded", 16))
    for n in range(4):
        ada(n, (4, 5, 6, 7)[n])
        if n:
            adacol(n - 1, n - 1, n - 1)
    adacol(3, 3, 3)
    pl.add("modfinal", vec=1, gain=8)
    pl.add("normalise", st=st)
    v = scr_version()
    g0 = turn("scr", ("scr_ready", v), ("mod", 1), ("mod", 0))
    pl.add("load_bias", which=0, after=("split_done", pl.splits))
    r = {}
    for i, name in enumerate(["qa", "ka", "va", "qb", "kb", "vb"]):
        r[name] = proj(W["w_in"], i * BANK, BANK, i * BANK, "plain", g0=g0)
        if name in ("va", "vb"):
            a, b = ("qa", "ka") if name == "va" else ("qb", "kb")
            for j, nm in enumerate((a, b)):
                blk = 4 * j + (0 if name == "va" else 8)
                col = i * BANK - (2 - j) * BANK
                for t in range(2):
                    r[nm + str(t)] = head_turn(col + 256 * t, blk + 2 * t, 2 + t, ("uses", r[nm]))

    def q_ready_of(q, k):
        return lambda h: [r[q + str(h // 4)], r[k + str(h // 4)]]

    gates = [lambda i=i: proj(W["w_in"], (6 + i) * BANK, BANK, (0, BANK, 3 * BANK, 4 * BANK)[i], "sigmoid", (6, 7), g0=g0)
             for i in range(4)]

    def ada_fill(n):
        row = {6: 4, 7: 5, 8: 6, 9: 7}.get(n)

        def go():
            ada(n, 6)
        return go, (None if row is None else (lambda: adacol(n, row, 7)))

    fa = [[gates[0]], [gates[1]], [gates[2]], [gates[3]]]
    for n in (4, 5, 6, 7):
        go, col = ada_fill(n)
        fa.append([go] if col is None else [go, col])
    fb = []
    for n in (8, 9, 10, 11):
        go, col = ada_fill(n)
        fb.append([go] if col is None else [go, col])
    n0, o = softmax_heads("moba", fa, "moba", 2 * BANK, HD, q_ready_of("qa", "ka"), r["va"])
    o_evac(o, ("scr", 0), False, n0)
    o = sb_heads(fb, 5 * BANK, q_ready_of("qb", "kb"), r["vb"])
    v = scr_version()
    o_evac(o, ("scr", BANK), True)
    g0 = turn("scr", ("scr_ready", v), None, None)
    for n in range(2):
        ua = proj(W["w_br_moba"], n * BANK, BANK, None, "hold", (4, 5), k_tiles=4, g0=g0)
        ub_ = proj(W["w_br_sb"], n * BANK, BANK, None, "hold", (6, 7), k_tiles=4, k_base=4, g0=g0)
        pl.add("mixbranch", n=n, ya=ua, yb=ub_, final=n == 1)
    v = scr_version()
    g0 = turn("scr", ("scr_ready", v), None, None)
    y = []
    for n in range(2):
        uses = proj(W["w_out"], n * BANK, BANK, None, "hold", (n, 2 + n), g0=g0)
        y += [uses]
    pl.add("modfinal", vec=3, gain=16)
    post("gate", [y[0][0], y[1][0], y[0][1], y[1][1]], gate=0)
    st = stats("X", ("x_ready", n_x[0]))
    pl.add("normalise", st=st)
    v = scr_version()
    g0 = turn("scr", ("scr_ready", v), ("mod", 3), ("mod", 2))

    def up_pair(wv, wg, cv0, cg0):
        def make(c):
            us = []
            for k0 in (0, 4):
                u = pl.unit(4, 2 * FC, [(0, FC, rows(wv, k0, 4, cv0 + c * FC, FC)),
                                        (FC, FC, rows(wg, k0, 4, cg0 + c * FC, FC))])
                us.append((u, k0))
            return us
        return make

    y = ffn(up_pair(W["w_up"], W["w_up"], 0, D_FF), None, True, g0, W["w_down"])
    post("gate", y, gate=1)
    st = stats("X", ("x_ready", n_x[0]))
    pl.add("finalnorm", st=st, row=rows_used[0])
    rows_used[0] += 1
    n_x[0] += 1

    for l in range(2):
        def gain(j):
            return ("gain", 24 + (l * 6 + j) * 8)

        def swiglu(i, j):
            g0 = turn("X", ("x_ready", n_x[0]), gain(j), None)
            st = stats("X", ("x_ready", n_x[0]))
            y = ffn(up_pair(W["ffn_wg"][l, i], W["ffn_wu"][l, i], 0, 0), st, False, g0, W["ffn_wd"][l, i])
            sy = stats("y", None, uses=y)
            post("norm", y, st=sy, factor=0.5)

        swiglu(0, 0)
        if l == 1:
            pl.add("load_bias", which=1, after=("x_ready", n_x[0]))
            pl.add("load_bias", which=2, after=("x_ready", n_x[0]))
        g0 = turn("X", ("x_ready", n_x[0]), gain(2), None)
        st = stats("X", ("x_ready", n_x[0]))
        if l == 0:
            w = W["even_w_in"][0]

            def ep(i, banks=None):
                n = BANK if i < 6 else EVEN_W - 6 * BANK
                return proj(w, i * BANK, n, i * BANK, "rstd", banks, st, g0=g0)

            u6 = ep(6)
            u0 = ep(0)
            r6 = rope(pl, 6 * BANK, 9, IDX_DIM, u6, True)
            u1 = ep(1)
            r0 = rope(pl, 0, 8, HD, u0)
            pl.add("idxturn", uses=[pl.use(2), pl.use(3)], after=("rope_ready", r6))
            u2 = ep(2)
            r1 = rope(pl, BANK, 8, HD, u1)
            for t in range(2):
                r[f"aq{t}"] = head_turn(256 * t, 2 * t, 2 + t, ("rope_ready", r0))
            for h in range(IDX_HEADS):
                pl.add("idx", h=h, use=pl.use(4 + h % 2))
            for t in range(2):
                r[f"ak{t}"] = head_turn(BANK + 256 * t, 4 + 2 * t, 2 + t, ("rope_ready", r1))

            held = {}

            def fill_proj(i):
                def go():
                    held[i] = ep(i, (6, 7))
                return go

            def fill_rope(i, nm, blk):
                def go():
                    held[nm] = rope(pl, i * BANK, 8, HD, held[i])
                return go

            def fill_turn(i, nm, blk):
                def go():
                    for t in range(2):
                        r[nm + str(t)] = head_turn(i * BANK + 256 * t, blk + 2 * t, 6 + t, ("rope_ready", held[nm]))
                return go

            def topk(j):
                return lambda: pl.add("topk", j=j)

            fills = [[topk(0), fill_proj(3)], [topk(1), topk(2)], [topk(3), fill_rope(3, "bq", 8), fill_proj(4)],
                     [topk(4), topk(5)], [fill_turn(3, "bq", 8), fill_rope(4, "bk", 12), fill_proj(5)],
                     [topk(6), topk(7)], [fill_turn(4, "bk", 12)]]
            n0, o = softmax_heads("diff", fills, "mask", 2 * BANK, 2 * HD, q_ready_of("aq", "ak"), u2, diff=True)
            sd = pl.new_stat(8)
            pl.add("diffout", uses=o, st=sd)
            n0, o = softmax_heads("dsa", [], "sel", 5 * BANK, HD, q_ready_of("bq", "bk"), held[5], base=8)
            v = scr_version()
            o_evac(o, ("scr", BANK), True, n0)
            g0 = turn("scr", ("scr_ready", v), None, None)
            wo = W["even_w_out"][0]
        else:
            w = W["odd_w_in"][0]
            uo = {}

            def op(i, banks=None):
                uo[i] = proj(w, i * BANK, BANK, i * BANK, "rstd", banks, st, g0=g0)

            def turns(i, nm, blk, banks):
                for t in range(2):
                    r[nm + str(t)] = head_turn(i * BANK + 256 * t, blk + 2 * t, banks + t, ("uses", uo[i]))

            op(0)
            op(2)
            op(4)
            turns(0, "oq", 0, 2)
            turns(2, "ok", 4, 2)
            fills = [[lambda: op(1, (6, 7))], [], [lambda: op(3, (6, 7))], [lambda: turns(1, "pq", 8, 6)],
                     [lambda: op(5, (6, 7))], [lambda: turns(3, "pk", 12, 6)]]
            n0, o = softmax_heads("odd", fills, "odd0", 4 * BANK, HD, q_ready_of("oq", "ok"), uo[4])
            o_evac(o, ("pr", 0), False, n0)
            n0, o = softmax_heads("odd", [], "odd1", 5 * BANK, HD, q_ready_of("pq", "pk"), uo[5], base=8)
            v = scr_version()
            o_evac(o, ("pr", BANK), True, n0)
            g0 = turn("pr", ("scr_ready", v), None, None)
            wo = W["odd_w_out"][0]
        y = [proj(wo, n * BANK, BANK, None, "hold", (n, 2 + n), g0=g0) for n in range(2)]
        y = [y[0][0], y[1][0], y[0][1], y[1][1]]
        sy = stats("y", None, uses=y)
        post("norm", y, st=sy, factor=1.0)
        swiglu(1, 4)
    pl.x_final = n_x[0]
    return pl


def rope(pl, col, heads, dim, uses, replicate=False):
    n = pl.ropes
    pl.ropes = n + 1
    pl.add("rope", col=col, heads=heads, dim=dim, uses=uses, replicate=replicate, i=n)
    return n + 1


def program(nc, consts, x, c, w_ada, b_ada, g_mix, w_in, w_br_moba, w_br_sb, w_out, rel_bias, g_ffn, w_up,
            w_conv, b_conv, w_down, g_final, norm_g, ffn_wg, ffn_wu, ffn_wd, even_w_in, even_w_out,
            even_lambda, even_subln, odd_w_in, odd_w_out, odd_rel_bias, table, out):
    with ExitStack() as ctx:
        def sb(name, shape, dt=F32):
            return ctx.enter_context(nc.sbuf_tensor(name, shape, dt))

        def sem(name):
            return ctx.enter_context(nc.semaphore(name))

        raw = sb("raw", [P, RAW, UNIT])
        w_hi = sb("w_hi", [P, SPLIT, UNIT], F32R)
        w_lo = sb("w_lo", [P, SPLIT, UNIT], F32R)
        X = sb("X", [P, TT, D])
        hT_hi = sb("hT_hi", [P, KT, S], F32R)
        hT_lo = sb("hT_lo", [P, KT, S], F32R)
        hc_hi = sb("hc_hi", [P, 2, 2 * S], F32R)
        hc_lo = sb("hc_lo", [P, 2, 2 * S], F32R)
        turned = sb("turned", [P, 2, BANK])
        scr = sb("scr", [P, TT, D])
        PR = sb("PR", [P, TT * EVEN_W])
        QK = sb("QK", [P, 16, S])
        IT = sb("IT", [P, 3, S])
        gate_rows = sb("gate_rows", [P, 2, D])
        g_row = sb("g_row", [P, D])
        ada_row = sb("ada_row", [P, 2, BANK])
        logit = sb("logit", [P, 2, SC])
        prob = sb("prob", [P, 4, SC])
        probT = sb("probT", [P, 2, SC])
        work = sb("work", [P, SC])
        junk = sb("junk", [P, D], BF16)
        CONSTS = 2 * P + 2 * SC + TT * 2 * HD + TT * 2 * IDX_DIM
        cst = sb("cst", [P, CONSTS])
        ident, later = cst[:, 0:P], cst[:, P:2 * P]
        chunk_mask = cst[:, 2 * P:2 * P + SC]
        minus_past = cst[:, 2 * P + SC:2 * P + 2 * SC]
        r64 = cst[:, 2 * P + 2 * SC:2 * P + 2 * SC + TT * 2 * HD].rearrange("p (t c) -> p t c", t=TT)
        r32 = cst[:, 2 * P + 2 * SC + TT * 2 * HD:CONSTS].rearrange("p (t c) -> p t c", t=TT)
        ones = sb("ones", [P, P])
        NV = 120
        cols = sb("cols", [P, NV])
        ada_b = sb("ada_b", [P, 48])
        conv_c = sb("conv_c", [P, 4 * CONV])
        mod = sb("mod", [P, 4, KT])
        c_act = sb("c_act", [P, KT])
        stat = sb("stat", [P, 512])
        nmax = sb("nmax", [P, 40, 2])
        sums = sb("sums", [P, 40, 2])
        rsum = sb("rsum", [P, 40, 2])
        top = sb("top", [P, 16])
        lam = sb("lam", [P, 4])
        lam_in = sb("lam_in", [P, 4, HD])
        subln = sb("subln", [P, P])
        bucket = sb("bucket", [8, REL_BUCKETS])
        dist = logit[0:8, 0, 0:BIAS_T]
        selbias = sb("selbias", [P, SC])

        psum = ctx.enter_context(nc.psum_tensor("psum", [P, 8, BANK], F32))

        sg = PR[:, 0:1024].rearrange("p (b t n) -> p b t n", b=2, t=TT)
        hid = PR[:, 1024:2048].rearrange("p (b t n) -> p b t n", b=2, t=TT)
        ub = PR[:, 2048:4096].rearrange("p (b t n) -> p b t n", b=2, t=TT)
        cv = PR[:, 4096:5120]
        gg = PR[:, 5120:5632]
        hfull = PR[:, 5632:6144]
        vec_rows = PR[:, 0:4 * P].rearrange("p (v n) -> p v n", v=4)
        pr = PR[:, :].rearrange("p (t n) -> p t n", t=TT)

        weight_loaded = [sem(f"weight_loaded{i}") for i in range(RAW)]
        hi_ready, lo_ready, unit_used = sem("hi_ready"), sem("lo_ready"), sem("unit_used")
        psum_ready = [sem(f"psum_ready{i}") for i in range(8)]
        psum_read = [sem(f"psum_read{i}") for i in range(8)]
        act_step, dve_step, pool_step = sem("act_step"), sem("dve_step"), sem("pool_step")
        consts_loaded, x_loaded, vectors_loaded = sem("consts_loaded"), sem("x_loaded"), sem("vectors_loaded")
        small_loaded, bucket_loaded, gate_bias_loaded = sem("small_loaded"), sem("bucket_loaded"), sem("gate_bias_loaded")
        rows_cleared = sem("rows_cleared")
        vectors_turned = sem("vectors_turned")
        c_act_ready, c_split = sem("c_act_ready"), sem("c_split")
        ones_ready = sem("ones_ready")
        ada_row_ready, mod_ready = sem("ada_row_ready"), sem("mod_ready")
        mod_final = sem("mod_final")
        turned_ready, split_done = sem("turned_ready"), sem("split_done")
        squares_ready, variance_ready, guess_ready, rstd_ready = (
            sem("squares_ready"), sem("variance_ready"), sem("guess_ready"), sem("rstd_ready"))
        x_ready, scr_ready = sem("x_ready"), sem("scr_ready")
        dist_ready, table_stored, bias_cleared = sem("dist_ready"), sem("table_stored"), sem("bias_cleared")
        bias_loaded = [sem(f"bias_loaded{i}") for i in range(3)]
        logits_ready, probs_ready, mixed_ready = sem("logits_ready"), sem("probs_ready"), sem("mixed_ready")
        z_ready, small_z_ready, softplus_ready, log_keep_ready = (
            sem("z_ready"), sem("small_z_ready"), sem("softplus_ready"), sem("log_keep_ready"))
        keep_ready = sem("keep_ready")
        arg_ready, weight_ready, weight_masked = sem("arg_ready"), sem("weight_ready"), sem("weight_masked")
        silu_ready, hidden_ready, u_ready, conv_first, conv_ready, gelu_ready = (
            sem("silu_ready"), sem("hidden_ready"), sem("u_ready"), sem("conv_first"), sem("conv_ready"),
            sem("gelu_ready"))
        rope_in, rope_swapped, rope_ready = sem("rope_in"), sem("rope_swapped"), sem("rope_ready")
        rel_ready, score_ready, selected = sem("rel_ready"), sem("score_ready"), sem("selected")
        lam_dots, lam_exp, lam_ready = sem("lam_dots"), sem("lam_exp"), sem("lam_ready")
        g_row_loaded, g_row_used = sem("g_row_loaded"), sem("g_row_used")
        stored = sem("stored")

        plan = build_plan(dict(w_ada=w_ada[0], w_in=w_in[0], w_br_moba=w_br_moba[0], w_br_sb=w_br_sb[0], w_out=w_out[0],
                               w_up=w_up[0], w_down=w_down[0], ffn_wg=ffn_wg, ffn_wu=ffn_wu, ffn_wd=ffn_wd,
                               even_w_in=even_w_in, even_w_out=even_w_out, odd_w_in=odd_w_in, odd_w_out=odd_w_out))
        steps, units = plan.steps, plan.units
        named = dict(x_loaded=x_loaded, x_ready=x_ready, scr_ready=scr_ready, split_done=split_done,
                     rope_ready=rope_ready, turned_ready=turned_ready)
        bufs = dict(X=X, scr=scr, pr=pr)

        def wait_ready(eng, use):
            if use.unit is not None:
                eng.wait_ge(unit_used, use.unit + 1)
            else:
                eng.wait_ge(psum_ready[use.bank], use.ready)

        def wait_read(eng, use):
            name, value = use.read_by
            eng.wait_ge(psum_read[use.bank] if name == "psum_read" else named[name], value)

        def wait_free(eng, use):
            if use.prev is not None:
                wait_read(eng, use.prev)

        def col(st, part, i):
            return stat[:, st[part][0] + i:st[part][0] + i + 1]

        def unit_view(tile, slot, u):
            nk, w, _ = units[u]
            return tile[:, slot, 0:nk * w]

        rel_bias_rows = dict(moba=lambda h: scr[:, :, :].rearrange("p t (g n) -> p (t g) n", n=S)[:, h, :],
                             odd0=lambda h: gate_rows[:, :, :].rearrange("p t (g n) -> p (t g) n", n=S)[:, h, :],
                             odd1=lambda h: scr[:, :, :].rearrange("p t (g n) -> p (t g) n", n=S)[:, h, :])

        block = ctx.enter_context(nc.Block())

        @block.sync
        def _(sp):
            for u, (nk, w, parts) in enumerate(units):
                s = u % RAW
                if u >= RAW:
                    sp.wait_ge(hi_ready, u - RAW + 1)
                    sp.wait_ge(lo_ready, u - RAW + 1)
                view = unit_view(raw, s, u).rearrange("p (k n) -> p k n", k=nk)
                for c0, n, src in parts:
                    sp.dma_start(view[:, :, c0:c0 + n], src).then_inc(weight_loaded[s], 16)
            sp.wait_ge(x_ready, plan.x_final)
            sp.dma_start(out[0].rearrange("(t p) d -> p t d", p=P), X[:, :, :]).then_inc(stored, 16)
            sp.wait_ge(stored, 16)

        landed = []
        seen = [0] * RAW
        for u, (nk, w, parts) in enumerate(units):
            seen[u % RAW] += 16 * len(parts)
            landed.append(seen[u % RAW])

        @block.gpsimd
        def _(pool):
            n = [0]

            def mark(ins):
                ins.then_inc(pool_step, 1)
                n[0] += 1
                return n[0]

            def link(ins):
                pool.wait_ge(pool_step, mark(ins))

            nc.gpsimd.memset(ones[:, :], 1.0).then_inc(ones_ready, 1)
            link(nc.gpsimd.memset(dist, NEG))
            pool.wait_ge(bucket_loaded, 16)
            bounds = t5_bounds()
            for b in range(REL_BUCKETS):
                a, e = P - 1 + bounds[b], P - 1 + bounds[b + 1]
                ins = nc.gpsimd.tensor_copy(dist[:, a:e], bucket[:, b:b + 1].to_broadcast([8, e - a]))
            ins.then_inc(dist_ready, 1)
            pool.wait_ge(dist_ready, 1)
            pool.dma_start(table, dist).then_inc(table_stored, 16)
            gain_rows = [g_final.rearrange("(o d) -> o d", o=1)]
            for l in range(2):
                for j in (1, 3, 5):
                    gain_rows.append(norm_g[l, j:j + 1, :])

            def load_gain(i):
                if i:
                    pool.wait_ge(g_row_used, i)
                pool.dma_start(g_row[:, :], gain_rows[i].to_broadcast([P, D])).then_inc(g_row_loaded, 16)

            load_gain(0)
            for kind, a in steps:
                if kind == "load_bias":
                    which = a["which"]
                    pool.wait_ge(named[a["after"][0]], a["after"][1])
                    if which == 0:
                        pool.wait_ge(table_stored, 16)
                        src = bass.AP(table.tensor, table.offset, [[1, P], [BIAS_T, 8], [1, S]])
                        pool.dma_start(scr[:, :, :].rearrange("p t (g n) -> p (t g) n", n=S), src)\
                            .then_inc(bias_loaded[0], 16)
                    else:
                        buf = (gate_rows, scr)[which - 1][:, :, :].rearrange("p t (g n) -> p (t g) n", n=S)
                        h0 = 8 * (which - 1)
                        table_w = odd_rel_bias.shape[2]
                        base = odd_rel_bias.offset + h0 * table_w
                        nc.gpsimd.memset(buf[0:CHUNK, :, 0:CHUNK], NEG).then_inc(bias_cleared, 1)
                        lo = bass.AP(odd_rel_bias.tensor, base, [[1, CHUNK], [table_w, 8], [1, S - CHUNK]])
                        hi = bass.AP(odd_rel_bias.tensor, base, [[1, CHUNK], [table_w, 8], [1, S]])
                        pool.dma_start(buf[0:CHUNK, :, CHUNK:S], lo).then_inc(bias_loaded[which], 16)
                        pool.dma_start(buf[CHUNK:P, :, :], hi).then_inc(bias_loaded[which], 16)
                elif kind == "rope":
                    c0, nh, dim, tab = a["col"], a["heads"], a["dim"], (r64 if a["dim"] == HD else r32)
                    w = nh * dim
                    for use in a["uses"]:
                        wait_read(pool, use)
                    if a["i"]:
                        pool.wait_ge(rope_ready, a["i"])
                    pool.wait_ge(consts_loaded, 16)
                    for t in range(TT):
                        sw = pr[:, t, c0:c0 + w].rearrange("p (h s d) -> p h s d", h=nh, s=2)[:, :, ::-1, :]
                        sn = tab[:, t, dim:2 * dim].rearrange("p (s d) -> p s d", s=2)[:, None, :, :]\
                            .to_broadcast([P, nh, 2, dim // 2])
                        o = scr[:, t, BANK:BANK + w].rearrange("p (h s d) -> p h s d", h=nh, s=2)
                        ins = nc.gpsimd.tensor_tensor(o, sw, sn, ALU.mult)
                    ins.then_inc(rope_swapped, 1)
                elif kind == "post" and a["mode"] == "norm" or kind == "finalnorm":
                    if a["row"] + 1 < len(gain_rows):
                        load_gain(a["row"] + 1)
                elif kind == "sb_z":
                    m = a["m"]
                    pool.wait_ge(softplus_ready, m + 1)
                    if m == 0:
                        pool.wait_ge(consts_loaded, 16)
                    nc.gpsimd.tensor_tensor(probT[:, m % 2, :], prob[:, m % 4, :], minus_past, ALU.mult)\
                        .then_inc(log_keep_ready, 1)
                elif kind == "sb_cum":
                    m = a["m"]
                    pool.wait_ge(weight_ready, m + 1)
                    for blk in (0, 2):
                        v = logit[:, m % 2, blk * P:(blk + 1) * P]
                        ins = nc.gpsimd.affine_select(out=v, in_=v, compare_op=ALU.is_gt, fill=0.0, base=0,
                                                      pattern=[[1, P]], channel_multiplier=-1)
                    ins.then_inc(weight_masked, 1)

        @block.scalar
        def _(act):
            n = [0]

            def mark(ins):
                ins.then_inc(act_step, 1)
                n[0] += 1
                return n[0]

            def link(ins):
                act.wait_ge(act_step, mark(ins))

            act.dma_start(PR[0:8, 0:P], c.rearrange("o (k n) -> (o k) n", n=P)).then_inc(vectors_loaded, 16)
            act.dma_start(PR[8:16, 0:P], g_mix.rearrange("o (k n) -> (o k) n", n=P)).then_inc(vectors_loaded, 16)
            act.dma_start(PR[16:24, 0:P], g_ffn.rearrange("o (k n) -> (o k) n", n=P)).then_inc(vectors_loaded, 16)
            act.dma_start(PR[24:120, 0:P], norm_g.rearrange("l j (k n) -> (l j k) n", n=P)).then_inc(vectors_loaded, 16)
            act.dma_start(PR[0:48, P:2 * P], b_ada.rearrange("o (k n) -> (o k) n", n=P)).then_inc(vectors_loaded, 16)
            act.dma_start(PR[0:88, 2 * P:3 * P], w_conv[0, 0:2].rearrange("j (k n) -> (j k) n", n=P))\
                .then_inc(vectors_loaded, 16)
            act.dma_start(PR[0:44, 3 * P:4 * P], w_conv[0, 2:3].rearrange("j (k n) -> (j k) n", n=P))\
                .then_inc(vectors_loaded, 16)
            act.dma_start(PR[44:88, 3 * P:4 * P], b_conv.rearrange("j (k n) -> (j k) n", n=P))\
                .then_inc(vectors_loaded, 16)
            act.dma_start(cst[:, :], consts).then_inc(consts_loaded, 16)
            act.dma_start(X[:, :, :], x[0].rearrange("(t p) d -> p t d", p=P)).then_inc(x_loaded, 16)
            act.dma_start(bucket[:, :], rel_bias).then_inc(bucket_loaded, 16)
            act.dma_start(gate_rows[:, 0, :], b_ada[0:1, 2 * D:3 * D].to_broadcast([P, D])).then_inc(gate_bias_loaded, 16)
            act.dma_start(gate_rows[:, 1, :], b_ada[0:1, 5 * D:6 * D].to_broadcast([P, D])).then_inc(gate_bias_loaded, 16)
            act.dma_start(lam_in[:, :, :], even_lambda.to_broadcast([P, 4, HD])).then_inc(small_loaded, 16)
            act.dma_start(subln[:, :], even_subln.to_broadcast([P, P])).then_inc(small_loaded, 16)

            def split(u):
                if u >= len(units):
                    return
                act.wait_ge(weight_loaded[u % RAW], landed[u])
                if u >= SPLIT:
                    act.wait_ge(unit_used, u - SPLIT + 1)
                nc.scalar.activation(unit_view(w_hi, u % SPLIT, u), unit_view(raw, u % RAW, u), ACT.Copy)\
                    .then_inc(hi_ready, 1)

            def feed(us):
                for u, _ in us:
                    split(u + LOOK)

            def guess(st):
                v, y = stat[:, st["v"][0]:st["v"][1]], stat[:, st["y"][0]:st["y"][1]]
                act.wait_ge(variance_ready, st["i"] + 1)
                link(nc.scalar.activation(y, v, ACT.Ln))
                nc.scalar.activation(y, y, ACT.Exp, scale=-0.5).then_inc(guess_ready, 1)

            def turned_out(use, ti, scale, bias, kt):
                wait_ready(act, use)
                if ti >= 2:
                    act.wait_ge(split_done, plan.turned_groups[ti - 2] + 1)
                if scale is None:
                    nc.scalar.activation(turned[:, ti % 2, :], psum[:, use.bank, :], ACT.Copy).then_inc(turned_ready, 1)
                    return
                if scale[0] == "mod":
                    act.wait_ge(mod_final, 1 if scale[1] == 1 else 2)
                for i in range(2):
                    dst, src = turned[:, ti % 2, i * S:(i + 1) * S], psum[:, use.bank, i * S:(i + 1) * S]
                    k = kt + i
                    if scale[0] == "mod":
                        ins = nc.scalar.activation(dst, src, ACT.Identity, scale=mod[:, scale[1], k:k + 1],
                                                   bias=mod[:, bias[1], k:k + 1])
                    else:
                        ins = nc.scalar.activation(dst, src, ACT.Copy, scale=cols[:, scale[1] + k:scale[1] + k + 1])
                ins.then_inc(turned_ready, 1)

            for kind, a in steps:
                if kind == "vectors":
                    for u in range(LOOK):
                        split(u)
                    act.wait_ge(vectors_turned, 1)
                    nc.scalar.activation(c_act[:, :], cols[:, 0:KT], ACT.Silu).then_inc(c_act_ready, 1)
                    act.wait_ge(lam_dots, 1)
                    nc.scalar.activation(lam[:, 0:2], lam[:, 0:2], ACT.Exp).then_inc(lam_exp, 1)
                elif kind == "ada":
                    feed(a["units"])
                    if a["gate"] is None:
                        if a["slot_free"] is not None:
                            wait_read(act, a["slot_free"])
                        wait_ready(act, a["use"])
                        nc.scalar.activation(ada_row[:, a["row"] % 2, :], psum[:, a["use"].bank, :], ACT.Copy)\
                            .then_inc(psum_read[a["use"].bank], 1)
                elif kind == "stats":
                    st, uses = a["st"], a["uses"]
                    if a["after"]:
                        act.wait_ge(named[a["after"][0]], a["after"][1])
                    if a["src"] == "y":
                        for use in uses:
                            wait_ready(act, use)
                    for t in range(TT):
                        if a["src"] == "X":
                            src = X[:, t, :]
                        else:
                            b = uses[2 * t].bank
                            src = psum[:, b:b + 2, :].rearrange("p b n -> p (b n)")
                        ins = nc.scalar.activation(junk[:, :], src, ACT.Square,
                                                   accum_out=stat[:, st["ss"][0] + t:st["ss"][0] + t + 1])
                        if t == 0:
                            link(ins)
                    ins.then_inc(squares_ready, 1)
                    guess(st)
                elif kind == "diffout":
                    for t in range(TT):
                        use = a["uses"][t]
                        wait_ready(act, use)
                        nc.scalar.activation(scr[:, t, BANK:D], psum[:, use.bank, :], ACT.Square)
                        nc.scalar.activation(scr[:, t, 0:BANK], psum[:, use.bank, :], ACT.Copy)\
                            .then_inc(psum_read[use.bank], 1)
                    guess(a["st"])
                elif kind == "turn":
                    turned_out(a["use"], a["ti"], a["scale"], a["bias"], a["kt"])
                elif kind == "proj":
                    feed(a["units"])
                    if a["mode"] == "hold":
                        continue
                    for t in range(TT):
                        use = a["uses"][t]
                        wait_ready(act, use)
                        dst, src = pr[:, t, a["dst"]:a["dst"] + a["n"]], psum[:, use.bank, 0:a["n"]]
                        if a["mode"] == "rstd":
                            act.wait_ge(rstd_ready, a["stat"]["i"] + 1)
                            ins = nc.scalar.activation(dst, src, ACT.Copy, scale=col(a["stat"], "r", t))
                        else:
                            ins = nc.scalar.activation(dst, src, ACT.Sigmoid if a["mode"] == "sigmoid" else ACT.Copy)
                        ins.then_inc(psum_read[use.bank], 1)
                elif kind == "headturn":
                    wait_ready(act, a["use"])
                    nc.scalar.activation(QK[:, a["block"]:a["block"] + 2, :].rearrange("p b n -> p (b n)"),
                                         psum[:, a["use"].bank, :], ACT.Copy).then_inc(psum_read[a["use"].bank], 1)
                elif kind == "idxturn":
                    for use, dst, w in ((a["uses"][0], IT[:, 0:2, :].rearrange("p b n -> p (b n)"), 2 * S),
                                        (a["uses"][1], IT[:, 2, :], S)):
                        wait_ready(act, use)
                        nc.scalar.activation(dst, psum[:, use.bank, 0:w], ACT.Copy).then_inc(psum_read[use.bank], 1)
                elif kind == "idx":
                    h, use = a["h"], a["use"]
                    wait_ready(act, use)
                    if h >= 2:
                        act.wait_ge(score_ready, h - 1)
                    nc.scalar.activation(logit[:, h % 2, :], psum[:, use.bank, 0:SC], ACT.Relu,
                                         scale=IDX_HEADS ** -0.5 * IDX_DIM ** -0.5).then_inc(psum_read[use.bank], 1)
                elif kind == "qk":
                    n_ = a["n"]
                    act.wait_ge(logits_ready, n_ + 1)
                    for t, (b, e) in enumerate(((0, P), (P, SC))):
                        ins = nc.scalar.activation(prob[:, n_ % 4, b:e], logit[:, n_ % 2, b:e], ACT.Exp,
                                                   bias=nmax[:, n_, t:t + 1], accum_out=sums[:, n_, t:t + 1])
                    ins.then_inc(probs_ready, 1)
                elif kind == "probturn":
                    wait_ready(act, a["use"])
                    nc.scalar.activation(probT[:, a["k"] % 2, :], psum[:, a["use"].bank, 0:SC], ACT.Copy)\
                        .then_inc(psum_read[a["use"].bank], 1)
                elif kind == "sb_z":
                    m, use = a["m"], a["use"]
                    wait_ready(act, use)
                    nc.scalar.activation(logit[:, m % 2, :], psum[:, use.bank, 0:SC], ACT.Copy, scale=SCALE)\
                        .then_inc(psum_read[use.bank], 1)
                    act.wait_ge(small_z_ready, m + 1)
                    link(nc.scalar.activation(prob[:, m % 4, :], prob[:, m % 4, :], ACT.Exp))
                    nc.scalar.activation(prob[:, m % 4, :], prob[:, m % 4, :], ACT.Ln, bias=1.0).then_inc(keep_ready, 1)
                elif kind == "sb_cum":
                    m = a["m"]
                    wait_read(act, a["use"])
                    nc.scalar.activation(logit[:, m % 2, :], logit[:, m % 2, :], ACT.Exp).then_inc(weight_ready, 1)
                elif kind == "up":
                    feed(a["units"])
                    c_ = a["c"]
                    for t in range(TT):
                        use = a["uses"][t]
                        wait_ready(act, use)
                        if a["conv"]:
                            nc.scalar.activation(ub[:, c_ % 2, t, :], psum[:, use.bank, :], ACT.Copy)\
                                .then_inc(psum_read[use.bank], 1)
                        else:
                            if c_ == 0:
                                act.wait_ge(rstd_ready, a["stat"]["i"] + 1)
                            nc.scalar.activation(sg[:, c_ % 2, t, :], psum[:, use.bank, 0:FC], ACT.Silu,
                                                 scale=col(a["stat"], "r", t)).then_inc(silu_ready, 1)
                elif kind == "down":
                    feed([(a["unit"], 0)])
                elif kind == "hturn":
                    if not a["conv"]:
                        turned_out(a["uses"][0], a["ti"], None, None, None)
                        continue
                    for half in (1, 0):
                        use = a["uses"][half]
                        wait_ready(act, use)
                        for i in range(2):
                            f = 2 * half + i
                            tile = half * (CONV // 2) + 2 * a["c"] + i
                            nc.scalar.activation(cv[:, f * S:(f + 1) * S], psum[:, use.bank, i * S:(i + 1) * S],
                                                 ACT.Identity, scale=conv_c[:, 2 * CONV + tile:2 * CONV + tile + 1],
                                                 bias=conv_c[:, 3 * CONV + tile:3 * CONV + tile + 1])\
                                .then_inc(conv_first, 1)
                    wait_read(act, a["uses"][1])
                    nc.scalar.activation(gg, cv[:, 2 * S:4 * S], ACT.Gelu_apprx_tanh).then_inc(gelu_ready, 1)

        @block.vector
        def _(dve):
            n = [0]

            def mark(ins):
                ins.then_inc(dve_step, 1)
                n[0] += 1
                return n[0]

            def link(ins):
                dve.wait_ge(dve_step, mark(ins))

            def split(u):
                if u >= len(units):
                    return
                dve.wait_ge(hi_ready, u + 1)
                nc.vector.tensor_tensor(unit_view(w_lo, u % SPLIT, u), unit_view(raw, u % RAW, u),
                                        unit_view(w_hi, u % SPLIT, u).bitcast(F32), ALU.subtract).then_inc(lo_ready, 1)

            def feed(us):
                for u, _ in us:
                    split(u + LOOK)

            def split_group(dst_hi, dst_lo, src):
                link(nc.vector.tensor_copy(dst_hi, src))
                nc.vector.tensor_tensor(dst_lo, src, dst_hi.bitcast(F32), ALU.subtract).then_inc(split_done, 1)

            def rms(st, size):
                ss, v, y, t, r = (stat[:, st[k][0]:st[k][1]] for k in ("ss", "v", "y", "t", "r"))
                nc.vector.tensor_scalar(v, ss, 1.0 / size, EPS, ALU.mult, ALU.add).then_inc(variance_ready, 1)
                dve.wait_ge(guess_ready, st["i"] + 1)
                link(nc.vector.tensor_tensor(t, y, y, ALU.mult))
                link(nc.vector.scalar_tensor_tensor(t, t, -0.5, v, ALU.mult, ALU.mult))
                nc.vector.scalar_tensor_tensor(r, t, 1.5, y, ALU.add, ALU.mult).then_inc(rstd_ready, 1)
                dve.wait_ge(rstd_ready, st["i"] + 1)

            x_v = [0]
            for kind, a in steps:
                if kind == "vectors":
                    for use, dst, w in ((a["uses"][0], cols[:, :], NV), (a["uses"][1], ada_b[:, :], 48),
                                        (a["uses"][2], conv_c[:, 0:88], 88), (a["uses"][3], conv_c[:, 88:176], 88)):
                        wait_ready(dve, use)
                        ins = nc.vector.tensor_copy(dst, psum[:, use.bank, 0:w])
                        ins.then_inc(psum_read[use.bank], 1)
                    for use in a["uses"]:
                        wait_read(dve, use)
                    nc.vector.memset(top[:, :], 0.0).then_inc(vectors_turned, 1)
                    dve.wait_ge(c_act_ready, 1)
                    bc = c_act[:, :, None].to_broadcast([P, KT, P])
                    hi = hc_hi[:, :, :].rearrange("p b (k n) -> p (b k) n", n=P)
                    lo = hc_lo[:, :, :].rearrange("p b (k n) -> p (b k) n", n=P)
                    link(nc.vector.tensor_copy(hi, bc))
                    nc.vector.tensor_tensor(lo, bc, hi.bitcast(F32), ALU.subtract).then_inc(c_split, 1)
                    for u in range(LOOK):
                        split(u)
                    dve.wait_ge(small_loaded, 32)
                    link(nc.vector.tensor_tensor(work[:, 0:2 * HD].rearrange("p (a n) -> p a n", a=2),
                                                 lam_in[:, 0::2, :], lam_in[:, 1::2, :], ALU.mult))
                    nc.vector.tensor_reduce(lam[:, 0:2], work[:, 0:2 * HD].rearrange("p (a n) -> p a n", a=2), AX.X,
                                            ALU.add).then_inc(lam_dots, 1)
                elif kind == "ada":
                    feed(a["units"])
                    if a["gate"] is not None:
                        use, half = a["use"], a["n"] % 2
                        dst = gate_rows[:, a["gate"], half * BANK:(half + 1) * BANK]
                        dve.wait_ge(gate_bias_loaded, 32)
                        wait_ready(dve, use)
                        nc.vector.tensor_tensor(dst, psum[:, use.bank, :], dst, ALU.add).then_inc(psum_read[use.bank], 1)
                elif kind == "adacol":
                    use, k0 = a["use"], 4 * (a["n"] % 2)
                    wait_ready(dve, use)
                    nc.vector.tensor_tensor(mod[:, a["vec"], k0:k0 + 4], psum[:, use.bank, 0:4],
                                            ada_b[:, 4 * a["n"]:4 * a["n"] + 4], ALU.add)\
                        .then_inc(psum_read[use.bank], 1)
                    wait_read(dve, use)
                elif kind == "modfinal":
                    nc.vector.scalar_tensor_tensor(mod[:, a["vec"], :], mod[:, a["vec"], :], 1.0,
                                                   cols[:, a["gain"]:a["gain"] + KT], ALU.add, ALU.mult)\
                        .then_inc(mod_final, 1)
                elif kind == "stats":
                    dve.wait_ge(squares_ready, a["si"])
                    rms(a["st"], D)
                elif kind == "normalise":
                    for t in range(TT):
                        ins = nc.vector.tensor_scalar(scr[:, t, :], X[:, t, :], col(a["st"], "r", t), None, ALU.mult)
                        if t == 0:
                            link(ins)
                    ins.then_inc(scr_ready, 1)
                elif kind == "turn":
                    if a["read_before"] is not None:
                        dve.wait_ge(unit_used, a["read_before"] + 1)
                    dve.wait_ge(turned_ready, a["ti"] + 1)
                    k = a["kt"]
                    split_group(hT_hi[:, k:k + 2, :].rearrange("p k n -> p (k n)"),
                                hT_lo[:, k:k + 2, :].rearrange("p k n -> p (k n)"), turned[:, a["ti"] % 2, :])
                elif kind == "proj":
                    feed(a["units"])
                elif kind == "down":
                    feed([(a["unit"], 0)])
                elif kind == "rope":
                    c0, nh, dim, tab = a["col"], a["heads"], a["dim"], (r64 if a["dim"] == HD else r32)
                    w = nh * dim
                    for use in a["uses"]:
                        wait_read(dve, use)
                    dve.wait_ge(consts_loaded, 16)
                    if a["i"]:
                        dve.wait_ge(rope_ready, a["i"])
                    for t in range(TT):
                        xs = pr[:, t, c0:c0 + w].rearrange("p (h d) -> p h d", h=nh)
                        cs = tab[:, t, 0:dim][:, None, :].to_broadcast([P, nh, dim])
                        link(nc.vector.tensor_tensor(scr[:, t, 0:w].rearrange("p (h d) -> p h d", h=nh), xs, cs, ALU.mult))
                    dve.wait_ge(rope_swapped, a["i"] + 1)
                    ins = nc.vector.tensor_tensor(pr[:, :, c0:c0 + w], scr[:, :, 0:w], scr[:, :, BANK:BANK + w], ALU.add)
                    if a["replicate"]:
                        link(ins)
                        key = pr[:, :, c0 + 256:c0 + 288][:, :, None, :].to_broadcast([P, TT, 4, IDX_DIM])
                        ins = nc.vector.tensor_copy(work[:, 0:TT * P].rearrange("p (t r d) -> p t r d", t=TT, r=4), key)
                    ins.then_inc(rope_ready, 1)
                elif kind == "idx":
                    h, use = a["h"], a["use"]
                    wait_read(dve, use)
                    for t, (b, e) in enumerate(((0, P), (P, SC))):
                        wcol = pr[:, t, 6 * BANK + 288 + h:6 * BANK + 289 + h]
                        before = chunk_mask if h == 0 else selbias
                        ins = nc.vector.scalar_tensor_tensor(selbias[:, b:e], logit[:, h % 2, b:e], wcol, before[:, b:e],
                                                             ALU.mult, ALU.add)
                        if t == 0:
                            link(ins)
                    ins.then_inc(score_ready, 1)
                    dve.wait_ge(score_ready, h + 1)
                elif kind == "topk":
                    if a["j"] == 0:
                        link(nc.vector.tensor_copy(work[:, :], selbias[:, :]))
                    tiles = ((0, P), (P, SC))
                    for t, (b, e) in enumerate(tiles):
                        m = mark(nc.vector.max(top[:, 8 * t:8 * t + 8], work[:, b:e]))
                    dve.wait_ge(dve_step, m)
                    for t, (b, e) in enumerate(tiles):
                        m = mark(nc.vector.match_replace(work[:, b:e], top[:, 8 * t:8 * t + 8], work[:, b:e], NEG))
                    dve.wait_ge(dve_step, m)
                    if a["j"] == TOPK // 8 - 1:
                        link(nc.vector.tensor_scalar(work[:, :], work[:, :], NEG, -NEG, ALU.is_equal, ALU.mult))
                        nc.vector.scalar_tensor_tensor(selbias[:, :], work[:, :], NEG, chunk_mask, ALU.add, ALU.add)\
                            .then_inc(selected, 1)
                        dve.wait_ge(selected, 1)
                elif kind == "qk":
                    n_, h, use, bias = a["n"], a["h"], a["use"], a["bias"]
                    wait_ready(dve, use)
                    s_, lg = psum[:, use.bank, 0:SC], logit[:, n_ % 2, :]
                    if bias in rel_bias_rows:
                        if h == 0:
                            which = ("moba", "odd0", "odd1").index(bias)
                            dve.wait_ge(bias_loaded[which], 16 if which == 0 else 32)
                            if which:
                                dve.wait_ge(bias_cleared, which)
                        rows = rel_bias_rows[bias](h)
                        mark(nc.vector.scalar_tensor_tensor(lg[:, 0:P], s_[:, 0:P], SCALE, rows[:, P - 1::-1],
                                                            ALU.mult, ALU.add))
                        nc.vector.scalar_tensor_tensor(lg[:, P:SC], s_[:, P:SC], SCALE, rows[:, S - 1::-1],
                                                       ALU.mult, ALU.add).then_inc(psum_read[use.bank], 1)
                    else:
                        nc.vector.scalar_tensor_tensor(lg, s_, SCALE, chunk_mask if bias == "mask" else selbias[:, :],
                                                       ALU.mult, ALU.add).then_inc(psum_read[use.bank], 1)
                    wait_read(dve, use)
                    mark(nc.vector.tensor_reduce(nmax[:, n_, 0:1], lg[:, 0:P], AX.X, ALU.max, negate=True))
                    nc.vector.tensor_reduce(nmax[:, n_, 1:2], lg[:, P:SC], AX.X, ALU.max, negate=True)\
                        .then_inc(logits_ready, 1)
                elif kind == "mix":
                    n_ = a["n"]
                    dve.wait_ge(probs_ready, n_ + 1)
                    if n_ == 9:
                        dve.wait_ge(lam_exp, 1)
                        link(nc.vector.tensor_scalar(lam[:, 2:3], lam[:, 1:2], lam[:, 0:1], -LAMBDA_INIT, ALU.subtract,
                                                     ALU.add))
                    link(nc.vector.reciprocal(rsum[:, n_ - 1:n_ + 1, :], sums[:, n_ - 1:n_ + 1, :]))
                    link(nc.vector.tensor_scalar(rsum[:, n_, :], rsum[:, n_, :], lam[:, 2:3], None, ALU.mult))
                    for t, (b, e) in enumerate(((0, P), (P, SC))):
                        m = mark(nc.vector.tensor_scalar(prob[:, n_ % 4, b:e], prob[:, n_ % 4, b:e], rsum[:, n_, t:t + 1],
                                                         None, ALU.mult))
                    dve.wait_ge(dve_step, m)
                    for t, (b, e) in enumerate(((0, P), (P, SC))):
                        ins = nc.vector.scalar_tensor_tensor(prob[:, (n_ - 1) % 4, b:e], prob[:, (n_ - 1) % 4, b:e],
                                                             rsum[:, n_ - 1, t:t + 1], prob[:, n_ % 4, b:e],
                                                             ALU.mult, ALU.add)
                        if t == 0:
                            mark(ins)
                    ins.then_inc(mixed_ready, 1)
                elif kind == "oevac":
                    buf, c0 = bufs[a["dst"][0]], a["dst"][1]
                    if a["mode"] == "norm":
                        n0 = a["n0"]
                        dve.wait_ge(probs_ready, n0 + 8)
                        link(nc.vector.reciprocal(rsum[:, n0:n0 + 8, :], sums[:, n0:n0 + 8, :]))
                    for t in range(TT):
                        use = a["uses"][t]
                        wait_ready(dve, use)
                        if a["mode"] == "norm":
                            ins = nc.vector.tensor_tensor(
                                buf[:, t, c0:c0 + BANK].rearrange("p (h d) -> p h d", d=HD),
                                psum[:, use.bank, :].rearrange("p (h d) -> p h d", d=HD),
                                rsum[:, n0:n0 + 8, t:t + 1].to_broadcast([P, 8, HD]), ALU.mult)
                        else:
                            ins = nc.vector.tensor_copy(buf[:, t, c0:c0 + BANK], psum[:, use.bank, :])
                        if a["final"] and t == 1:
                            ins.then_inc(scr_ready, 1)
                        else:
                            ins.then_inc(psum_read[use.bank], 1)
                            wait_read(dve, use)
                elif kind == "diffout":
                    st = a["st"]
                    for t in range(TT):
                        wait_read(dve, a["uses"][t])
                        s0 = st["ss"][0] + 4 * t
                        m = mark(nc.vector.tensor_reduce(stat[:, s0:s0 + 4],
                                                         scr[:, t, BANK:D].rearrange("p (h d) -> p h d", h=4), AX.X,
                                                         ALU.add))
                    dve.wait_ge(dve_step, m)
                    rms(st, 2 * HD)
                    for t in range(TT):
                        o = scr[:, t, 0:BANK].rearrange("p (h d) -> p h d", h=4)
                        r0 = st["r"][0] + 4 * t
                        link(nc.vector.tensor_tensor(o, o, stat[:, r0:r0 + 4][:, :, None].to_broadcast([P, 4, P]),
                                                     ALU.mult))
                        link(nc.vector.scalar_tensor_tensor(o, o, 1.0 - LAMBDA_INIT,
                                                            subln[:, None, :].to_broadcast([P, 4, P]), ALU.mult, ALU.mult))
                elif kind == "sb_z":
                    m_ = a["m"]
                    z, l = logit[:, m_ % 2, :], prob[:, m_ % 4, :]
                    wait_read(dve, a["use"])
                    nc.vector.scalar_tensor_tensor(l, z, -1.0, z, ALU.mult, ALU.min).then_inc(small_z_ready, 1)
                    dve.wait_ge(keep_ready, m_ + 1)
                    nc.vector.scalar_tensor_tensor(l, z, 0.0, l, ALU.max, ALU.add).then_inc(softplus_ready, 1)
                elif kind == "sb_cum":
                    m_, use = a["m"], a["use"]
                    wait_ready(dve, use)
                    nc.vector.tensor_tensor(logit[:, m_ % 2, :], psum[:, use.bank, 0:SC], logit[:, m_ % 2, :], ALU.add)\
                        .then_inc(psum_read[use.bank], 1)
                elif kind == "mixbranch":
                    half = a["n"]
                    for t in range(TT):
                        ya, yb = a["ya"][t], a["yb"][t]
                        dst = scr[:, t, half * BANK:(half + 1) * BANK]
                        tmp = prob[:, :, :].rearrange("p a n -> p (a n)")[:, t * BANK:(t + 1) * BANK]
                        wait_ready(dve, ya)
                        nc.vector.tensor_tensor(dst, psum[:, ya.bank, :], pr[:, t, half * BANK:(half + 1) * BANK],
                                                ALU.mult).then_inc(psum_read[ya.bank], 1)
                        wait_ready(dve, yb)
                        nc.vector.tensor_tensor(tmp, psum[:, yb.bank, :],
                                                pr[:, t, (3 + half) * BANK:(4 + half) * BANK], ALU.mult)\
                            .then_inc(psum_read[yb.bank], 1)
                        wait_read(dve, ya)
                        wait_read(dve, yb)
                        ins = nc.vector.tensor_tensor(dst, dst, tmp, ALU.add)
                        if a["final"] and t == 1:
                            ins.then_inc(scr_ready, 1)
                        else:
                            link(ins)
                elif kind == "up":
                    feed(a["units"])
                    if not a["conv"]:
                        c_ = a["c"]
                        for t in range(TT):
                            use = a["uses"][t]
                            dve.wait_ge(silu_ready, TT * a["ci"] + t + 1)
                            nc.vector.scalar_tensor_tensor(hid[:, c_ % 2, t, :], psum[:, use.bank, FC:2 * FC],
                                                           col(a["stat"], "r", t), sg[:, c_ % 2, t, :],
                                                           ALU.mult, ALU.mult).then_inc(psum_read[use.bank], 1)
                elif kind == "hturn":
                    if a["down_before"] is not None:
                        dve.wait_ge(unit_used, a["down_before"] + 1)
                    hi, lo = hc_hi[:, a["c"] % 2, :], hc_lo[:, a["c"] % 2, :]
                    if not a["conv"]:
                        dve.wait_ge(turned_ready, a["ti"] + 1)
                        split_group(hi, lo, turned[:, a["ti"] % 2, :])
                        continue
                    done = 0
                    for half in (1, 0):
                        use = a["uses"][half]
                        dve.wait_ge(conv_first, 4 * a["cc"] + (2 if half else 4))
                        for tap, shift in ((1, 1), (0, 2)):
                            for i in range(2):
                                f, tile = 2 * half + i, half * (CONV // 2) + 2 * a["c"] + i
                                v = cv[:, f * S + shift:(f + 1) * S]
                                ins = nc.vector.scalar_tensor_tensor(
                                    v, psum[:, use.bank, i * S:(i + 1) * S - shift],
                                    conv_c[:, tap * CONV + tile:tap * CONV + tile + 1], v, ALU.mult, ALU.add)
                                if tap == 1 or i == 0:
                                    m = mark(ins)
                            if tap == 1:
                                dve.wait_ge(dve_step, m)
                        ins.then_inc(psum_read[use.bank], 1)
                    wait_read(dve, a["uses"][0])
                    dve.wait_ge(dve_step, m)
                    dve.wait_ge(gelu_ready, a["cc"] + 1)
                    link(nc.vector.tensor_tensor(hfull, gg, cv[:, 0:2 * S], ALU.mult))
                    split_group(hi, lo, hfull)
                elif kind == "post":
                    if a["mode"] == "norm":
                        dve.wait_ge(g_row_loaded, 16 * (a["row"] + 1))
                    for t in range(TT):
                        for half in range(2):
                            use = a["uses"][2 * t + half]
                            cs = slice(half * BANK, (half + 1) * BANK)
                            wait_ready(dve, use)
                            if a["mode"] == "norm":
                                ins = nc.vector.scalar_tensor_tensor(scr[:, t, cs], psum[:, use.bank, :],
                                                                     col(a["st"], "r", t), g_row[:, cs], ALU.mult, ALU.mult)
                            else:
                                ins = nc.vector.tensor_tensor(scr[:, t, cs], psum[:, use.bank, :],
                                                              gate_rows[:, a["gate"], cs], ALU.mult)
                            ins.then_inc(psum_read[use.bank], 1)
                            wait_read(dve, use)
                    link(nc.vector.scalar_tensor_tensor(X[:, 0, :], scr[:, 0, :], a.get("factor", 1.0), X[:, 0, :],
                                                        ALU.mult, ALU.add))
                    if a["mode"] == "norm":
                        nc.vector.memset(top[:, 0:1], 0.0).then_inc(g_row_used, 1)
                    nc.vector.scalar_tensor_tensor(X[:, 1, :], scr[:, 1, :], a.get("factor", 1.0), X[:, 1, :],
                                                   ALU.mult, ALU.add).then_inc(x_ready, 1)
                    x_v[0] += 1
                    dve.wait_ge(x_ready, x_v[0])
                elif kind == "finalnorm":
                    dve.wait_ge(g_row_loaded, 16 * (a["row"] + 1))
                    for t in range(TT):
                        ins = nc.vector.scalar_tensor_tensor(X[:, t, :], X[:, t, :], col(a["st"], "r", t), g_row[:, :],
                                                             ALU.mult, ALU.mult)
                        if t == 0:
                            link(ins)
                    ins.then_inc(x_ready, 1)
                    x_v[0] += 1
                    dve.wait_ge(x_ready, x_v[0])
                    nc.vector.memset(top[:, 0:1], 0.0).then_inc(g_row_used, 1)

        @block.tensor
        def _(pe):
            split_seen = [0]

            def need_group(g):
                if g + 1 > split_seen[0]:
                    pe.wait_ge(split_done, g + 1)
                    split_seen[0] = g + 1

            def need_unit(u):
                pe.wait_ge(hi_ready, u + 1)
                pe.wait_ge(lo_ready, u + 1)

            def product(o, a_hi, a_lo, b_hi, b_lo, start, stop):
                nc.tensor.matmul(o, a_hi, b_hi, start=start, stop=False)
                nc.tensor.matmul(o, a_hi, b_lo, start=False, stop=False)
                return nc.tensor.matmul(o, a_lo, b_hi, start=False, stop=stop)

            def chunk(a, k_tiles, outs, group0, k_base=0):
                for u, k0 in a["units"]:
                    need_unit(u)
                    nk, w, _ = units[u]
                    for k in range(nk):
                        kk = k_base + k0 + k
                        need_group(group0 + kk // 2)
                        for t in range(TT):
                            sl = slice(t * P, (t + 1) * P)
                            b = slice(k * w, (k + 1) * w)
                            ins = product(psum[:, outs[t].bank, 0:w], hT_hi[:, kk, sl], hT_lo[:, kk, sl],
                                          w_hi[:, u % SPLIT, b], w_lo[:, u % SPLIT, b],
                                          k0 + k == 0, k0 + k == k_tiles - 1)
                    ins.then_inc(unit_used, 1)

            for kind, a in steps:
                if kind == "vectors":
                    pe.wait_ge(vectors_loaded, 16 * 8)
                    pe.wait_ge(consts_loaded, 16)
                    for i, (use, w) in enumerate(zip(a["uses"], (NV, 48, 88, 88))):
                        nc.tensor.transpose(psum[:, use.bank, 0:w], PR[0:w, i * P:(i + 1) * P], ident[0:w, 0:w])\
                            .then_inc(psum_ready[use.bank], 1)
                    pe.wait_ge(c_split, 1)
                elif kind == "ada":
                    use = a["use"]
                    wait_free(pe, use)
                    for u, k0 in a["units"]:
                        need_unit(u)
                        for k in range(4):
                            kk = k0 + k
                            sl = slice((kk % 4) * P, (kk % 4 + 1) * P)
                            b = slice(k * BANK, (k + 1) * BANK)
                            ins = product(psum[:, use.bank, :], hc_hi[:, kk // 4, sl], hc_lo[:, kk // 4, sl],
                                          w_hi[:, u % SPLIT, b], w_lo[:, u % SPLIT, b], kk == 0, kk == KT - 1)
                        ins.then_inc(unit_used, 1)
                elif kind == "adacol":
                    use = a["use"]
                    wait_free(pe, use)
                    wait_read(pe, a["row_use"])
                    pe.wait_ge(ones_ready, 1)
                    for j in range(4):
                        ins = nc.tensor.matmul(psum[:, use.bank, j:j + 1], ada_row[0:1, a["row"] % 2, j * P:(j + 1) * P],
                                               ones[0:1, 0:1], start=True, stop=True)
                    ins.then_inc(psum_ready[use.bank], 1)
                elif kind == "turn":
                    use, src = a["use"], bufs[a["src"]]
                    wait_free(pe, use)
                    if a["after"]:
                        pe.wait_ge(named[a["after"][0]], a["after"][1])
                    for i in range(2):
                        for t in range(TT):
                            k = a["kt"] + i
                            ins = nc.tensor.transpose(psum[:, use.bank, i * S + t * P:i * S + (t + 1) * P],
                                                      src[:, t, k * P:(k + 1) * P], ident)
                    ins.then_inc(psum_ready[use.bank], 1)
                elif kind == "proj":
                    for use in a["uses"]:
                        wait_free(pe, use)
                    chunk(a, 4 * len(a["units"]), a["uses"], a["g0"], a["k_base"])
                elif kind == "headturn":
                    use = a["use"]
                    wait_free(pe, use)
                    if a["after"][0] == "uses":
                        for u in a["after"][1]:
                            wait_read(pe, u)
                    else:
                        pe.wait_ge(rope_ready, a["after"][1])
                    for i in range(2):
                        for t in range(TT):
                            c0 = a["col"] + i * P
                            ins = nc.tensor.transpose(psum[:, use.bank, i * S + t * P:i * S + (t + 1) * P],
                                                      pr[:, t, c0:c0 + P], ident)
                    ins.then_inc(psum_ready[use.bank], 1)
                elif kind == "idxturn":
                    pe.wait_ge(rope_ready, a["after"][1])
                    use = a["uses"][0]
                    wait_free(pe, use)
                    for i in range(2):
                        for t in range(TT):
                            c0 = 6 * BANK + i * P
                            ins = nc.tensor.transpose(psum[:, use.bank, i * S + t * P:i * S + (t + 1) * P],
                                                      pr[:, t, c0:c0 + P], ident)
                    ins.then_inc(psum_ready[use.bank], 1)
                    use = a["uses"][1]
                    wait_free(pe, use)
                    for t in range(TT):
                        ins = nc.tensor.transpose(psum[:, use.bank, t * P:(t + 1) * P], work[:, t * P:(t + 1) * P], ident)
                    ins.then_inc(psum_ready[use.bank], 1)
                    for use in a["uses"]:
                        wait_read(pe, use)
                elif kind == "idx":
                    h, use = a["h"], a["use"]
                    wait_free(pe, use)
                    p0, b = IDX_DIM * (h % 4), h // 4
                    q, k = IT[p0:p0 + IDX_DIM, b, :], IT[p0:p0 + IDX_DIM, 2, :]
                    nc.tensor.matmul(psum[:, use.bank, 0:P], q[:, 0:P], k[:, 0:P], start=True, stop=True)
                    nc.tensor.matmul(psum[:, use.bank, P:SC], q[:, P:S], k[:, 0:S], start=True, stop=True)\
                        .then_inc(psum_ready[use.bank], 1)
                elif kind in ("qk", "sb_z"):
                    use = a["use"]
                    h, base = (a["h"], a["base"]) if kind == "qk" else (a["m"], 8)
                    for u in a["ready"]:
                        wait_read(pe, u)
                    wait_free(pe, use)
                    p0 = HD * (h % 2)
                    q, k = QK[p0:p0 + HD, base + h // 2, :], QK[p0:p0 + HD, base + 4 + h // 2, :]
                    if kind == "qk":
                        nc.tensor.matmul(psum[:, use.bank, 0:P], q[:, 0:P], k[:, 0:P], start=True, stop=True)
                        ins = nc.tensor.matmul(psum[:, use.bank, P:SC], q[:, P:S], k[:, 0:S], start=True, stop=True)
                    else:
                        nc.tensor.matmul(psum[:, use.bank, 0:S], k[:, 0:P], q[:, 0:S], start=True, stop=True)
                        ins = nc.tensor.matmul(psum[:, use.bank, S:SC], k[:, P:S], q[:, P:S], start=True, stop=True)
                    ins.then_inc(psum_ready[use.bank], 1)
                elif kind == "probturn":
                    n_, use = a["n"], a["use"]
                    wait_free(pe, use)
                    if a["diff"]:
                        pe.wait_ge(mixed_ready, (n_ - 7) // 2)
                        src = prob[:, (n_ - 1) % 4, :]
                    else:
                        pe.wait_ge(probs_ready, n_ + 1)
                        src = prob[:, n_ % 4, :]
                    for b in range(3):
                        ins = nc.tensor.transpose(psum[:, use.bank, b * P:(b + 1) * P], src[:, b * P:(b + 1) * P], ident)
                    ins.then_inc(psum_ready[use.bank], 1)
                elif kind in ("pv", "sb_pv"):
                    if kind == "pv":
                        if a["first"]:
                            for u in a["v_ready"]:
                                wait_read(pe, u)
                            for u in a["uses"]:
                                wait_free(pe, u)
                        wait_read(pe, a["turned"])
                        pT, w, o0, last = probT[:, a["k"] % 2, :], a["w"], a["slot"] * a["w"], a["last"]
                    else:
                        m = a["m"]
                        if m == 0:
                            for u in a["v_ready"]:
                                wait_read(pe, u)
                            for u in a["uses"]:
                                wait_free(pe, u)
                        pe.wait_ge(weight_masked, m + 1)
                        pT, w, o0, last = logit[:, m % 2, :], HD, m * HD, m == 7
                    vc = a["v"]
                    b0, b1 = a["uses"][0].bank, a["uses"][1].bank
                    ins = nc.tensor.matmul(psum[:, b0, o0:o0 + w], pT[:, 0:P], pr[:, 0, vc:vc + w], start=True, stop=True)
                    if last:
                        ins.then_inc(psum_ready[b0], 1)
                    nc.tensor.matmul(psum[:, b1, o0:o0 + w], pT[:, P:2 * P], pr[:, 0, vc:vc + w], start=True, stop=False)
                    ins = nc.tensor.matmul(psum[:, b1, o0:o0 + w], pT[:, 2 * P:SC], pr[:, 1, vc:vc + w], start=False,
                                           stop=True)
                    if last:
                        ins.then_inc(psum_ready[b1], 1)
                elif kind == "sb_cum":
                    m, use = a["m"], a["use"]
                    wait_free(pe, use)
                    pe.wait_ge(log_keep_ready, m + 1)
                    pe.wait_ge(ones_ready, 1)
                    lk, o = probT[:, m % 2, :], psum[:, use.bank, :]
                    nc.tensor.matmul(o[:, 0:S], later, lk[:, 0:S], start=True, stop=False)
                    nc.tensor.matmul(o[:, P:S], ones[:, :], lk[:, S:SC], start=False, stop=True)
                    nc.tensor.matmul(o[:, S:SC], later, lk[:, S:SC], start=True, stop=True)\
                        .then_inc(psum_ready[use.bank], 1)
                elif kind == "up":
                    for use in a["uses"]:
                        wait_free(pe, use)
                    chunk(a, KT, a["uses"], a["g0"])
                elif kind == "hturn":
                    for use in a["uses"]:
                        wait_free(pe, use)
                    for use in a["ups"]:
                        wait_read(pe, use)
                    src = (ub if a["conv"] else hid)[:, a["c"] % 2]
                    for i, use in enumerate(a["uses"]):
                        for f in range(2):
                            for t in range(TT):
                                c0 = (2 * i + f) * P
                                ins = nc.tensor.transpose(psum[:, use.bank, f * S + t * P:f * S + (t + 1) * P],
                                                          src[:, t, c0:c0 + P], ident)
                        ins.then_inc(psum_ready[use.bank], 1)
                elif kind == "down":
                    c_, u = a["c"], a["unit"]
                    need_unit(u)
                    need_group(a["g"])
                    if c_ == 0:
                        for use in a["uses"]:
                            wait_free(pe, use)
                    for k in range(2):
                        for t in range(TT):
                            sl = slice(k * S + t * P, k * S + (t + 1) * P)
                            for half in range(2):
                                b = slice(k * D + half * BANK, k * D + (half + 1) * BANK)
                                ins = product(psum[:, a["uses"][2 * t + half].bank, :], hc_hi[:, c_ % 2, sl],
                                              hc_lo[:, c_ % 2, sl], w_hi[:, u % SPLIT, b], w_lo[:, u % SPLIT, b],
                                              c_ == 0 and k == 0, c_ == NFC - 1 and k == 1)
                    ins.then_inc(unit_used, 1)


_INS = ["x", "c", "w_ada", "b_ada", "g_mix", "w_in", "w_br_moba", "w_br_sb", "w_out", "rel_bias", "g_ffn", "w_up",
        "w_conv", "b_conv", "w_down", "g_final", "norm_g_2", "ffn_wg_2", "ffn_wu_2", "ffn_wd_2", "even_w_in_2",
        "even_w_out_2", "even_lambda_2", "even_subln_2", "odd_w_in_2", "odd_w_out_2", "odd_rel_bias_2"]


def kernel(**inputs):
    import concourse.bacc as bacc
    from concourse.bass_utils import run_bass_kernel_spmd

    nc = bacc.Bacc("TRN2", target_bir_lowering=False, num_devices=1)
    arrays, args = {}, []
    for name, a in [("consts", constants())] + [(name, inputs[name]) for name in _INS]:
        a = np.ascontiguousarray(a)
        arrays[f"in_{name}_dram"] = a
        args.append(nc.dram_tensor(f"in_{name}_dram", a.shape, mybir.dt.from_np(a.dtype), kind="ExternalInput").ap())
    args.append(nc.dram_tensor("distance_table", (8, BIAS_T), F32, kind="Internal").ap())
    args.append(nc.dram_tensor("out_0_dram", (1, S, D), F32, kind="ExternalOutput").ap())
    program(nc, *args)
    r = run_bass_kernel_spmd(nc, [arrays], core_ids=[0])
    return r.results[0]["out_0_dram"]
```

```python
from contextlib import ExitStack

import numpy as np

import concourse.bass as bass
from concourse import mybir

F32 = mybir.dt.float32
F32R = mybir.dt.float32r
BF16 = mybir.dt.bfloat16
I32 = mybir.dt.int32
ACT = mybir.ActivationFunctionType
ALU = mybir.AluOpType
AX = mybir.AxisListType

P = 128
S = 256
TT = S // P
D = 1024
KT = D // P
HD = 64
D_FF = 2816
FC = 256
NFC = D_FF // FC
CONV = 2 * D_FF // P
BANK = 512
UNIT = 2048
RAW, SPLIT = 3, 3
LOOK = SPLIT - 1
EPS = 1e-6
NEG = -1e30
SCALE = HD ** -0.5
REL_BUCKETS = 32
REL_MAX_DIST = 128
CHUNK = 64
IDX_HEADS, IDX_DIM, TOPK = 8, 32, 64
LAMBDA_INIT = 0.2
EVEN_W = 3368
SC = P + S
BIAS_T = S + P - 1


def t5_bounds():
    exact = REL_BUCKETS // 2
    n = np.arange(S)
    large = exact + (np.log(np.maximum(n, exact).astype(np.float32) / exact)
                     / np.log(REL_MAX_DIST / exact) * (REL_BUCKETS - exact)).astype(np.int32)
    b = np.where(n < exact, n, np.minimum(large, REL_BUCKETS - 1))
    return [int(np.argmax(b >= i)) for i in range(REL_BUCKETS)] + [S]


def constants():
    p = np.arange(P)[:, None]
    k = np.arange(P)[None, :]
    ident = np.eye(P, dtype=np.float32)
    later = (p >= k).astype(np.float32)
    q_of = np.concatenate([p + 0 * k, p + P + 0 * k, p + P + 0 * k], 1)
    k_of = np.concatenate([k + 0 * p, k + 0 * p, k + P + 0 * p], 1)
    chunk_mask = np.where(k_of // CHUNK <= q_of // CHUNK, 0.0, NEG).astype(np.float32)
    past = np.concatenate([p < k, p < k + P, p < k], 1)
    minus_past = -past.astype(np.float32)

    def rope(dim):
        inv = (np.float32(10000.0) ** (-np.arange(0, dim, 2, dtype=np.float32) / np.float32(dim))).astype(np.float32)
        ang = (np.arange(S, dtype=np.float32)[:, None] * inv[None, :]).astype(np.float32)
        c, s = np.cos(ang), np.sin(ang)
        both = np.concatenate([c, c, -s, s], 1).astype(np.float32)
        return both.reshape(TT, P, 2 * dim).transpose(1, 0, 2).reshape(P, TT * 2 * dim)

    return np.ascontiguousarray(np.concatenate(
        [ident, later, chunk_mask, minus_past, rope(HD), rope(IDX_DIM)], 1).astype(np.float32))


class Use:

    def __init__(self, bank, prev, unit, ready, evacuated):
        self.bank, self.prev, self.unit, self.ready = bank, prev, unit, ready
        self.read_by = ("psum_read", evacuated)


class Plan:

    def __init__(self):
        self.steps, self.units, self.ada_units = [], [], []
        self.tenant, self.announced, self.evacuated = [None] * 8, [0] * 8, [0] * 8
        self.ropes = 0
        self.turned, self.turned_groups, self.squares = 0, [], 0
        self.splits = 0
        self.stats = 0
        self.stat_cols = 0

    def add(self, kind, **kw):
        self.steps.append((kind, kw))

    def unit(self, nk, w, parts):
        self.units.append((nk, w, parts))
        return len(self.units) - 1

    def use(self, bank, unit=None, read_by=None, by_unit=False):
        if unit is None and not by_unit:
            self.announced[bank] += 1
        if read_by is None:
            self.evacuated[bank] += 1
        use = Use(bank, self.tenant[bank], unit, self.announced[bank], self.evacuated[bank])
        if read_by is not None:
            use.read_by = read_by
        self.tenant[bank] = use
        return use

    def turned_use(self, bank):
        self.turned += 1
        return self.use(bank, read_by=("turned_ready", self.turned))

    def turn(self):
        self.splits += 1
        return self.splits - 1

    def new_stat(self, width, squares=0):
        c, i = self.stat_cols, self.stats
        self.stat_cols += 5 * width
        self.stats += 1
        self.squares += squares
        return dict(i=i, w=width, ss=(c, c + width), ss2=(c + width, c + 2 * width), v=(c + 2 * width, c + 3 * width),
                    t=(c + 3 * width, c + 4 * width), r=(c + 4 * width, c + 5 * width), squares=self.squares - squares)

    def load_order(self):
        order = []
        for kind, a in self.steps:
            if kind == "prime":
                order += [("w", s) for s in range(LOOK)]
            elif kind == "ada":
                order.append(("a", a["unit"]))
            elif kind in ("proj", "up", "down"):
                order += [("w", a["unit"] + LOOK)] if a["unit"] + LOOK < len(self.units) else []
        return order



def build_plan(W):
    pl = Plan()
    n_attn, n_sb, n_turned_heads, n_x, n_scr = [0], [0], [0], [0], [0]
    last_hT_unit = [None]

    def rows(w, k0, nk, c0, n):
        return w[k0 * P:(k0 + nk) * P, c0:c0 + n].rearrange("(k p) n -> p k n", p=P)

    def column_units(w, k_tiles, c0, n):
        made = []
        for k0 in range(0, k_tiles, 4):
            u = pl.unit(4, n, [(0, n, rows(w, k0, 4, c0, n))])
            made.append((u, k0))
        return made

    free_pair = [0]

    def pair():
        free_pair[0] ^= 1
        return (4, 5) if free_pair[0] else (6, 7)

    def proj(w, c0, n, dst, mode, banks=None, stat=None, k_tiles=KT, k_base=0, g0=0):
        us = column_units(w, k_tiles, c0, n)
        banks = banks or pair()
        uses = [pl.use(b, us[-1][0]) for b in banks]
        last_hT_unit[0] = us[-1][0]
        return uses, [dict(unit=u, k0=k0, n=n, dst=dst, mode=mode, uses=uses, stat=stat, k_base=k_base, g0=g0,
                           k_tiles=k_tiles, last=u == us[-1][0]) for u, k0 in us]

    def now(made):
        uses, parts = made
        for p in parts:
            pl.add("proj", **p)
        return uses

    sum_uses = []

    def ada(n, part):
        pl.ada_units.append((4, BANK, [(0, BANK, rows(W["w_ada"], 4 * part, 4, n * BANK, BANK))]))
        pl.add("ada", n=n, part=part, unit=len(pl.ada_units) - 1, slot_free=sum_uses[n - 2] if n >= 2 else None)

    def adasum(n, bank):
        gate = {4: 0, 5: 0, 10: 1, 11: 1}.get(n)
        use = pl.use(bank)
        sum_uses.append(use)
        pl.add("adasum", n=n, use=use, gate=gate, vec={0: 0, 1: 1, 3: 2, 4: 3}.get(n // 2))

    def group():
        g = pl.turn()
        pl.turned_groups.append(g)
        return g

    def turn(src, after, scale, bias, k0=0, nk=KT, banks=(4, 5, 6, 7)):
        first = pl.splits
        for j in range(nk // 2):
            if after[0] == "x_ready":
                w = ("x_ready", 2 * after[1] - 1) if j == 0 else ("x_ready", 2 * after[1]) if j == 2 else None
            else:
                w = after if j == 0 else None
            pl.add("turn", src=src, after=w, scale=scale, bias=bias,
                   kt=k0 + 2 * j, use=pl.turned_use(banks[j % len(banks)]), ti=pl.turned - 1, g=group(),
                   read_before=last_hT_unit[0])
        return first

    def stats(after):
        st = pl.new_stat(TT, TT)
        if after[0] == "x_ready":
            after = ("x_ready", 2 * after[1])
        pl.add("stats", after=after, st=st)
        return st

    def head_turn(col, block, banks, after):
        use = pl.use(banks)
        pl.add("headturn", col=col, block=block, use=use, after=after)
        return use

    def softmax_heads(name, fillers, bias, v_col, v_w, q_ready, v_ready, diff=False, base=0):
        n0 = n_attn[0]
        n_attn[0] += 8
        pend_v = []
        fill = list(fillers)

        def t_of(h):
            k = n_turned_heads[0]
            n_turned_heads[0] += 1
            use = pl.use(2 + k % 2)
            pl.add("probturn", n=n0 + h, k=k, use=use, diff=diff)
            return k, use

        state = dict(o=None)

        def pv(h, kt):
            first = state["o"] is None
            if first:
                state["o"] = [pl.use(0), pl.use(1)]
            nv = (h // 2) if diff else h
            last = h == 7
            pl.add("pv", n=n0 + h, k=kt[0], turned=kt[1], slot=nv, v=v_col + nv * v_w, w=v_w, uses=state["o"], first=first, last=last,
                   v_ready=v_ready)

        for i in range(8 + 2):
            if i < 8:
                h = i
                pl.add("qk", name=name, n=n0 + h, h=h, base=base, use=pl.use(4 + (n0 + h) % 2), bias=bias,
                       ready=q_ready(h))
            if fill:
                for f in fill.pop(0):
                    f()
            ready_v = len(pend_v)
            if 1 <= i <= 8:
                if not diff:
                    pend_v.append((i - 1, t_of(i - 1)))
                elif (i - 1) % 2 == 1:
                    pl.add("mix", n=n0 + i - 1)
                    pend_v.append((i - 1, t_of(i - 1)))
            if i < 8:
                pl.add("exp", n=n0 + i)
            if ready_v:
                pv(*pend_v.pop(0))
        while pend_v:
            pv(*pend_v.pop(0))
        while fill:
            for f in fill.pop(0):
                f()
        return n0, state["o"]

    def sb_heads(fillers, v_col, q_ready, v_ready):
        fill = list(fillers)
        o = [pl.use(0), pl.use(1)]
        cums = {}
        for i in range(8 + 3):
            if i < 8:
                pl.add("sb_z", m=i, use=pl.use(4 + i % 2), ready=q_ready(i))
            if fill:
                for f in fill.pop(0):
                    f()
            if 2 <= i <= 9:
                pl.add("sb_arg", m=i - 2, use=cums[i - 2])
            if 1 <= i <= 8:
                m = i - 1
                cums[m] = pl.use(2 + n_turned_heads[0] % 2)
                n_turned_heads[0] += 1
                pl.add("sb_keep", m=m)
                pl.add("sb_cum", m=m, use=cums[m])
            if i >= 3:
                m = i - 3
                pl.add("sb_pv", m=m, v=v_col + m * HD, uses=o, v_ready=v_ready)
        while fill:
            for f in fill.pop(0):
                f()
        return o

    def ffn(up_units, stat, conv, g0, w_down):
        y = [None] * 4
        ups = {}

        def up(c):
            us = up_units(c)
            banks = (4, 5) if c % 2 == 0 else (6, 7)
            uses = [pl.use(b, us[-1][0]) for b in banks]
            ups[c] = uses
            last_hT_unit[0] = us[-1][0]
            return [lambda u=u, k0=k0: pl.add("up", c=c, unit=u, k0=k0, uses=uses, stat=stat, conv=conv, g0=g0,
                                              ci=chunk_no[0] + c, last=k0 > 0) for u, k0 in us]

        def turn_hidden(c):
            banks = (4, 5) if c % 2 == 0 else (6, 7)
            uses = [pl.use(b) for b in banks] if conv else [pl.turned_use(banks[0])]
            g = pl.turn() if conv else group()
            before = downs[c - 2] if c >= 2 else None
            pl.add("hturn", c=c, ci=chunk_no[0] + c, uses=uses, ups=ups[c], conv=conv, g=g, down_before=before,
                   cc=conv_no[0] + c, ti=pl.turned - 1)
            gs[c] = g

        def down(c):
            u = pl.unit(2, D, [(0, D, rows(w_down, 2 * c, 2, 0, D))])
            downs[c] = u
            if c == 0:
                for b in range(4):
                    y[b] = pl.use(b, by_unit=b == 3)
            pl.add("down", c=c, unit=u, uses=y, g=gs[c])

        downs, gs = {}, {}
        for stage in up(0):
            stage()
        for c in range(1, NFC):
            first, second = up(c)
            first()
            if c == 1:
                turn_hidden(0)
            second()
            down(c - 1)
            turn_hidden(c)
        down(NFC - 1)
        y[3].unit = downs[NFC - 1]
        if not conv:
            chunk_no[0] += NFC
        else:
            conv_no[0] += NFC
        return y

    chunk_no, conv_no = [0], [0]

    def post(mode, y, **kw):
        pl.add("post", mode=mode, uses=y, row=rows_used[0], **kw)
        if mode == "norm":
            rows_used[0] += 1
        n_x[0] += 1
    rows_used = [0]

    def o_evac(o, dst, final, n0=None):
        if final:
            o[1].read_by = ("scr_ready", n_scr[0])
            pl.evacuated[o[1].bank] -= 1
        pl.add("oevac", mode="plain" if n0 is None else "norm", uses=o, n0=n0, dst=dst, final=final)

    def scr_version():
        n_scr[0] += 1
        return n_scr[0]

    pl.add("vectors", uses=[pl.use(b) for b in (4, 5, 6, 7)])
    st = None
    for n in range(4):
        ada(n, 0)
        ada(n, 1)
        if n == 0:
            st = stats(("x_loaded", 16))
        adasum(n, n)
    pl.add("modfinal", vec=1, gain=8)
    pl.add("normalise", st=st)
    pl.add("prime")
    v = scr_version()
    g0 = turn("scr", ("scr_ready", v), ("mod", 1), ("mod", 0))
    pl.add("load_bias", which=0, after=("split_done", pl.splits))
    r = {}

    def w_in_chunk(i, dst, mode, banks=None):
        return proj(W["w_in"], i * BANK, BANK, dst, mode, banks, g0=g0)

    def turns_of(name, i, blk, bank, after):
        for t in range(2):
            r[name + str(t)] = head_turn(i * BANK + 256 * t, blk + 2 * t, bank + t, after)

    def q_ready_of(q, k):
        return lambda h: [r[q + str(h // 4)], r[k + str(h // 4)]]

    later_ada = [(n, part) for n in range(4, 12) for part in range(2)]

    def ada_next(k, bank=3):
        for _ in range(k):
            n, part = later_ada.pop(0)
            ada(n, part)
            if part:
                adasum(n, bank)

    r["qa"] = now(w_in_chunk(0, 0, "plain"))
    ada_next(1)
    r["ka"] = now(w_in_chunk(1, BANK, "plain"))
    turns_of("qa", 0, 0, 2, ("uses", r["qa"]))
    ada_next(1)
    r["va"] = now(w_in_chunk(2, 2 * BANK, "plain"))
    turns_of("ka", 1, 4, 2, ("uses", r["ka"]))

    fillers = []

    def chunk_fillers(name, i, dst, mode):
        made = {}

        def first():
            made["uses"], made["parts"] = w_in_chunk(i, dst, mode, (6, 7))
            r[name] = made["uses"]
            pl.add("proj", **made["parts"][0])

        def second():
            pl.add("proj", **made["parts"][1])
        return first, second

    fa = []
    for name, i in (("qb", 3), ("kb", 4), ("vb", 5)):
        first, second = chunk_fillers(name, i, i * BANK, "plain")
        fa += [[first, lambda: ada_next(1)], [second]]
    fa.append([lambda: turns_of("qb", 3, 8, 6, ("uses", r["qb"])), lambda: turns_of("kb", 4, 12, 6, ("uses", r["kb"]))])
    fb = []
    for i in range(4):
        first, second = chunk_fillers(f"gate{i}", 6 + i, (0, BANK, 3 * BANK, 4 * BANK)[i], "tanh")
        fb += [[first, lambda: ada_next(1)], [second, lambda: ada_next(1)]]
    n0, o = softmax_heads("moba", fa, "moba", 2 * BANK, HD, q_ready_of("qa", "ka"), r["va"])
    o_evac(o, ("scr", 0), False, n0)
    o = sb_heads(fb, 5 * BANK, q_ready_of("qb", "kb"), r["vb"])
    v = scr_version()
    o_evac(o, ("scr", BANK), True)
    while later_ada:
        ada_next(1)
    g0 = turn("scr", ("scr_ready", v), None, None)
    for n in range(2):
        ua = now(proj(W["w_br_moba"], n * BANK, BANK, None, "hold", (4, 5), k_tiles=4, g0=g0))
        ub_ = now(proj(W["w_br_sb"], n * BANK, BANK, None, "hold", (6, 7), k_tiles=4, k_base=4, g0=g0))
        pl.add("mixbranch", n=n, ya=ua, yb=ub_, final=n == 1)
    v = scr_version()
    g0 = turn("scr", ("scr_ready", v), 0.5, None)
    y = [now(proj(W["w_out"], n * BANK, BANK, None, "hold", (n, 2 + n), g0=g0)) for n in range(2)]
    pl.add("modfinal", vec=3, gain=16)
    post("gate", [y[0][0], y[1][0], y[0][1], y[1][1]], gate=0)
    st = stats(("x_ready", n_x[0]))
    pl.add("normalise", st=st)
    v = scr_version()
    g0 = turn("scr", ("scr_ready", v), ("mod", 3), ("mod", 2))

    def up_pair(wv, wg, cv0, cg0):
        def make(c):
            us = []
            for k0 in (0, 4):
                u = pl.unit(4, 2 * FC, [(0, FC, rows(wv, k0, 4, cv0 + c * FC, FC)),
                                        (FC, FC, rows(wg, k0, 4, cg0 + c * FC, FC))])
                us.append((u, k0))
            return us
        return make

    y = ffn(up_pair(W["w_up"], W["w_up"], 0, D_FF), None, True, g0, W["w_down"])
    post("gate", y, gate=1)
    st = stats(("x_ready", n_x[0]))
    pl.add("finalnorm", st=st, row=rows_used[0])
    rows_used[0] += 1
    n_x[0] += 1

    for l in range(2):
        def gain(j):
            return ("gain", 24 + (l * 6 + j) * 8)

        def swiglu(i, j):
            g0 = turn("X", ("x_ready", n_x[0]), gain(j), None)
            st = stats(("x_ready", n_x[0]))
            y = ffn(up_pair(W["ffn_wg"][l, i], W["ffn_wu"][l, i], 0, 0), st, False, g0, W["ffn_wd"][l, i])
            post("norm", y, st=pl.new_stat(TT, 2 * TT), factor=0.5)

        swiglu(0, 0)
        if l == 1:
            pl.add("load_bias", which=1, after=("x_ready", n_x[0]))
            pl.add("load_bias", which=2, after=("x_ready", n_x[0]))
        g0 = turn("X", ("x_ready", n_x[0]), gain(2), None)
        st = stats(("x_ready", n_x[0]))
        if l == 0:
            w = W["even_w_in"][0]

            def ep(i, banks=None):
                n = BANK if i < 6 else EVEN_W - 6 * BANK
                return proj(w, i * BANK, n, i * BANK, "rstd", banks, st, g0=g0)

            u6 = now(ep(6))
            u0 = now(ep(0))
            r6 = rope(pl, 6 * BANK, 9, IDX_DIM, u6, True)
            u1 = now(ep(1))
            r0 = rope(pl, 0, 8, HD, u0)
            pl.add("idxturn", uses=[pl.use(2), pl.use(3)], after=("rope_ready", r6))
            u2, parts = ep(2)
            pl.add("proj", **parts[0])
            r1 = rope(pl, BANK, 8, HD, u1)
            for h in range(4):
                pl.add("idx", h=h, use=pl.use(h % 2))
            turns_of("aq", 0, 0, 2, ("rope_ready", r0))
            pl.add("proj", **parts[1])
            for h in range(4, IDX_HEADS):
                pl.add("idx", h=h, use=pl.use(h % 2))
            turns_of("ak", 1, 4, 2, ("rope_ready", r1))

            held = {}

            def first_of(i):
                def go():
                    held[i], held["parts"] = ep(i, (6, 7))
                    pl.add("proj", **held["parts"][0])
                return go

            def second_of():
                pl.add("proj", **held["parts"][1])

            def rope_of(i, name):
                def go():
                    held[name] = rope(pl, i * BANK, 8, HD, held[i])
                return go

            def fill_turn(i, nm, blk):
                return lambda: turns_of(nm, i, blk, 6, ("rope_ready", held[nm]))

            def topk(j):
                return lambda: pl.add("topk", j=j)

            fills = [[first_of(3), topk(0)], [second_of, topk(1)],
                     [first_of(4), topk(2), rope_of(3, "bq")], [second_of, topk(3)],
                     [fill_turn(3, "bq", 8), first_of(5), topk(4), rope_of(4, "bk")], [second_of, topk(5)],
                     [topk(6), fill_turn(4, "bk", 12)], [topk(7)]]
            n0, o = softmax_heads("diff", fills, "mask", 2 * BANK, 2 * HD, q_ready_of("aq", "ak"), u2, diff=True)
            sd = pl.new_stat(8)
            pl.add("diffout", uses=o, st=sd)
            n0, o = softmax_heads("dsa", [], "sel", 5 * BANK, HD, q_ready_of("bq", "bk"), held[5], base=8)
            v = scr_version()
            o_evac(o, ("scr", BANK), True, n0)
            g0 = turn("scr", ("scr_ready", v), None, None)
            wo = W["even_w_out"][0]
        else:
            w = W["odd_w_in"][0]
            uo = {}

            def op(i, banks=None):
                return proj(w, i * BANK, BANK, i * BANK, "rstd", banks, st, g0=g0)

            uo[0] = now(op(0))
            uo[2] = now(op(2))
            turns_of("oq", 0, 0, 2, ("uses", uo[0]))
            uo[4] = now(op(4))
            turns_of("ok", 2, 4, 2, ("uses", uo[2]))

            def odd_first(i):
                def go():
                    uo[i], uo["parts"] = op(i, (6, 7))
                    pl.add("proj", **uo["parts"][0])
                return go

            def odd_second():
                pl.add("proj", **uo["parts"][1])

            fills = [[odd_first(1)], [odd_second], [odd_first(3)], [odd_second],
                     [odd_first(5)], [odd_second], [lambda: turns_of("pq", 1, 8, 6, ("uses", uo[1]))],
                     [lambda: turns_of("pk", 3, 12, 6, ("uses", uo[3]))]]
            n0, o = softmax_heads("odd", fills, "odd0", 4 * BANK, HD, q_ready_of("oq", "ok"), uo[4])
            o_evac(o, ("pr", 0), False, n0)
            n0, o = softmax_heads("odd", [], "odd1", 5 * BANK, HD, q_ready_of("pq", "pk"), uo[5], base=8)
            v = scr_version()
            o_evac(o, ("pr", BANK), True, n0)
            g0 = turn("pr", ("scr_ready", v), None, None)
            wo = W["odd_w_out"][0]
        y = [now(proj(wo, n * BANK, BANK, None, "hold", (n, 2 + n), g0=g0)) for n in range(2)]
        y = [y[0][0], y[1][0], y[0][1], y[1][1]]
        post("norm", y, st=pl.new_stat(TT, 2 * TT), factor=1.0)
        swiglu(1, 4)
    pl.x_final = 2 * n_x[0]
    return pl


def rope(pl, col, heads, dim, uses, replicate=False):
    n = pl.ropes
    pl.ropes = n + 1
    pl.add("rope", col=col, heads=heads, dim=dim, uses=uses, replicate=replicate, i=n)
    return n + 1


def program(nc, consts, x, c, w_ada, b_ada, g_mix, w_in, w_br_moba, w_br_sb, w_out, rel_bias, g_ffn, w_up,
            w_conv, b_conv, w_down, g_final, norm_g, ffn_wg, ffn_wu, ffn_wd, even_w_in, even_w_out,
            even_lambda, even_subln, odd_w_in, odd_w_out, odd_rel_bias, table, out):
    with ExitStack() as ctx:
        def sb(name, shape, dt=F32):
            return ctx.enter_context(nc.sbuf_tensor(name, shape, dt))

        def sem(name):
            return ctx.enter_context(nc.semaphore(name))

        raw = sb("raw", [P, RAW, UNIT])
        w_hi = sb("w_hi", [P, SPLIT, UNIT], F32R)
        w_lo = sb("w_lo", [P, SPLIT, UNIT], F32R)
        X = sb("X", [P, TT, D])
        hT_hi = sb("hT_hi", [P, KT, S], F32R)
        hT_lo = sb("hT_lo", [P, KT, S], F32R)
        hc_hi = sb("hc_hi", [P, 2, 2 * S], F32R)
        hc_lo = sb("hc_lo", [P, 2, 2 * S], F32R)
        turned = sb("turned", [P, 2, BANK])
        scr = sb("scr", [P, TT, D])
        PR = sb("PR", [P, TT * EVEN_W])
        QK = sb("QK", [P, 16, S])
        IT = sb("IT", [P, 3, S])
        gate_rows = sb("gate_rows", [P, 2, D])
        g_row = sb("g_row", [P, D])
        ada_acc = sb("ada_acc", [P, 2, BANK])
        logit = sb("logit", [P, 4, SC])
        prob = sb("prob", [P, 4, SC])
        probT = sb("probT", [P, 2, SC])
        work = sb("work", [P, SC])
        junk = sb("junk", [P, 2, BANK], BF16)
        lam_in = work[:, 0:4 * HD].rearrange("p (a n) -> p a n", a=4)
        CONSTS = 2 * P + 2 * SC + TT * 2 * HD + TT * 2 * IDX_DIM
        cst = sb("cst", [P, CONSTS])
        ident, later = cst[:, 0:P], cst[:, P:2 * P]
        chunk_mask = cst[:, 2 * P:2 * P + SC]
        minus_past = cst[:, 2 * P + SC:2 * P + 2 * SC]
        r64 = cst[:, 2 * P + 2 * SC:2 * P + 2 * SC + TT * 2 * HD].rearrange("p (t c) -> p t c", t=TT)
        r32 = cst[:, 2 * P + 2 * SC + TT * 2 * HD:CONSTS].rearrange("p (t c) -> p t c", t=TT)
        ones = sb("ones", [P, P])
        NV = 120
        cols = sb("cols", [P, NV])
        ada_b = sb("ada_b", [P, 48])
        conv_c = sb("conv_c", [P, 4 * CONV])
        mod = sb("mod", [P, 4, KT])
        c_act = sb("c_act", [P, KT])
        stat = sb("stat", [P, 340])
        nmax = sb("nmax", [P, 40, 2])
        sums = sb("sums", [P, 40, 2])
        rsum = sb("rsum", [P, 40, 2])
        top = sb("top", [P, 16])
        lam = sb("lam", [P, 4])
        subln = sb("subln", [P, P])
        bucket = sb("bucket", [8, REL_BUCKETS])
        dist = logit[0:8, 0, 0:BIAS_T]
        selbias = sb("selbias", [P, SC])

        psum = ctx.enter_context(nc.psum_tensor("psum", [P, 8, BANK], F32))

        sg = PR[:, 0:1024].rearrange("p (b t n) -> p b t n", b=2, t=TT)
        hid = PR[:, 1024:2048].rearrange("p (b t n) -> p b t n", b=2, t=TT)
        ub = PR[:, 2048:4096].rearrange("p (b t n) -> p b t n", b=2, t=TT)
        cv = PR[:, 4096:5120]
        gg = PR[:, 5120:5632]
        hfull = PR[:, 5632:6144]
        vec_rows = PR[:, 0:4 * P].rearrange("p (v n) -> p v n", v=4)
        pr = PR[:, :].rearrange("p (t n) -> p t n", t=TT)

        weight_loaded = [sem(f"weight_loaded{i}") for i in range(RAW)]
        hi_ready, lo_ready, unit_used = sem("hi_ready"), sem("lo_ready"), sem("unit_used")
        psum_ready = [sem(f"psum_ready{i}") for i in range(8)]
        psum_read = [sem(f"psum_read{i}") for i in range(8)]
        act_step, dve_step, pool_step = sem("act_step"), sem("dve_step"), sem("pool_step")
        consts_loaded, x_loaded, vectors_loaded = sem("consts_loaded"), sem("x_loaded"), sem("vectors_loaded")
        small_loaded, bucket_loaded, gate_bias_loaded = sem("small_loaded"), sem("bucket_loaded"), sem("gate_bias_loaded")
        ada_used = sem("ada_used")
        vectors_turned = sem("vectors_turned")
        c_act_ready = sem("c_act_ready")
        ones_ready = sem("ones_ready")
        mod_final = sem("mod_final")
        turned_ready, split_done = sem("turned_ready"), sem("split_done")
        squares_ready, rstd_ready = sem("squares_ready"), sem("rstd_ready")
        x_ready, scr_ready = sem("x_ready"), sem("scr_ready")
        dist_ready, table_stored, bias_cleared = sem("dist_ready"), sem("table_stored"), sem("bias_cleared")
        bias_loaded = [sem(f"bias_loaded{i}") for i in range(3)]
        logits_ready, probs_ready, mixed_ready = sem("logits_ready"), sem("probs_ready"), sem("mixed_ready")
        log_ready, log_keep_ready = sem("log_ready"), sem("log_keep_ready")
        weight_ready, weight_masked = sem("weight_ready"), sem("weight_masked")
        silu_ready, conv_first, gelu_ready = sem("silu_ready"), sem("conv_first"), sem("gelu_ready")
        rope_swapped, rope_ready = sem("rope_swapped"), sem("rope_ready")
        score_ready, selected = sem("score_ready"), sem("selected")
        lam_dots, lam_exp, lam_ready = sem("lam_dots"), sem("lam_exp"), sem("lam_ready")
        g_row_loaded, g_row_used = sem("g_row_loaded"), sem("g_row_used")
        stored = sem("stored")

        plan = build_plan(dict(w_ada=w_ada[0], w_in=w_in[0], w_br_moba=w_br_moba[0], w_br_sb=w_br_sb[0], w_out=w_out[0],
                               w_up=w_up[0], w_down=w_down[0], ffn_wg=ffn_wg, ffn_wu=ffn_wu, ffn_wd=ffn_wd,
                               even_w_in=even_w_in, even_w_out=even_w_out, odd_w_in=odd_w_in, odd_w_out=odd_w_out))
        steps, units, ada_units = plan.steps, plan.units, plan.ada_units
        loads = plan.load_order()
        raw_slot, landed, loaded = {}, {}, [0] * RAW
        for i, what in enumerate(loads):
            raw_slot[what] = i % RAW
            loaded[i % RAW] += 16 * len((units if what[0] == "w" else ada_units)[what[1]][2])
            landed[what] = loaded[i % RAW]
        named = dict(x_loaded=x_loaded, x_ready=x_ready, scr_ready=scr_ready, split_done=split_done,
                     rope_ready=rope_ready, turned_ready=turned_ready)
        bufs = dict(X=X, scr=scr, pr=pr)

        def wait_ready(eng, use):
            if use.unit is not None:
                eng.wait_ge(unit_used, use.unit + 1)
            else:
                eng.wait_ge(psum_ready[use.bank], use.ready)

        def wait_read(eng, use):
            name, value = use.read_by
            eng.wait_ge(psum_read[use.bank] if name == "psum_read" else named[name], value)

        def wait_free(eng, use):
            if use.prev is not None:
                wait_read(eng, use.prev)

        def col(st, part, i):
            return stat[:, st[part][0] + i:st[part][0] + i + 1]

        def unit_view(tile, slot, u):
            nk, w, _ = units[u]
            return tile[:, slot, 0:nk * w]

        rel_bias_rows = dict(moba=lambda h: scr[:, :, :].rearrange("p t (g n) -> p (t g) n", n=S)[:, h, :],
                             odd0=lambda h: gate_rows[:, :, :].rearrange("p t (g n) -> p (t g) n", n=S)[:, h, :],
                             odd1=lambda h: scr[:, :, :].rearrange("p t (g n) -> p (t g) n", n=S)[:, h, :])

        block = ctx.enter_context(nc.Block())

        @block.sync
        def _(sp):
            for i, what in enumerate(loads):
                if i >= RAW:
                    before, number = loads[i - RAW]
                    if before == "w":
                        sp.wait_ge(hi_ready, number + 1)
                        sp.wait_ge(lo_ready, number + 1)
                    else:
                        sp.wait_ge(ada_used, number + 1)
                nk, w, parts = (units if what[0] == "w" else ada_units)[what[1]]
                view = raw[:, i % RAW, 0:nk * w].rearrange("p (k n) -> p k n", k=nk)
                for c0, n, src in parts:
                    sp.dma_start(view[:, :, c0:c0 + n], src).then_inc(weight_loaded[i % RAW], 16)
            sp.wait_ge(x_ready, plan.x_final)
            sp.dma_start(out[0].rearrange("(t p) d -> p t d", p=P), X[:, :, :]).then_inc(stored, 16)
            sp.wait_ge(stored, 16)

        @block.gpsimd
        def _(pool):
            n = [0]

            def mark(ins):
                ins.then_inc(pool_step, 1)
                n[0] += 1
                return n[0]

            def link(ins):
                pool.wait_ge(pool_step, mark(ins))

            nc.gpsimd.memset(ones[:, :], 1.0).then_inc(ones_ready, 1)
            link(nc.gpsimd.memset(dist, NEG))
            pool.wait_ge(bucket_loaded, 16)
            bounds = t5_bounds()
            for b in range(REL_BUCKETS):
                a, e = P - 1 + bounds[b], P - 1 + bounds[b + 1]
                ins = nc.gpsimd.tensor_copy(dist[:, a:e], bucket[:, b:b + 1].to_broadcast([8, e - a]))
            ins.then_inc(dist_ready, 1)
            pool.wait_ge(dist_ready, 1)
            pool.dma_start(table, dist).then_inc(table_stored, 16)
            gain_rows = [g_final.rearrange("(o d) -> o d", o=1)]
            for l in range(2):
                for j in (1, 3, 5):
                    gain_rows.append(norm_g[l, j:j + 1, :])

            def load_gain(i):
                if i:
                    pool.wait_ge(g_row_used, i)
                pool.dma_start(g_row[:, :], gain_rows[i].to_broadcast([P, D])).then_inc(g_row_loaded, 16)

            load_gain(0)
            for kind, a in steps:
                if kind == "load_bias":
                    which = a["which"]
                    pool.wait_ge(named[a["after"][0]], a["after"][1])
                    if which == 0:
                        pool.wait_ge(table_stored, 16)
                        src = bass.AP(table.tensor, table.offset, [[1, P], [BIAS_T, 8], [1, S]])
                        pool.dma_start(scr[:, :, :].rearrange("p t (g n) -> p (t g) n", n=S), src)\
                            .then_inc(bias_loaded[0], 16)
                    else:
                        buf = (gate_rows, scr)[which - 1][:, :, :].rearrange("p t (g n) -> p (t g) n", n=S)
                        h0 = 8 * (which - 1)
                        table_w = odd_rel_bias.shape[2]
                        base = odd_rel_bias.offset + h0 * table_w
                        nc.gpsimd.memset(buf[0:CHUNK, :, 0:CHUNK], NEG).then_inc(bias_cleared, 1)
                        lo = bass.AP(odd_rel_bias.tensor, base, [[1, CHUNK], [table_w, 8], [1, S - CHUNK]])
                        hi = bass.AP(odd_rel_bias.tensor, base, [[1, CHUNK], [table_w, 8], [1, S]])
                        pool.dma_start(buf[0:CHUNK, :, CHUNK:S], lo).then_inc(bias_loaded[which], 16)
                        pool.dma_start(buf[CHUNK:P, :, :], hi).then_inc(bias_loaded[which], 16)
                elif kind == "rope":
                    c0, nh, dim, tab = a["col"], a["heads"], a["dim"], (r64 if a["dim"] == HD else r32)
                    w = nh * dim
                    for use in a["uses"]:
                        wait_read(pool, use)
                    if a["i"]:
                        pool.wait_ge(rope_ready, a["i"])
                    pool.wait_ge(consts_loaded, 16)
                    for t in range(TT):
                        sw = pr[:, t, c0:c0 + w].rearrange("p (h s d) -> p h s d", h=nh, s=2)[:, :, ::-1, :]
                        sn = tab[:, t, dim:2 * dim].rearrange("p (s d) -> p s d", s=2)[:, None, :, :]\
                            .to_broadcast([P, nh, 2, dim // 2])
                        o = scr[:, t, BANK:BANK + w].rearrange("p (h s d) -> p h s d", h=nh, s=2)
                        ins = nc.gpsimd.tensor_tensor(o, sw, sn, ALU.mult)
                    ins.then_inc(rope_swapped, 1)
                elif kind == "post" and a["mode"] == "norm" or kind == "finalnorm":
                    if a["row"] + 1 < len(gain_rows):
                        load_gain(a["row"] + 1)
                elif kind == "sb_arg":
                    m = a["m"]
                    pool.wait_ge(weight_ready, m + 1)
                    for blk in (0, 2):
                        v = logit[:, m % 4, blk * P:(blk + 1) * P]
                        ins = nc.gpsimd.affine_select(out=v, in_=v, compare_op=ALU.is_gt, fill=0.0, base=0,
                                                      pattern=[[1, P]], channel_multiplier=-1)
                    ins.then_inc(weight_masked, 1)

        @block.scalar
        def _(act):
            n = [0]

            def mark(ins):
                ins.then_inc(act_step, 1)
                n[0] += 1
                return n[0]

            def link(ins):
                act.wait_ge(act_step, mark(ins))

            act.dma_start(PR[0:8, 0:P], c.rearrange("o (k n) -> (o k) n", n=P)).then_inc(vectors_loaded, 16)
            act.dma_start(PR[8:16, 0:P], g_mix.rearrange("o (k n) -> (o k) n", n=P)).then_inc(vectors_loaded, 16)
            act.dma_start(PR[16:24, 0:P], g_ffn.rearrange("o (k n) -> (o k) n", n=P)).then_inc(vectors_loaded, 16)
            act.dma_start(PR[24:120, 0:P], norm_g.rearrange("l j (k n) -> (l j k) n", n=P)).then_inc(vectors_loaded, 16)
            act.dma_start(PR[0:48, P:2 * P], b_ada.rearrange("o (k n) -> (o k) n", n=P)).then_inc(vectors_loaded, 16)
            act.dma_start(PR[0:88, 2 * P:3 * P], w_conv[0, 0:2].rearrange("j (k n) -> (j k) n", n=P))\
                .then_inc(vectors_loaded, 16)
            act.dma_start(PR[0:44, 3 * P:4 * P], w_conv[0, 2:3].rearrange("j (k n) -> (j k) n", n=P))\
                .then_inc(vectors_loaded, 16)
            act.dma_start(PR[44:88, 3 * P:4 * P], b_conv.rearrange("j (k n) -> (j k) n", n=P))\
                .then_inc(vectors_loaded, 16)
            act.dma_start(cst[:, :], consts).then_inc(consts_loaded, 16)
            act.dma_start(X[:, :, :], x[0].rearrange("(t p) d -> p t d", p=P)).then_inc(x_loaded, 16)
            act.dma_start(bucket[:, :], rel_bias).then_inc(bucket_loaded, 16)
            act.dma_start(gate_rows[:, 0, :], b_ada[0:1, 2 * D:3 * D].to_broadcast([P, D])).then_inc(gate_bias_loaded, 16)
            act.dma_start(gate_rows[:, 1, :], b_ada[0:1, 5 * D:6 * D].to_broadcast([P, D])).then_inc(gate_bias_loaded, 16)
            act.dma_start(lam_in[:, :, :], even_lambda.to_broadcast([P, 4, HD])).then_inc(small_loaded, 16)
            act.dma_start(subln[:, :], even_subln.to_broadcast([P, P])).then_inc(small_loaded, 16)

            def split(s):
                if s >= len(units):
                    return
                what = ("w", s)
                act.wait_ge(weight_loaded[raw_slot[what]], landed[what])
                if s >= SPLIT:
                    act.wait_ge(unit_used, s - SPLIT + 1)
                nc.scalar.activation(unit_view(w_hi, s % SPLIT, s), unit_view(raw, raw_slot[what], s), ACT.Copy)\
                    .then_inc(hi_ready, 1)

            def turned_out(use, ti, scale, bias, kt):
                wait_ready(act, use)
                if ti >= 2:
                    act.wait_ge(split_done, plan.turned_groups[ti - 2] + 1)
                if scale is None:
                    nc.scalar.activation(turned[:, ti % 2, :], psum[:, use.bank, :], ACT.Copy).then_inc(turned_ready, 1)
                    return
                if scale == 0.5:
                    nc.scalar.activation(turned[:, ti % 2, :], psum[:, use.bank, :], ACT.Copy, scale=0.5)\
                        .then_inc(turned_ready, 1)
                    return
                if scale[0] == "mod":
                    act.wait_ge(mod_final, 1 if scale[1] == 1 else 2)
                for i in range(2):
                    dst, src = turned[:, ti % 2, i * S:(i + 1) * S], psum[:, use.bank, i * S:(i + 1) * S]
                    k = kt + i
                    if scale[0] == "mod":
                        ins = nc.scalar.activation(dst, src, ACT.Identity, scale=mod[:, scale[1], k:k + 1],
                                                   bias=mod[:, bias[1], k:k + 1])
                    else:
                        ins = nc.scalar.activation(dst, src, ACT.Copy, scale=cols[:, scale[1] + k:scale[1] + k + 1])
                ins.then_inc(turned_ready, 1)

            for kind, a in steps:
                if kind == "vectors":
                    act.wait_ge(vectors_turned, 1)
                    nc.scalar.activation(c_act[:, :], cols[:, 0:KT], ACT.Silu).then_inc(c_act_ready, 1)
                    act.wait_ge(lam_dots, 1)
                    nc.scalar.activation(lam[:, 0:2], lam[:, 0:2], ACT.Exp).then_inc(lam_exp, 1)
                elif kind == "prime":
                    for s in range(LOOK):
                        split(s)
                elif kind == "stats":
                    st = a["st"]
                    act.wait_ge(named[a["after"][0]], a["after"][1])
                    for t in range(TT):
                        if st["squares"] + t:
                            act.wait_ge(squares_ready, st["squares"] + t)
                        nc.scalar.activation(junk[:, :, :].rearrange("p b n -> p (b n)"), X[:, t, :], ACT.Square,
                                             accum_out=col(st, "ss", t)).then_inc(squares_ready, 1)
                elif kind == "post":
                    if a["mode"] == "norm":
                        st = a["st"]
                        for j in range(2 * TT):
                            half, t = j // TT, j % TT
                            use = a["uses"][2 * t + half]
                            wait_ready(act, use)
                            act.wait_ge(squares_ready, st["squares"] + max(j - 1, 0))
                            nc.scalar.activation(junk[:, j % 2, :], psum[:, use.bank, :], ACT.Square,
                                                 accum_out=col(st, ("ss", "ss2")[half], t)).then_inc(squares_ready, 1)
                elif kind == "diffout":
                    for t in range(TT):
                        use = a["uses"][t]
                        wait_ready(act, use)
                        nc.scalar.activation(scr[:, t, BANK:D], psum[:, use.bank, :], ACT.Square)
                        nc.scalar.activation(scr[:, t, 0:BANK], psum[:, use.bank, :], ACT.Copy)\
                            .then_inc(psum_read[use.bank], 1)
                elif kind == "turn":
                    turned_out(a["use"], a["ti"], a["scale"], a["bias"], a["kt"])
                elif kind == "proj":
                    split(a["unit"] + LOOK)
                    if a["mode"] == "hold" or not a["last"]:
                        continue
                    for t in range(TT):
                        use = a["uses"][t]
                        wait_ready(act, use)
                        dst, src = pr[:, t, a["dst"]:a["dst"] + a["n"]], psum[:, use.bank, 0:a["n"]]
                        if a["mode"] == "rstd":
                            act.wait_ge(rstd_ready, a["stat"]["i"] + 1)
                            ins = nc.scalar.activation(dst, src, ACT.Copy, scale=col(a["stat"], "r", t))
                        else:
                            ins = nc.scalar.activation(dst, src, ACT.Tanh if a["mode"] == "tanh" else ACT.Copy,
                                                       scale=0.5 if a["mode"] == "tanh" else 1.0)
                        ins.then_inc(psum_read[use.bank], 1)
                elif kind == "headturn":
                    wait_ready(act, a["use"])
                    nc.scalar.activation(QK[:, a["block"]:a["block"] + 2, :].rearrange("p b n -> p (b n)"),
                                         psum[:, a["use"].bank, :], ACT.Copy).then_inc(psum_read[a["use"].bank], 1)
                elif kind == "idxturn":
                    for use, dst, w in ((a["uses"][0], IT[:, 0:2, :].rearrange("p b n -> p (b n)"), 2 * S),
                                        (a["uses"][1], IT[:, 2, :], S)):
                        wait_ready(act, use)
                        nc.scalar.activation(dst, psum[:, use.bank, 0:w], ACT.Copy).then_inc(psum_read[use.bank], 1)
                elif kind == "idx":
                    h, use = a["h"], a["use"]
                    wait_ready(act, use)
                    if h >= 2:
                        act.wait_ge(score_ready, h - 1)
                    nc.scalar.activation(logit[:, h % 2, :], psum[:, use.bank, 0:SC], ACT.Relu,
                                         scale=IDX_HEADS ** -0.5 * IDX_DIM ** -0.5).then_inc(psum_read[use.bank], 1)
                elif kind == "exp":
                    n_ = a["n"]
                    act.wait_ge(logits_ready, n_ + 1)
                    for t, (b, e) in enumerate(((0, P), (P, SC))):
                        ins = nc.scalar.activation(prob[:, n_ % 4, b:e], logit[:, n_ % 2, b:e], ACT.Exp,
                                                   bias=nmax[:, n_, t:t + 1], accum_out=sums[:, n_, t:t + 1])
                    ins.then_inc(probs_ready, 1)
                elif kind == "probturn":
                    wait_ready(act, a["use"])
                    nc.scalar.activation(probT[:, a["k"] % 2, :], psum[:, a["use"].bank, 0:SC], ACT.Copy)\
                        .then_inc(psum_read[a["use"].bank], 1)
                elif kind == "sb_z":
                    m = a["m"]
                    wait_read(act, a["use"])
                    l = prob[:, m % 4, :]
                    link(nc.scalar.activation(l, logit[:, m % 4, :], ACT.Abs))
                    link(nc.scalar.activation(l, l, ACT.Exp, scale=-1.0))
                    nc.scalar.activation(l, l, ACT.Ln, bias=1.0).then_inc(log_ready, 1)
                elif kind == "sb_arg":
                    m = a["m"]
                    wait_read(act, a["use"])
                    nc.scalar.activation(logit[:, m % 4, :], logit[:, m % 4, :], ACT.Exp).then_inc(weight_ready, 1)
                elif kind == "up":
                    split(a["unit"] + LOOK)
                    c_ = a["c"]
                    for t in range(TT if a["last"] else 0):
                        use = a["uses"][t]
                        wait_ready(act, use)
                        if a["conv"]:
                            nc.scalar.activation(ub[:, c_ % 2, t, :], psum[:, use.bank, :], ACT.Copy)\
                                .then_inc(psum_read[use.bank], 1)
                        else:
                            if c_ == 0:
                                act.wait_ge(rstd_ready, a["stat"]["i"] + 1)
                            nc.scalar.activation(sg[:, c_ % 2, t, :], psum[:, use.bank, 0:FC], ACT.Silu,
                                                 scale=col(a["stat"], "r", t)).then_inc(silu_ready, 1)
                elif kind == "down":
                    split(a["unit"] + LOOK)
                elif kind == "hturn":
                    if not a["conv"]:
                        turned_out(a["uses"][0], a["ti"], None, None, None)
                        continue
                    for half in (1, 0):
                        use = a["uses"][half]
                        wait_ready(act, use)
                        for i in range(2):
                            f = 2 * half + i
                            tile = half * (CONV // 2) + 2 * a["c"] + i
                            nc.scalar.activation(cv[:, f * S:(f + 1) * S], psum[:, use.bank, i * S:(i + 1) * S],
                                                 ACT.Identity, scale=conv_c[:, 2 * CONV + tile:2 * CONV + tile + 1],
                                                 bias=conv_c[:, 3 * CONV + tile:3 * CONV + tile + 1])\
                                .then_inc(conv_first, 1)
                    wait_read(act, a["uses"][1])
                    nc.scalar.activation(gg, cv[:, 2 * S:4 * S], ACT.Gelu_apprx_tanh).then_inc(gelu_ready, 1)

        @block.vector
        def _(dve):
            n = [0]

            def mark(ins):
                ins.then_inc(dve_step, 1)
                n[0] += 1
                return n[0]

            def link(ins):
                dve.wait_ge(dve_step, mark(ins))

            def split(s):
                if s >= len(units):
                    return
                dve.wait_ge(hi_ready, s + 1)
                nc.vector.tensor_tensor(unit_view(w_lo, s % SPLIT, s), unit_view(raw, raw_slot["w", s], s),
                                        unit_view(w_hi, s % SPLIT, s).bitcast(F32), ALU.subtract).then_inc(lo_ready, 1)

            def split_group(dst_hi, dst_lo, src):
                link(nc.vector.tensor_copy(dst_hi, src))
                nc.vector.tensor_tensor(dst_lo, src, dst_hi.bitcast(F32), ALU.subtract).then_inc(split_done, 1)

            def rms(st, size, factor=1.0):
                ss, v, t, r = (stat[:, st[k][0]:st[k][1]] for k in ("ss", "v", "t", "r"))
                link(nc.vector.tensor_scalar(v, ss, 1.0 / (size * factor * factor), EPS / (factor * factor), ALU.mult,
                                             ALU.add))
                link(nc.vector.tensor_scalar(t.bitcast(I32), v.bitcast(I32), 1, None, ALU.logical_shift_right))
                link(nc.vector.tensor_scalar(r.bitcast(I32), t.bitcast(I32), -1.0, float(0x5F3759DF), ALU.mult, ALU.add))
                for i in range(3):
                    link(nc.vector.tensor_tensor(t, r, r, ALU.mult))
                    link(nc.vector.scalar_tensor_tensor(t, t, -0.5, v, ALU.mult, ALU.mult))
                    ins = nc.vector.scalar_tensor_tensor(r, t, 1.5, r, ALU.add, ALU.mult)
                    if i < 2:
                        link(ins)
                ins.then_inc(rstd_ready, 1)
                dve.wait_ge(rstd_ready, st["i"] + 1)

            x_v = [0]
            for kind, a in steps:
                if kind == "vectors":
                    for use, dst, w in ((a["uses"][0], cols[:, :], NV), (a["uses"][1], ada_b[:, :], 48),
                                        (a["uses"][2], conv_c[:, 0:88], 88), (a["uses"][3], conv_c[:, 88:176], 88)):
                        wait_ready(dve, use)
                        ins = nc.vector.tensor_copy(dst, psum[:, use.bank, 0:w])
                        ins.then_inc(psum_read[use.bank], 1)
                    for use in a["uses"]:
                        wait_read(dve, use)
                    nc.vector.memset(top[:, :], 0.0).then_inc(vectors_turned, 1)
                    dve.wait_ge(c_act_ready, 1)
                    dve.wait_ge(small_loaded, 32)
                    link(nc.vector.tensor_tensor(work[:, 0:2 * HD].rearrange("p (a n) -> p a n", a=2),
                                                 lam_in[:, 0::2, :], lam_in[:, 1::2, :], ALU.mult))
                    nc.vector.tensor_reduce(lam[:, 0:2], work[:, 0:2 * HD].rearrange("p (a n) -> p a n", a=2), AX.X,
                                            ALU.add).then_inc(lam_dots, 1)
                elif kind == "prime":
                    for s in range(LOOK):
                        split(s)
                elif kind == "ada":
                    what = ("a", a["unit"])
                    acc = ada_acc[:, a["n"] % 2, :]
                    dve.wait_ge(weight_loaded[raw_slot[what]], landed[what])
                    if a["part"] == 0 and a["slot_free"] is not None:
                        wait_ready(dve, a["slot_free"])
                    for k in range(4):
                        kk = 4 * a["part"] + k
                        w = raw[:, raw_slot[what], k * BANK:(k + 1) * BANK]
                        if kk == 0:
                            ins = nc.vector.tensor_scalar(acc, w, c_act[:, 0:1], None, ALU.mult)
                        else:
                            ins = nc.vector.scalar_tensor_tensor(acc, w, c_act[:, kk:kk + 1], acc, ALU.mult, ALU.add)
                        if k < 3:
                            link(ins)
                    ins.then_inc(ada_used, 1)
                    dve.wait_ge(ada_used, a["unit"] + 1)
                elif kind == "adasum":
                    use, half = a["use"], a["n"] % 2
                    wait_ready(dve, use)
                    if a["gate"] is not None:
                        dst = gate_rows[:, a["gate"], half * BANK:(half + 1) * BANK]
                        dve.wait_ge(gate_bias_loaded, 32)
                        nc.vector.tensor_tensor(dst, psum[:, use.bank, :], dst, ALU.add).then_inc(psum_read[use.bank], 1)
                    else:
                        nc.vector.tensor_tensor(mod[:, a["vec"], 4 * half:4 * half + 4], psum[:, use.bank, 0:4],
                                                ada_b[:, 4 * a["n"]:4 * a["n"] + 4], ALU.add)\
                            .then_inc(psum_read[use.bank], 1)
                    wait_read(dve, use)
                elif kind == "modfinal":
                    nc.vector.scalar_tensor_tensor(mod[:, a["vec"], :], mod[:, a["vec"], :], 1.0,
                                                   cols[:, a["gain"]:a["gain"] + KT], ALU.add, ALU.mult)\
                        .then_inc(mod_final, 1)
                elif kind == "stats":
                    dve.wait_ge(squares_ready, a["st"]["squares"] + TT)
                    rms(a["st"], D)
                elif kind == "normalise":
                    for t in range(TT):
                        ins = nc.vector.tensor_scalar(scr[:, t, :], X[:, t, :], col(a["st"], "r", t), None, ALU.mult)
                        if t == 0:
                            link(ins)
                    ins.then_inc(scr_ready, 1)
                elif kind == "turn":
                    if a["read_before"] is not None:
                        dve.wait_ge(unit_used, a["read_before"] + 1)
                    dve.wait_ge(turned_ready, a["ti"] + 1)
                    k = a["kt"]
                    split_group(hT_hi[:, k:k + 2, :].rearrange("p k n -> p (k n)"),
                                hT_lo[:, k:k + 2, :].rearrange("p k n -> p (k n)"), turned[:, a["ti"] % 2, :])
                elif kind in ("proj", "down"):
                    split(a["unit"] + LOOK)
                elif kind == "rope":
                    c0, nh, dim, tab = a["col"], a["heads"], a["dim"], (r64 if a["dim"] == HD else r32)
                    w = nh * dim
                    for use in a["uses"]:
                        wait_read(dve, use)
                    dve.wait_ge(consts_loaded, 16)
                    if a["i"]:
                        dve.wait_ge(rope_ready, a["i"])
                    for t in range(TT):
                        xs = pr[:, t, c0:c0 + w].rearrange("p (h d) -> p h d", h=nh)
                        cs = tab[:, t, 0:dim][:, None, :].to_broadcast([P, nh, dim])
                        link(nc.vector.tensor_tensor(scr[:, t, 0:w].rearrange("p (h d) -> p h d", h=nh), xs, cs, ALU.mult))
                    dve.wait_ge(rope_swapped, a["i"] + 1)
                    ins = nc.vector.tensor_tensor(pr[:, :, c0:c0 + w], scr[:, :, 0:w], scr[:, :, BANK:BANK + w], ALU.add)
                    if a["replicate"]:
                        link(ins)
                        key = pr[:, :, c0 + 256:c0 + 288][:, :, None, :].to_broadcast([P, TT, 4, IDX_DIM])
                        ins = nc.vector.tensor_copy(work[:, 0:TT * P].rearrange("p (t r d) -> p t r d", t=TT, r=4), key)
                    ins.then_inc(rope_ready, 1)
                elif kind == "idx":
                    h, use = a["h"], a["use"]
                    wait_read(dve, use)
                    for t, (b, e) in enumerate(((0, P), (P, SC))):
                        wcol = pr[:, t, 6 * BANK + 288 + h:6 * BANK + 289 + h]
                        before = chunk_mask if h == 0 else selbias
                        ins = nc.vector.scalar_tensor_tensor(selbias[:, b:e], logit[:, h % 2, b:e], wcol, before[:, b:e],
                                                             ALU.mult, ALU.add)
                        if t == 0:
                            link(ins)
                    ins.then_inc(score_ready, 1)
                    dve.wait_ge(score_ready, h + 1)
                elif kind == "topk":
                    if a["j"] == 0:
                        link(nc.vector.tensor_copy(work[:, :], selbias[:, :]))
                    tiles = ((0, P), (P, SC))
                    for t, (b, e) in enumerate(tiles):
                        m = mark(nc.vector.max(top[:, 8 * t:8 * t + 8], work[:, b:e]))
                    dve.wait_ge(dve_step, m)
                    for t, (b, e) in enumerate(tiles):
                        m = mark(nc.vector.match_replace(work[:, b:e], top[:, 8 * t:8 * t + 8], work[:, b:e], NEG))
                    dve.wait_ge(dve_step, m)
                    if a["j"] == TOPK // 8 - 1:
                        link(nc.vector.tensor_scalar(work[:, :], work[:, :], NEG, -NEG, ALU.is_equal, ALU.mult))
                        nc.vector.scalar_tensor_tensor(selbias[:, :], work[:, :], NEG, chunk_mask, ALU.add, ALU.add)\
                            .then_inc(selected, 1)
                        dve.wait_ge(selected, 1)
                elif kind == "qk":
                    n_, h, use, bias = a["n"], a["h"], a["use"], a["bias"]
                    wait_ready(dve, use)
                    s_, lg = psum[:, use.bank, 0:SC], logit[:, n_ % 2, :]
                    if bias in rel_bias_rows:
                        if h == 0:
                            which = ("moba", "odd0", "odd1").index(bias)
                            dve.wait_ge(bias_loaded[which], 16 if which == 0 else 32)
                            if which:
                                dve.wait_ge(bias_cleared, which)
                        rows = rel_bias_rows[bias](h)
                        mark(nc.vector.scalar_tensor_tensor(lg[:, 0:P], s_[:, 0:P], SCALE, rows[:, P - 1::-1],
                                                            ALU.mult, ALU.add))
                        nc.vector.scalar_tensor_tensor(lg[:, P:SC], s_[:, P:SC], SCALE, rows[:, S - 1::-1],
                                                       ALU.mult, ALU.add).then_inc(psum_read[use.bank], 1)
                    else:
                        nc.vector.scalar_tensor_tensor(lg, s_, SCALE, chunk_mask if bias == "mask" else selbias[:, :],
                                                       ALU.mult, ALU.add).then_inc(psum_read[use.bank], 1)
                    wait_read(dve, use)
                    mark(nc.vector.tensor_reduce(nmax[:, n_, 0:1], lg[:, 0:P], AX.X, ALU.max, negate=True))
                    nc.vector.tensor_reduce(nmax[:, n_, 1:2], lg[:, P:SC], AX.X, ALU.max, negate=True)\
                        .then_inc(logits_ready, 1)
                elif kind == "mix":
                    n_ = a["n"]
                    dve.wait_ge(probs_ready, n_ + 1)
                    if n_ == 9:
                        dve.wait_ge(lam_exp, 1)
                        link(nc.vector.tensor_scalar(lam[:, 2:3], lam[:, 1:2], lam[:, 0:1], -LAMBDA_INIT, ALU.subtract,
                                                     ALU.add))
                    link(nc.vector.reciprocal(rsum[:, n_ - 1:n_ + 1, :], sums[:, n_ - 1:n_ + 1, :]))
                    link(nc.vector.tensor_scalar(rsum[:, n_, :], rsum[:, n_, :], lam[:, 2:3], None, ALU.mult))
                    for t, (b, e) in enumerate(((0, P), (P, SC))):
                        m = mark(nc.vector.tensor_scalar(prob[:, n_ % 4, b:e], prob[:, n_ % 4, b:e], rsum[:, n_, t:t + 1],
                                                         None, ALU.mult))
                    dve.wait_ge(dve_step, m)
                    for t, (b, e) in enumerate(((0, P), (P, SC))):
                        ins = nc.vector.scalar_tensor_tensor(prob[:, (n_ - 1) % 4, b:e], prob[:, (n_ - 1) % 4, b:e],
                                                             rsum[:, n_ - 1, t:t + 1], prob[:, n_ % 4, b:e],
                                                             ALU.mult, ALU.add)
                        if t == 0:
                            mark(ins)
                    ins.then_inc(mixed_ready, 1)
                elif kind == "oevac":
                    buf, c0 = bufs[a["dst"][0]], a["dst"][1]
                    if a["mode"] == "norm":
                        n0 = a["n0"]
                        dve.wait_ge(probs_ready, n0 + 8)
                        link(nc.vector.reciprocal(rsum[:, n0:n0 + 8, :], sums[:, n0:n0 + 8, :]))
                    for t in range(TT):
                        use = a["uses"][t]
                        wait_ready(dve, use)
                        if a["mode"] == "norm":
                            ins = nc.vector.tensor_tensor(
                                buf[:, t, c0:c0 + BANK].rearrange("p (h d) -> p h d", d=HD),
                                psum[:, use.bank, :].rearrange("p (h d) -> p h d", d=HD),
                                rsum[:, n0:n0 + 8, t:t + 1].to_broadcast([P, 8, HD]), ALU.mult)
                        else:
                            ins = nc.vector.tensor_copy(buf[:, t, c0:c0 + BANK], psum[:, use.bank, :])
                        if a["final"] and t == 1:
                            ins.then_inc(scr_ready, 1)
                        else:
                            ins.then_inc(psum_read[use.bank], 1)
                            wait_read(dve, use)
                elif kind == "diffout":
                    st = a["st"]
                    for t in range(TT):
                        wait_read(dve, a["uses"][t])
                        s0 = st["ss"][0] + 4 * t
                        m = mark(nc.vector.tensor_reduce(stat[:, s0:s0 + 4],
                                                         scr[:, t, BANK:D].rearrange("p (h d) -> p h d", h=4), AX.X,
                                                         ALU.add))
                    dve.wait_ge(dve_step, m)
                    rms(st, 2 * HD)
                    for t in range(TT):
                        o = scr[:, t, 0:BANK].rearrange("p (h d) -> p h d", h=4)
                        r0 = st["r"][0] + 4 * t
                        link(nc.vector.tensor_tensor(o, o, stat[:, r0:r0 + 4][:, :, None].to_broadcast([P, 4, P]),
                                                     ALU.mult))
                        link(nc.vector.scalar_tensor_tensor(o, o, 1.0 - LAMBDA_INIT,
                                                            subln[:, None, :].to_broadcast([P, 4, P]), ALU.mult, ALU.mult))
                elif kind == "sb_z":
                    use = a["use"]
                    wait_ready(dve, use)
                    nc.vector.tensor_scalar(logit[:, a["m"] % 4, :], psum[:, use.bank, 0:SC], SCALE, None, ALU.mult)\
                        .then_inc(psum_read[use.bank], 1)
                elif kind == "sb_keep":
                    m_ = a["m"]
                    z, l = logit[:, m_ % 4, :], prob[:, m_ % 4, :]
                    dve.wait_ge(log_ready, m_ + 1)
                    dve.wait_ge(consts_loaded, 16)
                    link(nc.vector.scalar_tensor_tensor(l, z, 0.0, l, ALU.max, ALU.add))
                    nc.vector.tensor_tensor(probT[:, m_ % 2, :], l, minus_past, ALU.mult).then_inc(log_keep_ready, 1)
                elif kind == "sb_arg":
                    m_, use = a["m"], a["use"]
                    wait_ready(dve, use)
                    nc.vector.tensor_tensor(logit[:, m_ % 4, :], psum[:, use.bank, 0:SC], logit[:, m_ % 4, :], ALU.add)\
                        .then_inc(psum_read[use.bank], 1)
                elif kind == "mixbranch":
                    half = a["n"]
                    for t in range(TT):
                        ya, yb = a["ya"][t], a["yb"][t]
                        dst = scr[:, t, half * BANK:(half + 1) * BANK]
                        tmp = prob[:, :, :].rearrange("p a n -> p (a n)")[:, t * BANK:(t + 1) * BANK]
                        wait_ready(dve, ya)
                        nc.vector.scalar_tensor_tensor(dst, pr[:, t, half * BANK:(half + 1) * BANK], 1.0,
                                                       psum[:, ya.bank, :], ALU.add, ALU.mult)\
                            .then_inc(psum_read[ya.bank], 1)
                        wait_ready(dve, yb)
                        nc.vector.scalar_tensor_tensor(tmp, pr[:, t, (3 + half) * BANK:(4 + half) * BANK], 1.0,
                                                       psum[:, yb.bank, :], ALU.add, ALU.mult)\
                            .then_inc(psum_read[yb.bank], 1)
                        wait_read(dve, ya)
                        wait_read(dve, yb)
                        ins = nc.vector.tensor_tensor(dst, dst, tmp, ALU.add)
                        if a["final"] and t == 1:
                            ins.then_inc(scr_ready, 1)
                        else:
                            link(ins)
                elif kind == "up":
                    split(a["unit"] + LOOK)
                    if not a["conv"] and a["last"]:
                        c_ = a["c"]
                        for t in range(TT):
                            use = a["uses"][t]
                            dve.wait_ge(silu_ready, TT * a["ci"] + t + 1)
                            nc.vector.scalar_tensor_tensor(hid[:, c_ % 2, t, :], psum[:, use.bank, FC:2 * FC],
                                                           col(a["stat"], "r", t), sg[:, c_ % 2, t, :],
                                                           ALU.mult, ALU.mult).then_inc(psum_read[use.bank], 1)
                elif kind == "hturn":
                    if a["down_before"] is not None:
                        dve.wait_ge(unit_used, a["down_before"] + 1)
                    hi, lo = hc_hi[:, a["c"] % 2, :], hc_lo[:, a["c"] % 2, :]
                    if not a["conv"]:
                        dve.wait_ge(turned_ready, a["ti"] + 1)
                        split_group(hi, lo, turned[:, a["ti"] % 2, :])
                        continue
                    done = 0
                    for half in (1, 0):
                        use = a["uses"][half]
                        dve.wait_ge(conv_first, 4 * a["cc"] + (2 if half else 4))
                        for tap, shift in ((1, 1), (0, 2)):
                            for i in range(2):
                                f, tile = 2 * half + i, half * (CONV // 2) + 2 * a["c"] + i
                                v = cv[:, f * S + shift:(f + 1) * S]
                                ins = nc.vector.scalar_tensor_tensor(
                                    v, psum[:, use.bank, i * S:(i + 1) * S - shift],
                                    conv_c[:, tap * CONV + tile:tap * CONV + tile + 1], v, ALU.mult, ALU.add)
                                if tap == 1 or i == 0:
                                    m = mark(ins)
                            if tap == 1:
                                dve.wait_ge(dve_step, m)
                        ins.then_inc(psum_read[use.bank], 1)
                    wait_read(dve, a["uses"][0])
                    dve.wait_ge(dve_step, m)
                    dve.wait_ge(gelu_ready, a["cc"] + 1)
                    link(nc.vector.tensor_tensor(hfull, gg, cv[:, 0:2 * S], ALU.mult))
                    split_group(hi, lo, hfull)
                elif kind == "post":
                    norm = a["mode"] == "norm"
                    if norm:
                        dve.wait_ge(g_row_loaded, 16 * (a["row"] + 1))
                    for j in range(2 * TT):
                        half, t = j // TT, j % TT
                        use = a["uses"][2 * t + half]
                        cs = slice(half * BANK, (half + 1) * BANK)
                        if norm:
                            dve.wait_ge(squares_ready, a["st"]["squares"] + j + 1)
                        else:
                            wait_ready(dve, use)
                        rows = g_row[:, cs] if norm else gate_rows[:, a["gate"], cs]
                        nc.vector.tensor_tensor(scr[:, t, cs], psum[:, use.bank, :], rows, ALU.mult)\
                            .then_inc(psum_read[use.bank], 1)
                    if norm:
                        st = a["st"]
                        ss, ss2 = stat[:, st["ss"][0]:st["ss"][1]], stat[:, st["ss2"][0]:st["ss2"][1]]
                        link(nc.vector.tensor_tensor(ss, ss, ss2, ALU.add))
                        rms(st, D, a["factor"])
                    for use in a["uses"]:
                        wait_read(dve, use)
                    for half in range(2):
                        for t in range(TT):
                            cs = slice(half * BANK, (half + 1) * BANK)
                            f = col(a["st"], "r", t) if norm else 1.0
                            ins = nc.vector.scalar_tensor_tensor(X[:, t, cs], scr[:, t, cs], f, X[:, t, cs], ALU.mult,
                                                                 ALU.add)
                            if t == 0:
                                mark(ins)
                        ins.then_inc(x_ready, 1)
                    x_v[0] += 2
                    dve.wait_ge(dve_step, n[0])
                    dve.wait_ge(x_ready, x_v[0])
                    if norm:
                        nc.vector.memset(top[:, 0:1], 0.0).then_inc(g_row_used, 1)
                elif kind == "finalnorm":
                    dve.wait_ge(g_row_loaded, 16 * (a["row"] + 1))
                    for half in range(2):
                        cs = slice(half * BANK, (half + 1) * BANK)
                        for t in range(TT):
                            ins = nc.vector.scalar_tensor_tensor(X[:, t, cs], X[:, t, cs], col(a["st"], "r", t),
                                                                 g_row[:, cs], ALU.mult, ALU.mult)
                            if t == 0:
                                mark(ins)
                        ins.then_inc(x_ready, 1)
                    x_v[0] += 2
                    dve.wait_ge(dve_step, n[0])
                    dve.wait_ge(x_ready, x_v[0])
                    nc.vector.memset(top[:, 0:1], 0.0).then_inc(g_row_used, 1)

        @block.tensor
        def _(pe):
            split_seen = [0]

            def need_group(g):
                if g + 1 > split_seen[0]:
                    pe.wait_ge(split_done, g + 1)
                    split_seen[0] = g + 1

            def need_unit(u):
                pe.wait_ge(hi_ready, u + 1)
                pe.wait_ge(lo_ready, u + 1)

            def product(o, a_hi, a_lo, b_hi, b_lo, start, stop):
                nc.tensor.matmul(o, a_hi, b_hi, start=start, stop=False)
                nc.tensor.matmul(o, a_hi, b_lo, start=False, stop=False)
                return nc.tensor.matmul(o, a_lo, b_hi, start=False, stop=stop)

            def chunk(a, k_tiles, k_base=0):
                s, k0, outs = a["unit"], a["k0"], a["uses"]
                if k0 == 0:
                    for use in outs:
                        wait_free(pe, use)
                need_unit(s)
                nk, w, _ = units[s]
                for k in range(nk):
                    kk = k_base + k0 + k
                    need_group(a["g0"] + kk // 2)
                    for t in range(TT):
                        sl = slice(t * P, (t + 1) * P)
                        b = slice(k * w, (k + 1) * w)
                        ins = product(psum[:, outs[t].bank, 0:w], hT_hi[:, kk, sl], hT_lo[:, kk, sl],
                                      w_hi[:, s % SPLIT, b], w_lo[:, s % SPLIT, b],
                                      k0 + k == 0, k0 + k == k_tiles - 1)
                ins.then_inc(unit_used, 1)

            for kind, a in steps:
                if kind == "vectors":
                    pe.wait_ge(vectors_loaded, 16 * 8)
                    pe.wait_ge(consts_loaded, 16)
                    for i, (use, w) in enumerate(zip(a["uses"], (NV, 48, 88, 88))):
                        nc.tensor.transpose(psum[:, use.bank, 0:w], PR[0:w, i * P:(i + 1) * P], ident[0:w, 0:w])\
                            .then_inc(psum_ready[use.bank], 1)
                elif kind == "adasum":
                    use = a["use"]
                    acc = ada_acc[:, a["n"] % 2, :]
                    wait_free(pe, use)
                    pe.wait_ge(ada_used, 2 * (a["n"] + 1))
                    pe.wait_ge(ones_ready, 1)
                    if a["gate"] is not None:
                        ins = nc.tensor.matmul(psum[:, use.bank, :], ones[:, :], acc, start=True, stop=True)
                    else:
                        for j in range(4):
                            ins = nc.tensor.matmul(psum[:, use.bank, j:j + 1], acc[:, j * P:(j + 1) * P], ones[:, 0:1],
                                                   start=True, stop=True)
                    ins.then_inc(psum_ready[use.bank], 1)
                elif kind == "turn":
                    use, src = a["use"], bufs[a["src"]]
                    wait_free(pe, use)
                    if a["after"]:
                        pe.wait_ge(named[a["after"][0]], a["after"][1])
                    for i in range(2):
                        for t in range(TT):
                            k = a["kt"] + i
                            ins = nc.tensor.transpose(psum[:, use.bank, i * S + t * P:i * S + (t + 1) * P],
                                                      src[:, t, k * P:(k + 1) * P], ident)
                    ins.then_inc(psum_ready[use.bank], 1)
                elif kind == "proj":
                    chunk(a, a["k_tiles"], a["k_base"])
                elif kind == "headturn":
                    use = a["use"]
                    wait_free(pe, use)
                    if a["after"][0] == "uses":
                        for u in a["after"][1]:
                            wait_read(pe, u)
                    else:
                        pe.wait_ge(rope_ready, a["after"][1])
                    for i in range(2):
                        for t in range(TT):
                            c0 = a["col"] + i * P
                            ins = nc.tensor.transpose(psum[:, use.bank, i * S + t * P:i * S + (t + 1) * P],
                                                      pr[:, t, c0:c0 + P], ident)
                    ins.then_inc(psum_ready[use.bank], 1)
                elif kind == "idxturn":
                    pe.wait_ge(rope_ready, a["after"][1])
                    use = a["uses"][0]
                    wait_free(pe, use)
                    for i in range(2):
                        for t in range(TT):
                            c0 = 6 * BANK + i * P
                            ins = nc.tensor.transpose(psum[:, use.bank, i * S + t * P:i * S + (t + 1) * P],
                                                      pr[:, t, c0:c0 + P], ident)
                    ins.then_inc(psum_ready[use.bank], 1)
                    use = a["uses"][1]
                    wait_free(pe, use)
                    for t in range(TT):
                        ins = nc.tensor.transpose(psum[:, use.bank, t * P:(t + 1) * P], work[:, t * P:(t + 1) * P], ident)
                    ins.then_inc(psum_ready[use.bank], 1)
                    for use in a["uses"]:
                        wait_read(pe, use)
                elif kind == "idx":
                    h, use = a["h"], a["use"]
                    wait_free(pe, use)
                    p0, b = IDX_DIM * (h % 4), h // 4
                    q, k = IT[p0:p0 + IDX_DIM, b, :], IT[p0:p0 + IDX_DIM, 2, :]
                    nc.tensor.matmul(psum[:, use.bank, 0:P], q[:, 0:P], k[:, 0:P], start=True, stop=True)
                    nc.tensor.matmul(psum[:, use.bank, P:SC], q[:, P:S], k[:, 0:S], start=True, stop=True)\
                        .then_inc(psum_ready[use.bank], 1)
                elif kind in ("qk", "sb_z"):
                    use = a["use"]
                    h, base = (a["h"], a["base"]) if kind == "qk" else (a["m"], 8)
                    for u in a["ready"]:
                        wait_read(pe, u)
                    wait_free(pe, use)
                    p0 = HD * (h % 2)
                    q, k = QK[p0:p0 + HD, base + h // 2, :], QK[p0:p0 + HD, base + 4 + h // 2, :]
                    if kind == "qk":
                        nc.tensor.matmul(psum[:, use.bank, 0:P], q[:, 0:P], k[:, 0:P], start=True, stop=True)
                        ins = nc.tensor.matmul(psum[:, use.bank, P:SC], q[:, P:S], k[:, 0:S], start=True, stop=True)
                    else:
                        nc.tensor.matmul(psum[:, use.bank, 0:S], k[:, 0:P], q[:, 0:S], start=True, stop=True)
                        ins = nc.tensor.matmul(psum[:, use.bank, S:SC], k[:, P:S], q[:, P:S], start=True, stop=True)
                    ins.then_inc(psum_ready[use.bank], 1)
                elif kind == "probturn":
                    n_, use = a["n"], a["use"]
                    wait_free(pe, use)
                    if a["diff"]:
                        pe.wait_ge(mixed_ready, (n_ - 7) // 2)
                        src = prob[:, (n_ - 1) % 4, :]
                    else:
                        pe.wait_ge(probs_ready, n_ + 1)
                        src = prob[:, n_ % 4, :]
                    for b in range(3):
                        ins = nc.tensor.transpose(psum[:, use.bank, b * P:(b + 1) * P], src[:, b * P:(b + 1) * P], ident)
                    ins.then_inc(psum_ready[use.bank], 1)
                elif kind in ("pv", "sb_pv"):
                    if kind == "pv":
                        if a["first"]:
                            for u in a["v_ready"]:
                                wait_read(pe, u)
                            for u in a["uses"]:
                                wait_free(pe, u)
                        wait_read(pe, a["turned"])
                        pT, w, o0, last = probT[:, a["k"] % 2, :], a["w"], a["slot"] * a["w"], a["last"]
                    else:
                        m = a["m"]
                        if m == 0:
                            for u in a["v_ready"]:
                                wait_read(pe, u)
                            for u in a["uses"]:
                                wait_free(pe, u)
                        pe.wait_ge(weight_masked, m + 1)
                        pT, w, o0, last = logit[:, m % 4, :], HD, m * HD, m == 7
                    vc = a["v"]
                    b0, b1 = a["uses"][0].bank, a["uses"][1].bank
                    ins = nc.tensor.matmul(psum[:, b0, o0:o0 + w], pT[:, 0:P], pr[:, 0, vc:vc + w], start=True, stop=True)
                    if last:
                        ins.then_inc(psum_ready[b0], 1)
                    nc.tensor.matmul(psum[:, b1, o0:o0 + w], pT[:, P:2 * P], pr[:, 0, vc:vc + w], start=True, stop=False)
                    ins = nc.tensor.matmul(psum[:, b1, o0:o0 + w], pT[:, 2 * P:SC], pr[:, 1, vc:vc + w], start=False,
                                           stop=True)
                    if last:
                        ins.then_inc(psum_ready[b1], 1)
                elif kind == "sb_cum":
                    m, use = a["m"], a["use"]
                    wait_free(pe, use)
                    pe.wait_ge(log_keep_ready, m + 1)
                    pe.wait_ge(ones_ready, 1)
                    lk, o = probT[:, m % 2, :], psum[:, use.bank, :]
                    nc.tensor.matmul(o[:, 0:S], later, lk[:, 0:S], start=True, stop=False)
                    nc.tensor.matmul(o[:, P:S], ones[:, :], lk[:, S:SC], start=False, stop=True)
                    nc.tensor.matmul(o[:, S:SC], later, lk[:, S:SC], start=True, stop=True)\
                        .then_inc(psum_ready[use.bank], 1)
                elif kind == "up":
                    chunk(a, KT)
                elif kind == "hturn":
                    for use in a["uses"]:
                        wait_free(pe, use)
                    for use in a["ups"]:
                        wait_read(pe, use)
                    src = (ub if a["conv"] else hid)[:, a["c"] % 2]
                    for i, use in enumerate(a["uses"]):
                        for f in range(2):
                            for t in range(TT):
                                c0 = (2 * i + f) * P
                                ins = nc.tensor.transpose(psum[:, use.bank, f * S + t * P:f * S + (t + 1) * P],
                                                          src[:, t, c0:c0 + P], ident)
                        ins.then_inc(psum_ready[use.bank], 1)
                elif kind == "down":
                    c_, u = a["c"], a["unit"]
                    need_unit(u)
                    need_group(a["g"])
                    if c_ == 0:
                        for use in a["uses"]:
                            wait_free(pe, use)
                    order = [(k, t, half) for k in range(2) for t in range(TT) for half in range(2)]
                    if c_ == NFC - 1:
                        order = [(k, t, half) for half in range(2) for k in range(2) for t in range(TT)]
                    for k, t, half in order:
                        sl = slice(k * S + t * P, k * S + (t + 1) * P)
                        b = slice(k * D + half * BANK, k * D + (half + 1) * BANK)
                        use = a["uses"][2 * t + half]
                        ins = product(psum[:, use.bank, :], hc_hi[:, c_ % 2, sl], hc_lo[:, c_ % 2, sl],
                                      w_hi[:, u % SPLIT, b], w_lo[:, u % SPLIT, b],
                                      c_ == 0 and k == 0, c_ == NFC - 1 and k == 1)
                        if c_ == NFC - 1 and k == 1 and use.unit is None:
                            ins.then_inc(psum_ready[use.bank], 1)
                    ins.then_inc(unit_used, 1)


_INS = ["x", "c", "w_ada", "b_ada", "g_mix", "w_in", "w_br_moba", "w_br_sb", "w_out", "rel_bias", "g_ffn", "w_up",
        "w_conv", "b_conv", "w_down", "g_final", "norm_g_2", "ffn_wg_2", "ffn_wu_2", "ffn_wd_2", "even_w_in_2",
        "even_w_out_2", "even_lambda_2", "even_subln_2", "odd_w_in_2", "odd_w_out_2", "odd_rel_bias_2"]


def kernel(**inputs):
    import concourse.bacc as bacc
    from concourse.bass_utils import run_bass_kernel_spmd

    nc = bacc.Bacc("TRN2", target_bir_lowering=False, num_devices=1)
    arrays, args = {}, []
    for name, a in [("consts", constants())] + [(name, inputs[name]) for name in _INS]:
        a = np.ascontiguousarray(a)
        arrays[f"in_{name}_dram"] = a
        args.append(nc.dram_tensor(f"in_{name}_dram", a.shape, mybir.dt.from_np(a.dtype), kind="ExternalInput").ap())
    args.append(nc.dram_tensor("distance_table", (8, BIAS_T), F32, kind="Internal").ap())
    args.append(nc.dram_tensor("out_0_dram", (1, S, D), F32, kind="ExternalOutput").ap())
    program(nc, *args)
    r = run_bass_kernel_spmd(nc, [arrays], core_ids=[0])
    return r.results[0]["out_0_dram"]
```

```python
from contextlib import ExitStack

import numpy as np

import concourse.bass as bass
from concourse import mybir

F32 = mybir.dt.float32
F32R = mybir.dt.float32r
BF16 = mybir.dt.bfloat16
I32 = mybir.dt.int32
ACT = mybir.ActivationFunctionType
ALU = mybir.AluOpType
AX = mybir.AxisListType

P = 128
S = 256
TT = S // P
D = 1024
KT = D // P
HD = 64
D_FF = 2816
FC = 256
NFC = D_FF // FC
CONV = 2 * D_FF // P
BANK = 512
UNIT = 2048
RAW, SPLIT = 3, 3
LOOK = SPLIT - 1
EPS = 1e-6
NEG = -1e30
SCALE = HD ** -0.5
REL_BUCKETS = 32
REL_MAX_DIST = 128
CHUNK = 64
IDX_HEADS, IDX_DIM, TOPK = 8, 32, 64
LAMBDA_INIT = 0.2
EVEN_W = 3368
SC = P + S
BIAS_T = S + P - 1


def t5_bounds():
    exact = REL_BUCKETS // 2
    n = np.arange(S)
    large = exact + (np.log(np.maximum(n, exact).astype(np.float32) / exact)
                     / np.log(REL_MAX_DIST / exact) * (REL_BUCKETS - exact)).astype(np.int32)
    b = np.where(n < exact, n, np.minimum(large, REL_BUCKETS - 1))
    return [int(np.argmax(b >= i)) for i in range(REL_BUCKETS)] + [S]


def constants():
    p = np.arange(P)[:, None]
    k = np.arange(P)[None, :]
    ident = np.eye(P, dtype=np.float32)
    later = (p >= k).astype(np.float32)
    q_of = np.concatenate([p + 0 * k, p + P + 0 * k, p + P + 0 * k], 1)
    k_of = np.concatenate([k + 0 * p, k + 0 * p, k + P + 0 * p], 1)
    chunk_mask = np.where(k_of // CHUNK <= q_of // CHUNK, 0.0, NEG).astype(np.float32)
    past = np.concatenate([p < k, p < k + P, p < k], 1)
    minus_past = -past.astype(np.float32)

    def rope(dim):
        inv = (np.float32(10000.0) ** (-np.arange(0, dim, 2, dtype=np.float32) / np.float32(dim))).astype(np.float32)
        ang = (np.arange(S, dtype=np.float32)[:, None] * inv[None, :]).astype(np.float32)
        c, s = np.cos(ang), np.sin(ang)
        both = np.concatenate([c, c, -s, s], 1).astype(np.float32)
        return both.reshape(TT, P, 2 * dim).transpose(1, 0, 2).reshape(P, TT * 2 * dim)

    return np.ascontiguousarray(np.concatenate(
        [ident, later, chunk_mask, minus_past, rope(HD), rope(IDX_DIM)], 1).astype(np.float32))


class Use:

    def __init__(self, bank, prev, unit, ready, evacuated):
        self.bank, self.prev, self.unit, self.ready = bank, prev, unit, ready
        self.read_by = ("psum_read", evacuated)


class Plan:

    def __init__(self):
        self.steps, self.units, self.ada_units = [], [], []
        self.ada_done = []
        self.tenant, self.announced, self.evacuated = [None] * 8, [0] * 8, [0] * 8
        self.ropes = 0
        self.turned, self.turned_groups, self.squares = 0, [], 0
        self.splits = 0
        self.stats = 0
        self.stat_cols = 0

    def add(self, kind, **kw):
        self.steps.append((kind, kw))

    def unit(self, nk, w, parts):
        self.units.append((nk, w, parts))
        return len(self.units) - 1

    def use(self, bank, unit=None, read_by=None, by_unit=False):
        if unit is None and not by_unit:
            self.announced[bank] += 1
        if read_by is None:
            self.evacuated[bank] += 1
        use = Use(bank, self.tenant[bank], unit, self.announced[bank], self.evacuated[bank])
        if read_by is not None:
            use.read_by = read_by
        self.tenant[bank] = use
        return use

    def turned_use(self, bank):
        self.turned += 1
        return self.use(bank, read_by=("turned_ready", self.turned))

    def turn(self):
        self.splits += 1
        return self.splits - 1

    def new_stat(self, width, squares=0):
        c, i = self.stat_cols, self.stats
        self.stat_cols += 5 * width
        self.stats += 1
        self.squares += squares
        return dict(i=i, w=width, ss=(c, c + width), ss2=(c + width, c + 2 * width), v=(c + 2 * width, c + 3 * width),
                    t=(c + 3 * width, c + 4 * width), r=(c + 4 * width, c + 5 * width), squares=self.squares - squares)

    def load_order(self):
        order = []
        for kind, a in self.steps:
            if kind == "prime":
                order += [("w", s) for s in a["units"]]
            elif kind == "ada":
                order.append(("a", a["unit"]))
            elif kind in ("proj", "up") or kind == "down" and a["part"][0] == 0:
                order += [("w", a["unit"] + LOOK)] if a["unit"] + LOOK < len(self.units) else []
        return order


def build_plan(W):
    pl = Plan()
    n_attn, n_turned_heads, n_x, n_scr = [0], [0], [0], [0]
    last_hT_unit = [None]

    def rows(w, k0, nk, c0, n):
        return w[k0 * P:(k0 + nk) * P, c0:c0 + n].rearrange("(k p) n -> p k n", p=P)

    def column_units(w, k_tiles, c0, n):
        made = []
        for k0 in range(0, k_tiles, 4):
            u = pl.unit(4, n, [(0, n, rows(w, k0, 4, c0, n))])
            made.append((u, k0))
        return made

    free_pair = [0]

    def pair():
        free_pair[0] ^= 1
        return (4, 5) if free_pair[0] else (6, 7)

    def proj(w, c0, n, dst, mode, banks=None, stat=None, k_tiles=KT, k_base=0, g0=0):
        us = column_units(w, k_tiles, c0, n)
        banks = banks or pair()
        uses = [pl.use(b, us[-1][0]) for b in banks]
        last_hT_unit[0] = us[-1][0]
        return uses, [dict(unit=u, k0=k0, n=n, dst=dst, mode=mode, uses=uses, stat=stat, k_base=k_base, g0=g0,
                           k_tiles=k_tiles, last=u == us[-1][0]) for u, k0 in us]

    def now(made):
        uses, parts = made
        for p in parts:
            pl.add("proj", **p)
        return uses

    sum_uses, n_ada = [], [0]

    def ada_unit(n, part, done):
        pl.ada_done.append(done)
        pl.ada_units.append((4, BANK, [(0, BANK, rows(W["w_ada"], 4 * part, 4, n * BANK, BANK))]))
        return len(pl.ada_units) - 1

    def ada(n, part, shared=None):
        n_ada[0] += 1
        u = ada_unit(n, part, shared or n_ada[0])
        pl.add("ada", n=n, part=part, unit=u, done=n_ada[0], tiles=2 if shared else 4, slot_free=sum_uses[n - 2] if n >= 2 else None)

    def adasum(n, bank=None, shared=None):
        gate = {4: 0, 5: 0, 10: 1, 11: 1}.get(n)
        unit = None
        if shared:
            unit, use = shared
        else:
            use = pl.use(bank)
        sum_uses.append(use)
        pl.add("adasum", n=n, use=use, unit=unit, done=2 * n + 2, gate=gate, vec={0: 0, 1: 1, 3: 2, 4: 3}.get(n // 2))

    def group():
        g = pl.turn()
        pl.turned_groups.append(g)
        return g

    def turn(src, after, scale, bias, k0=0, nk=KT, banks=(4, 5, 6, 7)):
        first = pl.splits
        for j in range(nk // 2):
            if after[0] == "x_ready":
                w = ("x_ready", 2 * after[1] - 1) if j == 0 else ("x_ready", 2 * after[1]) if j == 2 else None
            elif after[0] == "halves":
                w = ("scr_ready", after[1 + j // 2]) if j % 2 == 0 else None
            else:
                w = after if j == 0 else None
            pl.add("turn", src=src, after=w, scale=scale, bias=bias,
                   kt=k0 + 2 * j, use=pl.turned_use(banks[j % len(banks)]), ti=pl.turned - 1, g=group(),
                   read_before=last_hT_unit[0])
        return first

    def stats(after):
        halves = after[0] == "x_ready"
        st = pl.new_stat(TT, 2 * TT if halves else TT)
        pl.add("stats", after=after, st=st)
        return st

    def head_turn(col, block, banks, after):
        use = pl.use(banks)
        pl.add("headturn", col=col, block=block, use=use, after=after)
        return use

    def softmax_heads(fillers, bias, v_col, v_w, q_ready, v_ready, diff=False, base=0):
        n0 = n_attn[0]
        n_attn[0] += 8
        pend_v = []
        fill = list(fillers)

        def t_of(h):
            k = n_turned_heads[0]
            n_turned_heads[0] += 1
            use = pl.use(2 + k % 2)
            pl.add("probturn", n=n0 + h, k=k, use=use, diff=diff)
            return k, use

        state = dict(o=None)

        def pv(h, kt):
            first = state["o"] is None
            if first:
                state["o"] = [pl.use(0), pl.use(1)]
            nv = (h // 2) if diff else h
            last = h == 7
            pl.add("pv", n=n0 + h, k=kt[0], turned=kt[1], slot=nv, v=v_col + nv * v_w, w=v_w, uses=state["o"], first=first, last=last,
                   v_ready=v_ready())

        for i in range(8 + 3):
            if diff and i in (3, 5, 7, 9):
                pl.add("mix", n=n0 + i - 2)
            if i < 8:
                h = i
                pl.add("qk", n=n0 + h, h=h, base=base, use=pl.use(4 + (n0 + h) % 2), bias=bias,
                       ready=q_ready(h))
            if fill:
                for f in fill.pop(0):
                    f()
            ready_v = len(pend_v)
            if 2 <= i <= 9 and (not diff or i % 2 == 1):
                pend_v.append((i - 2, t_of(i - 2)))
            if i < 8:
                pl.add("exp", n=n0 + i)
            if ready_v:
                pv(*pend_v.pop(0))
        while pend_v:
            pv(*pend_v.pop(0))
        while fill:
            for f in fill.pop(0):
                f()
        return n0, state["o"]

    def sb_heads(fillers, v_col, q_ready, v_ready):
        fill = list(fillers)
        o = [pl.use(0), pl.use(1)]

        def filler():
            if fill:
                for f in fill.pop(0):
                    f()

        for i in range(4 + 2):
            this, before, last = (2 * i, 2 * i + 1), (2 * i - 2, 2 * i - 1), (2 * i - 4, 2 * i - 3)
            if i >= 2:
                for m in last:
                    pl.add("sb_pv", m=m, v=v_col + m * HD, uses=o, v_ready=v_ready)
            if 1 <= i <= 4:
                for m in before:
                    pl.add("sb_keep", m=m)
            if i < 4:
                for m in this:
                    pl.add("sb_z", m=m, use=pl.use(4 + m % 2, read_by=("z_ready", m + 1)), ready=q_ready(m))
                pl.add("sb_log", pair=this)
            if i <= 4:
                filler()
            if 1 <= i <= 4:
                cums = []
                for m in before:
                    cums.append(pl.use(2 + n_turned_heads[0] % 2))
                    n_turned_heads[0] += 1
                    pl.add("sb_cum", m=m, use=cums[-1])
            if i < 4:
                filler()
            if 1 <= i <= 4:
                for m, use in zip(before, cums):
                    pl.add("sb_arg", m=m, use=use)
            if i <= 4:
                filler()
        while fill:
            filler()
        return o

    def ffn(up_units, stat, conv, g0, w_down):
        y = [None] * 4
        ups = {}

        def up(c):
            us = up_units(c)
            banks = (4, 5) if c % 2 == 0 else (6, 7)
            uses = [pl.use(b, us[-1][0]) for b in banks]
            ups[c] = uses
            last_hT_unit[0] = us[-1][0]
            return [lambda u=u, k0=k0: pl.add("up", c=c, unit=u, k0=k0, uses=uses, stat=stat, conv=conv, g0=g0,
                                              ci=chunk_no[0] + c, last=k0 > 0) for u, k0 in us]

        def turn_hidden(c):
            banks = (4, 5) if c % 2 == 0 else (6, 7)
            uses = [pl.use(b) for b in banks] if conv else [pl.turned_use(banks[0])]
            g = pl.turn() if conv else group()
            before = downs[c - 2] if c >= 2 else None
            pl.add("hturn", c=c, ci=chunk_no[0] + c, uses=uses, ups=ups[c], conv=conv, g=g, down_before=before,
                   cc=conv_no[0] + c, ti=pl.turned - 1)
            gs[c] = g

        def down(c):
            u = pl.unit(2, D, [(0, D, rows(w_down, 2 * c, 2, 0, D))])
            downs[c] = u
            if c == 0:
                for b in range(4):
                    y[b] = pl.use(b, by_unit=b == 3)
            if c != NFC - 2:
                pl.add("down", c=c, unit=u, uses=y, g=gs[c], part=(0, 8))
                return
            cut = 2 if conv else 4
            pl.add("down", c=c, unit=u, uses=y, g=gs[c], part=(0, cut))
            turn_hidden(c + 1)
            pl.add("down", c=c, unit=u, uses=y, g=gs[c], part=(cut, 8))

        downs, gs = {}, {}
        for stage in up(0):
            stage()
        for c in range(1, NFC):
            first, second = up(c)
            first()
            if c == 1:
                turn_hidden(0)
            second()
            down(c - 1)
            if c < NFC - 1:
                turn_hidden(c)
        down(NFC - 1)
        y[3].unit = downs[NFC - 1]
        if not conv:
            chunk_no[0] += NFC
        else:
            conv_no[0] += NFC
        return y

    chunk_no, conv_no = [0], [0]

    def post(mode, y, **kw):
        pl.add("post", mode=mode, uses=y, row=rows_used[0], **kw)
        if mode == "norm":
            rows_used[0] += 1
        n_x[0] += 1
    rows_used = [0]

    def o_evac(o, dst, final, n0=None):
        if final:
            n_scr[0] += 1
            o[1].read_by = ("scr_ready", n_scr[0])
            pl.evacuated[o[1].bank] -= 1
        pl.add("oevac", mode="plain" if n0 is None else "norm", uses=o, n0=n0, dst=dst, final=final)

    def scr_version():
        n_scr[0] += 1
        return n_scr[0]

    pl.add("condition", use=pl.use(3, read_by=("c_act_ready", 1)))
    st = None
    shared = None
    for n in range(4):
        ada(n, 0)
        if n == 0:
            pl.add("vectors", uses=[pl.use(b) for b in (4, 5, 6, 7)])
        else:
            adasum(n - 1, shared=shared)
        if n == 1:
            st = stats(("x_loaded", 16))
        if n == 3:
            pl.add("normalise", st=st)
        use = pl.use(n)
        ada(n, 1, use)
        shared = (len(pl.ada_units) - 1, use)
    adasum(3, shared=shared)
    pl.add("modfinal", vec=1, gain=0)
    pl.add("prime", units=[0])
    g0 = turn("scr", ("halves", scr_version(), scr_version()), ("mod", 1), ("mod", 0))
    pl.add("prime", units=list(range(1, LOOK)))
    pl.add("late_loads")
    pl.add("load_bias", which=0, after=("split_done", pl.splits))
    r = {}

    def w_in_chunk(i, dst, mode, banks=None):
        return proj(W["w_in"], i * BANK, BANK, dst, mode, banks, g0=g0)

    def turns_of(name, i, blk, bank, after):
        for t in range(2):
            r[name + str(t)] = head_turn(i * BANK + 256 * t, blk + 2 * t, bank + t, after)

    def q_ready_of(q, k):
        return lambda h: [r[q + str(h // 4)], r[k + str(h // 4)]]

    later_ada = [(n, part) for n in range(4, 12) for part in range(2)]

    sum_due = []

    def sum_next(bank=3):
        if sum_due:
            adasum(sum_due.pop(), bank)

    def ada_next(bank=3):
        n, part = later_ada.pop(0)
        ada(n, part)
        sum_next(bank)
        if part:
            sum_due.append(n)

    r["qa"] = now(w_in_chunk(0, 0, "plain"))
    ada_next()
    r["ka"] = now(w_in_chunk(1, BANK, "plain"))
    turns_of("qa", 0, 0, 2, ("uses", r["qa"]))
    ada_next()
    r["va"] = now(w_in_chunk(2, 2 * BANK, "plain"))
    turns_of("ka", 1, 4, 2, ("uses", r["ka"]))


    def chunk_fillers(name, i, dst, mode):
        made = {}

        def first():
            made["uses"], made["parts"] = w_in_chunk(i, dst, mode, (6, 7))
            r[name] = made["uses"]
            pl.add("proj", **made["parts"][0])

        def second():
            pl.add("proj", **made["parts"][1])
        return first, second

    fa = []
    for name, i in (("qb", 3), ("kb", 4), ("vb", 5)):
        first, second = chunk_fillers(name, i, i * BANK, "plain")
        fa += [[first, ada_next], [second]]
    fa.append([lambda: turns_of("qb", 3, 8, 6, ("uses", r["qb"])), lambda: turns_of("kb", 4, 12, 6, ("uses", r["kb"]))])
    fb = []
    for i in range(4):
        first, second = chunk_fillers(f"gate{i}", 6 + i, (0, BANK, 3 * BANK, 4 * BANK)[i], "tanh")
        fb += [[first], [second], [ada_next]]
    n0, o = softmax_heads(fa, "moba", 2 * BANK, HD, q_ready_of("qa", "ka"), lambda: r["va"])
    pl.add("lambda")
    o_evac(o, ("scr", 0), False, n0)

    def branch(w, n, k_base, banks, g0):
        return now(proj(W[w], n * BANK, BANK, None, "hold", banks, k_tiles=4, k_base=k_base, g0=g0))

    moba_out, ua, y = o, [], []
    moba_g0 = None

    def turn_moba():
        nonlocal moba_g0
        moba_g0 = turn("scr", ("uses", moba_out), None, None, 0, 4, (6, 7))

    fb += [[turn_moba], [lambda: ua.append(branch("w_br_moba", 0, 0, (4, 5), moba_g0))]]
    o = sb_heads(fb, 5 * BANK, q_ready_of("qb", "kb"), r["vb"])
    o_evac(o, ("scr", BANK), True)
    v = n_scr[0]
    ada_next(3)
    ua.append(branch("w_br_moba", 1, 0, (2, 3), moba_g0))
    g0 = turn("scr", ("scr_ready", v), None, None, 4, 4, (6, 7)) - 2
    ada_next(0)
    ub_ = [branch("w_br_sb", 0, 4, (6, 7), g0)]
    ada_next(0)
    ub_.append(branch("w_br_sb", 1, 4, (0, 1), g0))
    pl.add("mixbranch", n=0, ya=ua[0], yb=ub_[0])
    g0 = turn("scr", ("scr_ready", scr_version()), 0.5, None, 0, 4, (6, 7))
    pl.add("mixbranch", n=1, ya=ua[1], yb=ub_[1])
    for n in range(2):
        if n == 1:
            g0 = turn("scr", ("scr_ready", scr_version()), 0.5, None, 4, 4, (6, 7)) - 2
        for half in range(2):
            u = pl.unit(4, BANK, [(0, BANK, rows(W["w_out"], 4 * n, 4, half * BANK, BANK))])
            if n == 0:
                y.append([pl.use(half, by_unit=True), pl.use(2 + half, by_unit=True)])
            else:
                for use in y[half]:
                    use.unit = u
            last_hT_unit[0] = u
            pl.add("proj", unit=u, k0=4 * n, n=BANK, dst=None, mode="hold", uses=y[half], stat=None, k_base=0, g0=g0,
                   k_tiles=KT, last=n == 1)
            if later_ada:
                ada_next(4)
    sum_next(4)
    pl.add("modfinal", vec=3, gain=8)
    post("gate", [y[0][0], y[1][0], y[0][1], y[1][1]], gate=0)
    st = stats(("x_ready", n_x[0]))
    pl.add("normalise", st=st)
    g0 = turn("scr", ("halves", scr_version(), scr_version()), ("mod", 3), ("mod", 2))

    def up_pair(wv, wg, cv0, cg0):
        def make(c):
            us = []
            for k0 in (0, 4):
                u = pl.unit(4, 2 * FC, [(0, FC, rows(wv, k0, 4, cv0 + c * FC, FC)),
                                        (FC, FC, rows(wg, k0, 4, cg0 + c * FC, FC))])
                us.append((u, k0))
            return us
        return make

    y = ffn(up_pair(W["w_up"], W["w_up"], 0, D_FF), None, True, g0, W["w_down"])
    post("gate", y, gate=1)
    st = stats(("x_ready", n_x[0]))
    pl.add("finalnorm", st=st, row=rows_used[0])
    rows_used[0] += 1
    n_x[0] += 1

    for l in range(2):
        def gain(j):
            return ("gain", 16 + (l * 6 + j) * 8)

        def swiglu(i, j):
            g0 = turn("X", ("x_ready", n_x[0]), gain(j), None)
            st = stats(("x_ready", n_x[0]))
            y = ffn(up_pair(W["ffn_wg"][l, i], W["ffn_wu"][l, i], 0, 0), st, False, g0, W["ffn_wd"][l, i])
            post("norm", y, st=pl.new_stat(TT, 2 * TT), factor=0.5)

        outs = {}

        def turn_first(src, after):
            def go():
                outs["g0"] = turn(src, after, None, None, 0, 4, (6, 7))
            return go

        def out_unit(w, half, part, g0):
            u = pl.unit(4, BANK, [(0, BANK, rows(w, 4 * part, 4, half * BANK, BANK))])
            if part:
                for use in outs[half]:
                    use.unit = u
            last_hT_unit[0] = u
            pl.add("proj", unit=u, k0=4 * part, n=BANK, dst=None, mode="hold", uses=outs[half], stat=None, k_base=0,
                   g0=g0, k_tiles=KT, last=part == 1)

        def out_first(w):
            def go():
                outs[0] = [pl.use(b, by_unit=True) for b in (6, 7)]
                out_unit(w, 0, 0, outs["g0"])
            return go

        def out_rest(src, w):
            outs[1] = [pl.use(b, by_unit=True) for b in (2, 3)]
            out_unit(w, 1, 0, outs["g0"])
            g0 = turn(src, ("scr_ready", n_scr[0]), None, None, 4, 4, (4, 5)) - 2
            for half in range(2):
                out_unit(w, half, 1, g0)
            return [outs[0][0], outs[1][0], outs[0][1], outs[1][1]]

        swiglu(0, 0)
        if l == 1:
            pl.add("load_bias", which=1, after=("x_ready", n_x[0]))
            pl.add("load_bias", which=2, after=("x_ready", n_x[0]))
        g0 = turn("X", ("x_ready", n_x[0]), gain(2), None)
        st = stats(("x_ready", n_x[0]))
        if l == 0:
            w = W["even_w_in"][0]

            def ep(i, banks=None):
                n = BANK if i < 6 else EVEN_W - 6 * BANK
                return proj(w, i * BANK, n, i * BANK, "rstd", banks, st, g0=g0)

            u6 = now(ep(6))
            u0 = now(ep(0))
            r6 = rope(pl, 6 * BANK, 9, IDX_DIM, u6, True)
            u1 = now(ep(1))
            r0 = rope(pl, 0, 8, HD, u0)
            pl.add("idxturn", uses=[pl.use(2), pl.use(3)], after=("rope_ready", r6))
            u2, parts = ep(2)
            pl.add("proj", **parts[0])
            r1 = rope(pl, BANK, 8, HD, u1)
            for h in range(4):
                pl.add("idx", h=h, use=pl.use(h % 2))
            turns_of("aq", 0, 0, 2, ("rope_ready", r0))
            pl.add("proj", **parts[1])
            for h in range(4, IDX_HEADS):
                pl.add("idx", h=h, use=pl.use(h % 2))
            turns_of("ak", 1, 4, 2, ("rope_ready", r1))

            held = {}

            def first_of(i):
                def go():
                    held[i], held["parts"] = ep(i, (6, 7))
                    pl.add("proj", **held["parts"][0])
                return go

            def second_of():
                pl.add("proj", **held["parts"][1])

            def rope_of(i, name):
                def go():
                    held[name] = rope(pl, i * BANK, 8, HD, held[i])
                return go

            def fill_turn(i, nm, blk):
                return lambda: turns_of(nm, i, blk, 6, ("rope_ready", held[nm]))

            def topk(j):
                return lambda: pl.add("topk", j=j)

            fills = [[first_of(3), topk(0)], [second_of, topk(1)], [topk(2), rope_of(3, "bq")],
                     [first_of(4), topk(3)], [second_of, topk(4)],
                     [fill_turn(3, "bq", 8), topk(5), rope_of(4, "bk")],
                     [topk(6)], [topk(7), fill_turn(4, "bk", 12)]]
            n0, o = softmax_heads(fills, "mask", 2 * BANK, 2 * HD, q_ready_of("aq", "ak"), lambda: u2,
                                  diff=True)
            sd = pl.new_stat(8)
            pl.add("diffout", uses=o, st=sd)
            v = scr_version()
            fills = [[first_of(5)], [second_of, lambda: pl.add("diffnorm", uses=o_diff, st=sd, v=v)], [], [], [],
                     [turn_first("scr", ("scr_ready", v))], [out_first(W["even_w_out"][0])]]
            o_diff = o
            n0, o = softmax_heads(fills, "sel", 5 * BANK, HD, q_ready_of("bq", "bk"), lambda: held[5], base=8)
            o_evac(o, ("scr", BANK), True, n0)
            y = out_rest("scr", W["even_w_out"][0])
        else:
            w = W["odd_w_in"][0]
            uo = {}

            def op(i, banks=None):
                return proj(w, i * BANK, BANK, i * BANK, "rstd", banks, st, g0=g0)

            uo[0] = now(op(0))
            uo[2] = now(op(2))
            turns_of("oq", 0, 0, 2, ("uses", uo[0]))
            uo[4] = now(op(4))
            turns_of("ok", 2, 4, 2, ("uses", uo[2]))

            def odd_first(i):
                def go():
                    uo[i], uo["parts"] = op(i, (6, 7))
                    pl.add("proj", **uo["parts"][0])
                return go

            def odd_second():
                pl.add("proj", **uo["parts"][1])

            fills = [[odd_first(1)], [odd_second], [], [lambda: turns_of("pq", 1, 8, 6, ("uses", uo[1]))],
                     [odd_first(3)], [odd_second], [], [lambda: turns_of("pk", 3, 12, 6, ("uses", uo[3]))]]
            n0, o = softmax_heads(fills, "odd0", 4 * BANK, HD, q_ready_of("oq", "ok"), lambda: uo[4])
            o_evac(o, ("pr", 0), False, n0)
            fills = [[odd_first(5)], [odd_second], [], [turn_first("pr", ("uses", o))], [], [out_first(W["odd_w_out"][0])]]
            n0, o = softmax_heads(fills, "odd1", 5 * BANK, HD, q_ready_of("pq", "pk"), lambda: uo[5], base=8)
            o_evac(o, ("pr", BANK), True, n0)
            y = out_rest("pr", W["odd_w_out"][0])
        post("norm", y, st=pl.new_stat(TT, 2 * TT), factor=1.0)
        swiglu(1, 4)
    pl.x_final = 2 * n_x[0]
    return pl


def rope(pl, col, heads, dim, uses, replicate=False):
    n = pl.ropes
    pl.ropes = n + 1
    pl.add("rope", col=col, heads=heads, dim=dim, uses=uses, replicate=replicate, i=n)
    return n + 1


def program(nc, consts, x, c, w_ada, b_ada, g_mix, w_in, w_br_moba, w_br_sb, w_out, rel_bias, g_ffn, w_up,
            w_conv, b_conv, w_down, g_final, norm_g, ffn_wg, ffn_wu, ffn_wd, even_w_in, even_w_out,
            even_lambda, even_subln, odd_w_in, odd_w_out, odd_rel_bias, table, out):
    with ExitStack() as ctx:
        def sb(name, shape, dt=F32):
            return ctx.enter_context(nc.sbuf_tensor(name, shape, dt))

        def sem(name):
            return ctx.enter_context(nc.semaphore(name))

        raw = sb("raw", [P, RAW, UNIT])
        w_hi = sb("w_hi", [P, SPLIT, UNIT], F32R)
        w_lo = sb("w_lo", [P, SPLIT, UNIT], F32R)
        X = sb("X", [P, TT, D])
        hT_hi = sb("hT_hi", [P, KT, S], F32R)
        hT_lo = sb("hT_lo", [P, KT, S], F32R)
        hc_hi = sb("hc_hi", [P, 2, 2 * S], F32R)
        hc_lo = sb("hc_lo", [P, 2, 2 * S], F32R)
        turned = sb("turned", [P, 2, BANK])
        scr = sb("scr", [P, TT, D])
        PR = sb("PR", [P, TT * EVEN_W])
        QK = sb("QK", [P, 16, S])
        IT = sb("IT", [P, 3, S])
        gate_rows = sb("gate_rows", [P, 2, D])
        g_row = sb("g_row", [P, D])
        ada_acc = sb("ada_acc", [P, 2, BANK])
        logit = sb("logit", [P, 4, SC])
        prob = sb("prob", [P, 4, SC])
        probT = sb("probT", [P, 2, SC])
        work = sb("work", [P, SC])
        junk = sb("junk", [P, 2, BANK], BF16)
        lam_in = work[:, 0:4 * HD].rearrange("p (a n) -> p a n", a=4)
        CONSTS = 2 * P + 2 * SC + TT * 2 * HD + TT * 2 * IDX_DIM
        cst = sb("cst", [P, CONSTS])
        ident, later = cst[:, 0:P], cst[:, P:2 * P]
        chunk_mask = cst[:, 2 * P:2 * P + SC]
        minus_past = cst[:, 2 * P + SC:2 * P + 2 * SC]
        r64 = cst[:, 2 * P + 2 * SC:2 * P + 2 * SC + TT * 2 * HD].rearrange("p (t c) -> p t c", t=TT)
        r32 = cst[:, 2 * P + 2 * SC + TT * 2 * HD:CONSTS].rearrange("p (t c) -> p t c", t=TT)
        ones = sb("ones", [P, P])
        NV = 112
        cols = sb("cols", [P, NV])
        ada_b = sb("ada_b", [P, 48])
        conv_c = sb("conv_c", [P, 4 * CONV])
        mod = sb("mod", [P, 4, KT])
        c_act = sb("c_act", [P, KT])
        stat = sb("stat", [P, 340])
        nmax = sb("nmax", [P, 40, 2])
        sums = sb("sums", [P, 40, 2])
        rsum = sb("rsum", [P, 40, 2])
        top = sb("top", [P, 16])
        lam = sb("lam", [P, 4])
        subln = sb("subln", [P, P])
        bucket = sb("bucket", [8, REL_BUCKETS])
        dist = logit[0:8, 0, 0:BIAS_T]
        selbias = sb("selbias", [P, SC])

        psum = ctx.enter_context(nc.psum_tensor("psum", [P, 8, BANK], F32))

        sg = PR[:, 0:1024].rearrange("p (b t n) -> p b t n", b=2, t=TT)
        hid = PR[:, 1024:2048].rearrange("p (b t n) -> p b t n", b=2, t=TT)
        ub = PR[:, 2048:4096].rearrange("p (b t n) -> p b t n", b=2, t=TT)
        cv = PR[:, 4096:5120]
        gg = PR[:, 5120:5632]
        hfull = PR[:, 5632:6144]
        c_rows = PR[0:KT, 4 * P:5 * P]
        pr = PR[:, :].rearrange("p (t n) -> p t n", t=TT)

        weight_loaded = [sem(f"weight_loaded{i}") for i in range(RAW)]
        hi_ready, lo_ready, unit_used = sem("hi_ready"), sem("lo_ready"), sem("unit_used")
        psum_ready = [sem(f"psum_ready{i}") for i in range(8)]
        psum_read = [sem(f"psum_read{i}") for i in range(8)]
        act_step, dve_step, pool_step = sem("act_step"), sem("dve_step"), sem("pool_step")
        c_loaded, ident_loaded = sem("c_loaded"), sem("ident_loaded")
        consts_loaded, x_loaded, vectors_loaded = sem("consts_loaded"), sem("x_loaded"), sem("vectors_loaded")
        small_loaded, bucket_loaded, gate_bias_loaded = sem("small_loaded"), sem("bucket_loaded"), sem("gate_bias_loaded")
        ada_used = sem("ada_used")
        c_act_ready = sem("c_act_ready")
        ones_ready = sem("ones_ready")
        mod_final = sem("mod_final")
        turned_ready, split_done = sem("turned_ready"), sem("split_done")
        squares_ready, rstd_ready = sem("squares_ready"), sem("rstd_ready")
        x_ready, scr_ready = sem("x_ready"), sem("scr_ready")
        dist_ready, table_stored, bias_cleared = sem("dist_ready"), sem("table_stored"), sem("bias_cleared")
        bias_loaded = [sem(f"bias_loaded{i}") for i in range(3)]
        logits_ready, probs_ready, mixed_ready = sem("logits_ready"), sem("probs_ready"), sem("mixed_ready")
        z_ready, log_ready, log_keep_ready = sem("z_ready"), sem("log_ready"), sem("log_keep_ready")
        weight_ready, weight_masked = sem("weight_ready"), sem("weight_masked")
        silu_ready, conv_first, gelu_ready = sem("silu_ready"), sem("conv_first"), sem("gelu_ready")
        rope_swapped, rope_ready = sem("rope_swapped"), sem("rope_ready")
        score_ready, selected = sem("score_ready"), sem("selected")
        lam_dots, lam_exp = sem("lam_dots"), sem("lam_exp")
        g_row_loaded, g_row_used = sem("g_row_loaded"), sem("g_row_used")
        stored = sem("stored")

        plan = build_plan(dict(w_ada=w_ada[0], w_in=w_in[0], w_br_moba=w_br_moba[0], w_br_sb=w_br_sb[0], w_out=w_out[0],
                               w_up=w_up[0], w_down=w_down[0], ffn_wg=ffn_wg, ffn_wu=ffn_wu, ffn_wd=ffn_wd,
                               even_w_in=even_w_in, even_w_out=even_w_out, odd_w_in=odd_w_in, odd_w_out=odd_w_out))
        steps, units, ada_units = plan.steps, plan.units, plan.ada_units
        loads = plan.load_order()
        raw_slot, landed, loaded = {}, {}, [0] * RAW
        for i, what in enumerate(loads):
            raw_slot[what] = i % RAW
            loaded[i % RAW] += 16 * len((units if what[0] == "w" else ada_units)[what[1]][2])
            landed[what] = loaded[i % RAW]
        named = dict(x_loaded=x_loaded, x_ready=x_ready, scr_ready=scr_ready, split_done=split_done,
                     rope_ready=rope_ready, turned_ready=turned_ready, c_act_ready=c_act_ready,
                     z_ready=z_ready)
        bufs = dict(X=X, scr=scr, pr=pr)

        def wait_ready(eng, use):
            if use.unit is not None:
                eng.wait_ge(unit_used, use.unit + 1)
            else:
                eng.wait_ge(psum_ready[use.bank], use.ready)

        def wait_read(eng, use):
            name, value = use.read_by
            eng.wait_ge(psum_read[use.bank] if name == "psum_read" else named[name], value)

        def wait_free(eng, use):
            if use.prev is not None:
                wait_read(eng, use.prev)

        def col(st, part, i):
            return stat[:, st[part][0] + i:st[part][0] + i + 1]

        def unit_view(tile, slot, u):
            nk, w, _ = units[u]
            return tile[:, slot, 0:nk * w]

        rel_bias_rows = dict(moba=lambda h: scr[:, :, :].rearrange("p t (g n) -> p (t g) n", n=S)[:, h, :],
                             odd0=lambda h: gate_rows[:, :, :].rearrange("p t (g n) -> p (t g) n", n=S)[:, h, :],
                             odd1=lambda h: scr[:, :, :].rearrange("p t (g n) -> p (t g) n", n=S)[:, h, :])

        block = ctx.enter_context(nc.Block())

        @block.sync
        def _(sp):
            sp.dma_start(c_rows[:, :], c.rearrange("o (k n) -> (o k) n", n=P)).then_inc(c_loaded, 16)
            sp.dma_start(cst[:, 0:P], consts[:, 0:P]).then_inc(ident_loaded, 16)
            for i, what in enumerate(loads):
                if i >= RAW:
                    before, number = loads[i - RAW]
                    if before == "w":
                        sp.wait_ge(hi_ready, number + 1)
                        sp.wait_ge(lo_ready, number + 1)
                    elif isinstance(plan.ada_done[number], int):
                        sp.wait_ge(ada_used, plan.ada_done[number])
                    else:
                        wait_ready(sp, plan.ada_done[number])
                nk, w, parts = (units if what[0] == "w" else ada_units)[what[1]]
                view = raw[:, i % RAW, 0:nk * w].rearrange("p (k n) -> p k n", k=nk)
                for c0, n, src in parts:
                    sp.dma_start(view[:, :, c0:c0 + n], src).then_inc(weight_loaded[i % RAW], 16)
            sp.wait_ge(x_ready, plan.x_final)
            sp.dma_start(out[0].rearrange("(t p) d -> p t d", p=P), X[:, :, :]).then_inc(stored, 16)
            sp.wait_ge(stored, 16)

        @block.gpsimd
        def _(pool):
            n = [0]

            def mark(ins):
                ins.then_inc(pool_step, 1)
                n[0] += 1
                return n[0]

            def link(ins):
                pool.wait_ge(pool_step, mark(ins))

            nc.gpsimd.memset(ones[:, :], 1.0).then_inc(ones_ready, 1)
            link(nc.gpsimd.memset(dist, NEG))
            pool.wait_ge(bucket_loaded, 16)
            bounds = t5_bounds()
            for b in range(REL_BUCKETS):
                a, e = P - 1 + bounds[b], P - 1 + bounds[b + 1]
                ins = nc.gpsimd.tensor_copy(dist[:, a:e], bucket[:, b:b + 1].to_broadcast([8, e - a]))
            ins.then_inc(dist_ready, 1)
            pool.wait_ge(dist_ready, 1)
            pool.dma_start(table, dist).then_inc(table_stored, 16)
            gain_rows = [g_final.rearrange("(o d) -> o d", o=1)]
            for l in range(2):
                for j in (1, 3, 5):
                    gain_rows.append(norm_g[l, j:j + 1, :])

            def load_gain(i):
                if i:
                    pool.wait_ge(g_row_used, i)
                pool.dma_start(g_row[:, :], gain_rows[i].to_broadcast([P, D])).then_inc(g_row_loaded, 16)

            load_gain(0)
            for kind, a in steps:
                if kind == "load_bias":
                    which = a["which"]
                    pool.wait_ge(named[a["after"][0]], a["after"][1])
                    if which == 0:
                        pool.wait_ge(table_stored, 16)
                        src = bass.AP(table.tensor, table.offset, [[1, P], [BIAS_T, 8], [1, S]])
                        pool.dma_start(scr[:, :, :].rearrange("p t (g n) -> p (t g) n", n=S), src)\
                            .then_inc(bias_loaded[0], 16)
                    else:
                        buf = (gate_rows, scr)[which - 1][:, :, :].rearrange("p t (g n) -> p (t g) n", n=S)
                        h0 = 8 * (which - 1)
                        table_w = odd_rel_bias.shape[2]
                        base = odd_rel_bias.offset + h0 * table_w
                        nc.gpsimd.memset(buf[0:CHUNK, :, 0:CHUNK], NEG).then_inc(bias_cleared, 1)
                        lo = bass.AP(odd_rel_bias.tensor, base, [[1, CHUNK], [table_w, 8], [1, S - CHUNK]])
                        hi = bass.AP(odd_rel_bias.tensor, base, [[1, CHUNK], [table_w, 8], [1, S]])
                        pool.dma_start(buf[0:CHUNK, :, CHUNK:S], lo).then_inc(bias_loaded[which], 16)
                        pool.dma_start(buf[CHUNK:P, :, :], hi).then_inc(bias_loaded[which], 16)
                elif kind == "rope":
                    c0, nh, dim, tab = a["col"], a["heads"], a["dim"], (r64 if a["dim"] == HD else r32)
                    w = nh * dim
                    for use in a["uses"]:
                        wait_read(pool, use)
                    if a["i"]:
                        pool.wait_ge(rope_ready, a["i"])
                    pool.wait_ge(consts_loaded, 16)
                    for t in range(TT):
                        sw = pr[:, t, c0:c0 + w].rearrange("p (h s d) -> p h s d", h=nh, s=2)[:, :, ::-1, :]
                        sn = tab[:, t, dim:2 * dim].rearrange("p (s d) -> p s d", s=2)[:, None, :, :]\
                            .to_broadcast([P, nh, 2, dim // 2])
                        o = scr[:, t, BANK:BANK + w].rearrange("p (h s d) -> p h s d", h=nh, s=2)
                        ins = nc.gpsimd.tensor_tensor(o, sw, sn, ALU.mult)
                    ins.then_inc(rope_swapped, 1)
                elif kind == "post" and a["mode"] == "norm" or kind == "finalnorm":
                    if a["row"] + 1 < len(gain_rows):
                        load_gain(a["row"] + 1)
                elif kind == "sb_arg":
                    m = a["m"]
                    pool.wait_ge(weight_ready, m + 1)
                    for blk in (0, 2):
                        v = logit[:, m % 4, blk * P:(blk + 1) * P]
                        ins = nc.gpsimd.affine_select(out=v, in_=v, compare_op=ALU.is_gt, fill=0.0, base=0,
                                                      pattern=[[1, P]], channel_multiplier=-1)
                    ins.then_inc(weight_masked, 1)

        @block.scalar
        def _(act):
            n = [0]

            def mark(ins):
                ins.then_inc(act_step, 1)
                n[0] += 1
                return n[0]

            def link(ins):
                act.wait_ge(act_step, mark(ins))

            act.dma_start(PR[0:8, 0:P], g_mix.rearrange("o (k n) -> (o k) n", n=P)).then_inc(vectors_loaded, 16)
            act.dma_start(PR[8:16, 0:P], g_ffn.rearrange("o (k n) -> (o k) n", n=P)).then_inc(vectors_loaded, 16)
            act.dma_start(PR[16:112, 0:P], norm_g.rearrange("l j (k n) -> (l j k) n", n=P)).then_inc(vectors_loaded, 16)
            act.dma_start(PR[0:48, P:2 * P], b_ada.rearrange("o (k n) -> (o k) n", n=P)).then_inc(vectors_loaded, 16)
            act.dma_start(PR[0:88, 2 * P:3 * P], w_conv[0, 0:2].rearrange("j (k n) -> (j k) n", n=P))\
                .then_inc(vectors_loaded, 16)
            act.dma_start(PR[0:44, 3 * P:4 * P], w_conv[0, 2:3].rearrange("j (k n) -> (j k) n", n=P))\
                .then_inc(vectors_loaded, 16)
            act.dma_start(PR[44:88, 3 * P:4 * P], b_conv.rearrange("j (k n) -> (j k) n", n=P))\
                .then_inc(vectors_loaded, 16)
            act.dma_start(X[:, :, :], x[0].rearrange("(t p) d -> p t d", p=P)).then_inc(x_loaded, 16)
            act.dma_start(bucket[:, :], rel_bias).then_inc(bucket_loaded, 16)

            def split(s):
                if s >= len(units):
                    return
                what = ("w", s)
                act.wait_ge(weight_loaded[raw_slot[what]], landed[what])
                if s >= SPLIT:
                    act.wait_ge(unit_used, s - SPLIT + 1)
                nc.scalar.activation(unit_view(w_hi, s % SPLIT, s), unit_view(raw, raw_slot[what], s), ACT.Copy)\
                    .then_inc(hi_ready, 1)

            def turned_out(use, ti, scale, bias, kt):
                wait_ready(act, use)
                if ti >= 2:
                    act.wait_ge(split_done, plan.turned_groups[ti - 2] + 1)
                if scale is None:
                    nc.scalar.activation(turned[:, ti % 2, :], psum[:, use.bank, :], ACT.Copy).then_inc(turned_ready, 1)
                    return
                if scale == 0.5:
                    nc.scalar.activation(turned[:, ti % 2, :], psum[:, use.bank, :], ACT.Copy, scale=0.5)\
                        .then_inc(turned_ready, 1)
                    return
                if scale[0] == "mod":
                    act.wait_ge(mod_final, 1 if scale[1] == 1 else 2)
                for i in range(2):
                    dst, src = turned[:, ti % 2, i * S:(i + 1) * S], psum[:, use.bank, i * S:(i + 1) * S]
                    k = kt + i
                    if scale[0] == "mod":
                        ins = nc.scalar.activation(dst, src, ACT.Identity, scale=mod[:, scale[1], k:k + 1],
                                                   bias=mod[:, bias[1], k:k + 1])
                    else:
                        ins = nc.scalar.activation(dst, src, ACT.Copy, scale=cols[:, scale[1] + k:scale[1] + k + 1])
                ins.then_inc(turned_ready, 1)

            for kind, a in steps:
                if kind == "condition":
                    wait_ready(act, a["use"])
                    nc.scalar.activation(c_act[:, :], psum[:, a["use"].bank, 0:KT], ACT.Silu).then_inc(c_act_ready, 1)
                elif kind == "late_loads":
                    act.dma_start(gate_rows[:, 0, :], b_ada[0:1, 2 * D:3 * D].to_broadcast([P, D])).then_inc(gate_bias_loaded, 16)
                    act.dma_start(gate_rows[:, 1, :], b_ada[0:1, 5 * D:6 * D].to_broadcast([P, D])).then_inc(gate_bias_loaded, 16)
                    act.dma_start(lam_in[:, :, :], even_lambda.to_broadcast([P, 4, HD])).then_inc(small_loaded, 16)
                    act.dma_start(subln[:, :], even_subln.to_broadcast([P, P])).then_inc(small_loaded, 16)
                    act.dma_start(cst[:, P:CONSTS], consts[:, P:CONSTS]).then_inc(consts_loaded, 16)
                elif kind == "lambda":
                    act.wait_ge(lam_dots, 1)
                    nc.scalar.activation(lam[:, 0:2], lam[:, 0:2], ACT.Exp).then_inc(lam_exp, 1)
                elif kind == "prime":
                    for s in a["units"]:
                        split(s)
                elif kind == "stats":
                    st = a["st"]
                    name, value = a["after"]
                    for j in range(2 * TT if name == "x_ready" else 0):
                        half, t = j // TT, j % TT
                        if t == 0:
                            act.wait_ge(x_ready, 2 * value - 1 + half)
                        act.wait_ge(squares_ready, st["squares"] + max(j - 1, 0))
                        nc.scalar.activation(junk[:, j % 2, :], X[:, t, half * BANK:(half + 1) * BANK], ACT.Square,
                                             accum_out=col(st, ("ss", "ss2")[half], t)).then_inc(squares_ready, 1)
                    if name != "x_ready":
                        act.wait_ge(named[name], value)
                    for t in range(TT if name != "x_ready" else 0):
                        if st["squares"] + t:
                            act.wait_ge(squares_ready, st["squares"] + t)
                        nc.scalar.activation(junk[:, :, :].rearrange("p b n -> p (b n)"), X[:, t, :], ACT.Square,
                                             accum_out=col(st, "ss", t)).then_inc(squares_ready, 1)
                elif kind == "post":
                    if a["mode"] == "norm":
                        st = a["st"]
                        for j in range(2 * TT):
                            half, t = j // TT, j % TT
                            use = a["uses"][2 * t + half]
                            wait_ready(act, use)
                            act.wait_ge(squares_ready, st["squares"] + max(j - 1, 0))
                            nc.scalar.activation(junk[:, j % 2, :], psum[:, use.bank, :], ACT.Square,
                                                 accum_out=col(st, ("ss", "ss2")[half], t)).then_inc(squares_ready, 1)
                elif kind == "diffout":
                    for t in range(TT):
                        use = a["uses"][t]
                        wait_ready(act, use)
                        nc.scalar.activation(scr[:, t, BANK:D], psum[:, use.bank, :], ACT.Square)
                        nc.scalar.activation(scr[:, t, 0:BANK], psum[:, use.bank, :], ACT.Copy)\
                            .then_inc(psum_read[use.bank], 1)
                elif kind == "turn":
                    turned_out(a["use"], a["ti"], a["scale"], a["bias"], a["kt"])
                elif kind == "proj":
                    split(a["unit"] + LOOK)
                    if a["mode"] == "hold" or not a["last"]:
                        continue
                    for t in range(TT):
                        use = a["uses"][t]
                        wait_ready(act, use)
                        dst, src = pr[:, t, a["dst"]:a["dst"] + a["n"]], psum[:, use.bank, 0:a["n"]]
                        if a["mode"] == "rstd":
                            act.wait_ge(rstd_ready, a["stat"]["i"] + 1)
                            ins = nc.scalar.activation(dst, src, ACT.Copy, scale=col(a["stat"], "r", t))
                        else:
                            ins = nc.scalar.activation(dst, src, ACT.Tanh if a["mode"] == "tanh" else ACT.Copy,
                                                       scale=0.5 if a["mode"] == "tanh" else 1.0)
                        ins.then_inc(psum_read[use.bank], 1)
                elif kind == "headturn":
                    wait_ready(act, a["use"])
                    nc.scalar.activation(QK[:, a["block"]:a["block"] + 2, :].rearrange("p b n -> p (b n)"),
                                         psum[:, a["use"].bank, :], ACT.Copy).then_inc(psum_read[a["use"].bank], 1)
                elif kind == "idxturn":
                    for use, dst, w in ((a["uses"][0], IT[:, 0:2, :].rearrange("p b n -> p (b n)"), 2 * S),
                                        (a["uses"][1], IT[:, 2, :], S)):
                        wait_ready(act, use)
                        nc.scalar.activation(dst, psum[:, use.bank, 0:w], ACT.Copy).then_inc(psum_read[use.bank], 1)
                elif kind == "idx":
                    h, use = a["h"], a["use"]
                    wait_ready(act, use)
                    if h >= 2:
                        act.wait_ge(score_ready, h - 1)
                    nc.scalar.activation(logit[:, h % 2, :], psum[:, use.bank, 0:SC], ACT.Relu,
                                         scale=IDX_HEADS ** -0.5 * IDX_DIM ** -0.5).then_inc(psum_read[use.bank], 1)
                elif kind == "exp":
                    n_ = a["n"]
                    act.wait_ge(logits_ready, n_ + 1)
                    for t, (b, e) in enumerate(((0, P), (P, SC))):
                        ins = nc.scalar.activation(prob[:, n_ % 4, b:e], logit[:, n_ % 4, b:e], ACT.Exp,
                                                   bias=nmax[:, n_, t:t + 1], accum_out=sums[:, n_, t:t + 1])
                    ins.then_inc(probs_ready, 1)
                elif kind == "probturn":
                    wait_ready(act, a["use"])
                    nc.scalar.activation(probT[:, a["k"] % 2, :], psum[:, a["use"].bank, 0:SC], ACT.Copy)\
                        .then_inc(psum_read[a["use"].bank], 1)
                elif kind == "sb_log":
                    for m in a["pair"]:
                        act.wait_ge(z_ready, m + 1)
                        done = mark(nc.scalar.activation(prob[:, m % 4, :], logit[:, m % 4, :], ACT.Abs))
                    act.wait_ge(act_step, done)
                    for m in a["pair"]:
                        done = mark(nc.scalar.activation(prob[:, m % 4, :], prob[:, m % 4, :], ACT.Exp, scale=-1.0))
                    act.wait_ge(act_step, done)
                    for m in a["pair"]:
                        nc.scalar.activation(prob[:, m % 4, :], prob[:, m % 4, :], ACT.Ln, bias=1.0).then_inc(log_ready, 1)
                elif kind == "sb_arg":
                    m = a["m"]
                    wait_read(act, a["use"])
                    nc.scalar.activation(logit[:, m % 4, :], logit[:, m % 4, :], ACT.Exp).then_inc(weight_ready, 1)
                elif kind == "up":
                    split(a["unit"] + LOOK)
                    c_ = a["c"]
                    for t in range(TT if a["last"] else 0):
                        use = a["uses"][t]
                        wait_ready(act, use)
                        if a["conv"]:
                            nc.scalar.activation(ub[:, c_ % 2, t, :], psum[:, use.bank, :], ACT.Copy)\
                                .then_inc(psum_read[use.bank], 1)
                        else:
                            if c_ == 0:
                                act.wait_ge(rstd_ready, a["stat"]["i"] + 1)
                            nc.scalar.activation(sg[:, c_ % 2, t, :], psum[:, use.bank, 0:FC], ACT.Silu,
                                                 scale=col(a["stat"], "r", t)).then_inc(silu_ready, 1)
                elif kind == "down":
                    if a["part"][0] == 0:
                        split(a["unit"] + LOOK)
                elif kind == "hturn":
                    if not a["conv"]:
                        turned_out(a["uses"][0], a["ti"], None, None, None)
                        continue
                    for half in (1, 0):
                        use = a["uses"][half]
                        wait_ready(act, use)
                        for i in range(2):
                            f = 2 * half + i
                            tile = half * (CONV // 2) + 2 * a["c"] + i
                            nc.scalar.activation(cv[:, f * S:(f + 1) * S], psum[:, use.bank, i * S:(i + 1) * S],
                                                 ACT.Identity, scale=conv_c[:, 2 * CONV + tile:2 * CONV + tile + 1],
                                                 bias=conv_c[:, 3 * CONV + tile:3 * CONV + tile + 1])\
                                .then_inc(conv_first, 1)
                    wait_read(act, a["uses"][1])
                    nc.scalar.activation(gg, cv[:, 2 * S:4 * S], ACT.Gelu_apprx_tanh).then_inc(gelu_ready, 1)

        @block.vector
        def _(dve):
            n = [0]

            def mark(ins):
                ins.then_inc(dve_step, 1)
                n[0] += 1
                return n[0]

            def link(ins):
                dve.wait_ge(dve_step, mark(ins))

            def split(s):
                if s >= len(units):
                    return
                dve.wait_ge(hi_ready, s + 1)
                nc.vector.tensor_tensor(unit_view(w_lo, s % SPLIT, s), unit_view(raw, raw_slot["w", s], s),
                                        unit_view(w_hi, s % SPLIT, s).bitcast(F32), ALU.subtract).then_inc(lo_ready, 1)

            def split_group(dst_hi, dst_lo, src):
                link(nc.vector.tensor_copy(dst_hi, src))
                nc.vector.tensor_tensor(dst_lo, src, dst_hi.bitcast(F32), ALU.subtract).then_inc(split_done, 1)

            def rms(st, size, factor=1.0):
                ss, v, t, r = (stat[:, st[k][0]:st[k][1]] for k in ("ss", "v", "t", "r"))
                link(nc.vector.tensor_scalar(v, ss, 1.0 / (size * factor * factor), EPS / (factor * factor), ALU.mult,
                                             ALU.add))
                link(nc.vector.tensor_scalar(t.bitcast(I32), v.bitcast(I32), 1, None, ALU.logical_shift_right))
                link(nc.vector.tensor_scalar(r.bitcast(I32), t.bitcast(I32), -1.0, float(0x5F3759DF), ALU.mult, ALU.add))
                link(nc.vector.tensor_tensor(t, r, r, ALU.mult))
                link(nc.vector.tensor_tensor(t, t, v, ALU.mult))
                link(nc.vector.scalar_tensor_tensor(t, t, -10.0 / 3.0, t, ALU.add, ALU.mult))
                link(nc.vector.scalar_tensor_tensor(r, t, 5.0, r, ALU.add, ALU.mult))
                link(nc.vector.tensor_tensor(t, r, r, ALU.mult))
                link(nc.vector.scalar_tensor_tensor(t, t, -0.5 * (3.0 / 8.0) ** 3, v, ALU.mult, ALU.mult))
                ins = nc.vector.scalar_tensor_tensor(r, t, 1.5 * 3.0 / 8.0, r, ALU.add, ALU.mult)
                ins.then_inc(rstd_ready, 1)
                dve.wait_ge(rstd_ready, st["i"] + 1)

            x_v = [0]
            for kind, a in steps:
                if kind == "vectors":
                    for use, dst, w in ((a["uses"][0], cols[:, :], NV), (a["uses"][1], ada_b[:, :], 48),
                                        (a["uses"][2], conv_c[:, 0:88], 88), (a["uses"][3], conv_c[:, 88:176], 88)):
                        wait_ready(dve, use)
                        ins = nc.vector.tensor_copy(dst, psum[:, use.bank, 0:w])
                        ins.then_inc(psum_read[use.bank], 1)
                    for use in a["uses"]:
                        wait_read(dve, use)
                elif kind == "lambda":
                    dve.wait_ge(small_loaded, 32)
                    link(nc.vector.tensor_tensor(work[:, 0:2 * HD].rearrange("p (a n) -> p a n", a=2),
                                                 lam_in[:, 0::2, :], lam_in[:, 1::2, :], ALU.mult))
                    nc.vector.tensor_reduce(lam[:, 0:2], work[:, 0:2 * HD].rearrange("p (a n) -> p a n", a=2), AX.X,
                                            ALU.add).then_inc(lam_dots, 1)
                elif kind == "prime":
                    for s in a["units"]:
                        split(s)
                elif kind == "ada":
                    what = ("a", a["unit"])
                    acc = ada_acc[:, a["n"] % 2, :]
                    dve.wait_ge(weight_loaded[raw_slot[what]], landed[what])
                    if a["n"] == 0 and a["part"] == 0:
                        dve.wait_ge(c_act_ready, 1)
                    if a["part"] == 0 and a["slot_free"] is not None:
                        wait_ready(dve, a["slot_free"])
                    for k in range(a["tiles"]):
                        kk = 4 * a["part"] + k
                        w = raw[:, raw_slot[what], k * BANK:(k + 1) * BANK]
                        if kk == 0:
                            ins = nc.vector.tensor_scalar(acc, w, c_act[:, 0:1], None, ALU.mult)
                        else:
                            ins = nc.vector.scalar_tensor_tensor(acc, w, c_act[:, kk:kk + 1], acc, ALU.mult, ALU.add)
                        if k < a["tiles"] - 1:
                            link(ins)
                    ins.then_inc(ada_used, 1)
                    dve.wait_ge(ada_used, a["done"])
                elif kind == "adasum":
                    use, half = a["use"], a["n"] % 2
                    wait_ready(dve, use)
                    if a["gate"] is not None:
                        dst = gate_rows[:, a["gate"], half * BANK:(half + 1) * BANK]
                        dve.wait_ge(gate_bias_loaded, 32)
                        nc.vector.tensor_tensor(dst, psum[:, use.bank, :], dst, ALU.add).then_inc(psum_read[use.bank], 1)
                    else:
                        cols4, bias4 = mod[:, a["vec"], 4 * half:4 * half + 4], ada_b[:, 4 * a["n"]:4 * a["n"] + 4]
                        if a["unit"] is not None:
                            link(nc.vector.tensor_tensor(cols4, psum[:, use.bank, 4:8], bias4, ALU.add))
                            bias4 = cols4
                        nc.vector.tensor_tensor(cols4, psum[:, use.bank, 0:4], bias4, ALU.add)\
                            .then_inc(psum_read[use.bank], 1)
                    wait_read(dve, use)
                elif kind == "modfinal":
                    nc.vector.scalar_tensor_tensor(mod[:, a["vec"], :], mod[:, a["vec"], :], 1.0,
                                                   cols[:, a["gain"]:a["gain"] + KT], ALU.add, ALU.mult)\
                        .then_inc(mod_final, 1)
                elif kind == "stats":
                    st = a["st"]
                    if a["after"][0] == "x_ready":
                        dve.wait_ge(squares_ready, st["squares"] + 2 * TT)
                        ss, ss2 = stat[:, st["ss"][0]:st["ss"][1]], stat[:, st["ss2"][0]:st["ss2"][1]]
                        link(nc.vector.tensor_tensor(ss, ss, ss2, ALU.add))
                    else:
                        dve.wait_ge(squares_ready, st["squares"] + TT)
                    rms(st, D)
                elif kind == "normalise":
                    for half in range(2):
                        cs = slice(half * BANK, (half + 1) * BANK)
                        for t in range(TT):
                            ins = nc.vector.tensor_scalar(scr[:, t, cs], X[:, t, cs], col(a["st"], "r", t), None, ALU.mult)
                            if t == 0:
                                mark(ins)
                        ins.then_inc(scr_ready, 1)
                    dve.wait_ge(dve_step, n[0])
                elif kind == "turn":
                    if a["read_before"] is not None:
                        dve.wait_ge(unit_used, a["read_before"] + 1)
                    dve.wait_ge(turned_ready, a["ti"] + 1)
                    k = a["kt"]
                    split_group(hT_hi[:, k:k + 2, :].rearrange("p k n -> p (k n)"),
                                hT_lo[:, k:k + 2, :].rearrange("p k n -> p (k n)"), turned[:, a["ti"] % 2, :])
                elif kind == "proj" or kind == "down" and a["part"][0] == 0:
                    split(a["unit"] + LOOK)
                elif kind == "rope":
                    c0, nh, dim, tab = a["col"], a["heads"], a["dim"], (r64 if a["dim"] == HD else r32)
                    w = nh * dim
                    for use in a["uses"]:
                        wait_read(dve, use)
                    dve.wait_ge(consts_loaded, 16)
                    if a["i"]:
                        dve.wait_ge(rope_ready, a["i"])
                    for t in range(TT):
                        xs = pr[:, t, c0:c0 + w].rearrange("p (h d) -> p h d", h=nh)
                        cs = tab[:, t, 0:dim][:, None, :].to_broadcast([P, nh, dim])
                        link(nc.vector.tensor_tensor(scr[:, t, 0:w].rearrange("p (h d) -> p h d", h=nh), xs, cs, ALU.mult))
                    dve.wait_ge(rope_swapped, a["i"] + 1)
                    ins = nc.vector.tensor_tensor(pr[:, :, c0:c0 + w], scr[:, :, 0:w], scr[:, :, BANK:BANK + w], ALU.add)
                    if a["replicate"]:
                        link(ins)
                        key = pr[:, :, c0 + 256:c0 + 288][:, :, None, :].to_broadcast([P, TT, 4, IDX_DIM])
                        ins = nc.vector.tensor_copy(work[:, 0:TT * P].rearrange("p (t r d) -> p t r d", t=TT, r=4), key)
                    ins.then_inc(rope_ready, 1)
                elif kind == "idx":
                    h, use = a["h"], a["use"]
                    wait_read(dve, use)
                    for t, (b, e) in enumerate(((0, P), (P, SC))):
                        wcol = pr[:, t, 6 * BANK + 288 + h:6 * BANK + 289 + h]
                        before = chunk_mask if h == 0 else selbias
                        ins = nc.vector.scalar_tensor_tensor(selbias[:, b:e], logit[:, h % 2, b:e], wcol, before[:, b:e],
                                                             ALU.mult, ALU.add)
                        if t == 0:
                            link(ins)
                    ins.then_inc(score_ready, 1)
                    dve.wait_ge(score_ready, h + 1)
                elif kind == "topk":
                    if a["j"] == 0:
                        link(nc.vector.tensor_copy(work[:, :], selbias[:, :]))
                    tiles = ((0, P), (P, SC))
                    for t, (b, e) in enumerate(tiles):
                        m = mark(nc.vector.max(top[:, 8 * t:8 * t + 8], work[:, b:e]))
                    dve.wait_ge(dve_step, m)
                    for t, (b, e) in enumerate(tiles):
                        m = mark(nc.vector.match_replace(work[:, b:e], top[:, 8 * t:8 * t + 8], work[:, b:e], NEG))
                    dve.wait_ge(dve_step, m)
                    if a["j"] == TOPK // 8 - 1:
                        link(nc.vector.tensor_scalar(work[:, :], work[:, :], NEG, -NEG, ALU.is_equal, ALU.mult))
                        nc.vector.scalar_tensor_tensor(selbias[:, :], work[:, :], NEG, chunk_mask, ALU.add, ALU.add)\
                            .then_inc(selected, 1)
                        dve.wait_ge(selected, 1)
                elif kind == "qk":
                    n_, h, use, bias = a["n"], a["h"], a["use"], a["bias"]
                    wait_ready(dve, use)
                    s_, lg = psum[:, use.bank, 0:SC], logit[:, n_ % 4, :]
                    if bias in rel_bias_rows:
                        if h == 0:
                            which = ("moba", "odd0", "odd1").index(bias)
                            dve.wait_ge(bias_loaded[which], 16 if which == 0 else 32)
                            if which:
                                dve.wait_ge(bias_cleared, which)
                        rows = rel_bias_rows[bias](h)
                        mark(nc.vector.scalar_tensor_tensor(lg[:, 0:P], s_[:, 0:P], SCALE, rows[:, P - 1::-1],
                                                            ALU.mult, ALU.add))
                        nc.vector.scalar_tensor_tensor(lg[:, P:SC], s_[:, P:SC], SCALE, rows[:, S - 1::-1],
                                                       ALU.mult, ALU.add).then_inc(psum_read[use.bank], 1)
                    else:
                        nc.vector.scalar_tensor_tensor(lg, s_, SCALE, chunk_mask if bias == "mask" else selbias[:, :],
                                                       ALU.mult, ALU.add).then_inc(psum_read[use.bank], 1)
                    wait_read(dve, use)
                    mark(nc.vector.tensor_reduce(nmax[:, n_, 0:1], lg[:, 0:P], AX.X, ALU.max, negate=True))
                    nc.vector.tensor_reduce(nmax[:, n_, 1:2], lg[:, P:SC], AX.X, ALU.max, negate=True)\
                        .then_inc(logits_ready, 1)
                elif kind == "mix":
                    n_ = a["n"]
                    dve.wait_ge(probs_ready, n_ + 1)
                    if n_ == 9:
                        dve.wait_ge(lam_exp, 1)
                        link(nc.vector.tensor_scalar(lam[:, 2:3], lam[:, 1:2], lam[:, 0:1], -LAMBDA_INIT, ALU.subtract,
                                                     ALU.add))
                    link(nc.vector.reciprocal(rsum[:, n_ - 1:n_ + 1, :], sums[:, n_ - 1:n_ + 1, :]))
                    link(nc.vector.tensor_scalar(rsum[:, n_, :], rsum[:, n_, :], lam[:, 2:3], None, ALU.mult))
                    for t, (b, e) in enumerate(((0, P), (P, SC))):
                        m = mark(nc.vector.tensor_scalar(prob[:, n_ % 4, b:e], prob[:, n_ % 4, b:e], rsum[:, n_, t:t + 1],
                                                         None, ALU.mult))
                    dve.wait_ge(dve_step, m)
                    for t, (b, e) in enumerate(((0, P), (P, SC))):
                        ins = nc.vector.scalar_tensor_tensor(prob[:, (n_ - 1) % 4, b:e], prob[:, (n_ - 1) % 4, b:e],
                                                             rsum[:, n_ - 1, t:t + 1], prob[:, n_ % 4, b:e],
                                                             ALU.mult, ALU.add)
                        if t == 0:
                            mark(ins)
                    ins.then_inc(mixed_ready, 1)
                elif kind == "oevac":
                    buf, c0 = bufs[a["dst"][0]], a["dst"][1]
                    if a["mode"] == "norm":
                        n0 = a["n0"]
                        dve.wait_ge(probs_ready, n0 + 8)
                        link(nc.vector.reciprocal(rsum[:, n0:n0 + 8, :], sums[:, n0:n0 + 8, :]))
                    for t in range(TT):
                        use = a["uses"][t]
                        wait_ready(dve, use)
                        if a["mode"] == "norm":
                            ins = nc.vector.tensor_tensor(
                                buf[:, t, c0:c0 + BANK].rearrange("p (h d) -> p h d", d=HD),
                                psum[:, use.bank, :].rearrange("p (h d) -> p h d", d=HD),
                                rsum[:, n0:n0 + 8, t:t + 1].to_broadcast([P, 8, HD]), ALU.mult)
                        else:
                            ins = nc.vector.tensor_copy(buf[:, t, c0:c0 + BANK], psum[:, use.bank, :])
                        if a["final"] and t == 1:
                            ins.then_inc(scr_ready, 1)
                        else:
                            ins.then_inc(psum_read[use.bank], 1)
                            wait_read(dve, use)
                elif kind == "diffnorm":
                    st = a["st"]
                    for t in range(TT):
                        wait_read(dve, a["uses"][t])
                        s0 = st["ss"][0] + 4 * t
                        m = mark(nc.vector.tensor_reduce(stat[:, s0:s0 + 4],
                                                         scr[:, t, BANK:D].rearrange("p (h d) -> p h d", h=4), AX.X,
                                                         ALU.add))
                    dve.wait_ge(dve_step, m)
                    rms(st, 2 * HD)
                    for t in range(TT):
                        o = scr[:, t, 0:BANK].rearrange("p (h d) -> p h d", h=4)
                        r0 = st["r"][0] + 4 * t
                        link(nc.vector.tensor_tensor(o, o, stat[:, r0:r0 + 4][:, :, None].to_broadcast([P, 4, P]),
                                                     ALU.mult))
                        ins = nc.vector.scalar_tensor_tensor(o, o, 1.0 - LAMBDA_INIT,
                                                             subln[:, None, :].to_broadcast([P, 4, P]), ALU.mult, ALU.mult)
                        if t == 0:
                            link(ins)
                    ins.then_inc(scr_ready, 1)
                    dve.wait_ge(scr_ready, a["v"])
                elif kind == "sb_z":
                    use = a["use"]
                    wait_ready(dve, use)
                    nc.vector.tensor_scalar(logit[:, a["m"] % 4, :], psum[:, use.bank, 0:SC], SCALE, None, ALU.mult)\
                        .then_inc(z_ready, 1)
                elif kind == "sb_keep":
                    m_ = a["m"]
                    z, l = logit[:, m_ % 4, :], prob[:, m_ % 4, :]
                    dve.wait_ge(log_ready, m_ + 1)
                    dve.wait_ge(consts_loaded, 16)
                    link(nc.vector.scalar_tensor_tensor(l, z, 0.0, l, ALU.max, ALU.add))
                    nc.vector.tensor_tensor(probT[:, m_ % 2, :], l, minus_past, ALU.mult).then_inc(log_keep_ready, 1)
                elif kind == "sb_arg":
                    m_, use = a["m"], a["use"]
                    wait_ready(dve, use)
                    nc.vector.tensor_tensor(logit[:, m_ % 4, :], psum[:, use.bank, 0:SC], logit[:, m_ % 4, :], ALU.add)\
                        .then_inc(psum_read[use.bank], 1)
                elif kind == "mixbranch":
                    half = a["n"]
                    for t in range(TT):
                        ya, yb = a["ya"][t], a["yb"][t]
                        dst = scr[:, t, half * BANK:(half + 1) * BANK]
                        tmp = prob[:, :, :].rearrange("p a n -> p (a n)")[:, t * BANK:(t + 1) * BANK]
                        wait_ready(dve, ya)
                        nc.vector.scalar_tensor_tensor(dst, pr[:, t, half * BANK:(half + 1) * BANK], 1.0,
                                                       psum[:, ya.bank, :], ALU.add, ALU.mult)\
                            .then_inc(psum_read[ya.bank], 1)
                        wait_ready(dve, yb)
                        nc.vector.scalar_tensor_tensor(tmp, pr[:, t, (3 + half) * BANK:(4 + half) * BANK], 1.0,
                                                       psum[:, yb.bank, :], ALU.add, ALU.mult)\
                            .then_inc(psum_read[yb.bank], 1)
                        wait_read(dve, ya)
                        wait_read(dve, yb)
                        ins = nc.vector.tensor_tensor(dst, dst, tmp, ALU.add)
                        if t == 1:
                            ins.then_inc(scr_ready, 1)
                        else:
                            link(ins)
                elif kind == "up":
                    split(a["unit"] + LOOK)
                    if not a["conv"] and a["last"]:
                        c_ = a["c"]
                        for t in range(TT):
                            use = a["uses"][t]
                            dve.wait_ge(silu_ready, TT * a["ci"] + t + 1)
                            nc.vector.scalar_tensor_tensor(hid[:, c_ % 2, t, :], psum[:, use.bank, FC:2 * FC],
                                                           col(a["stat"], "r", t), sg[:, c_ % 2, t, :],
                                                           ALU.mult, ALU.mult).then_inc(psum_read[use.bank], 1)
                elif kind == "hturn":
                    if a["down_before"] is not None:
                        dve.wait_ge(unit_used, a["down_before"] + 1)
                    hi, lo = hc_hi[:, a["c"] % 2, :], hc_lo[:, a["c"] % 2, :]
                    if not a["conv"]:
                        dve.wait_ge(turned_ready, a["ti"] + 1)
                        split_group(hi, lo, turned[:, a["ti"] % 2, :])
                        continue
                    done = 0
                    for half in (1, 0):
                        use = a["uses"][half]
                        dve.wait_ge(conv_first, 4 * a["cc"] + (2 if half else 4))
                        for tap, shift in ((1, 1), (0, 2)):
                            for i in range(2):
                                f, tile = 2 * half + i, half * (CONV // 2) + 2 * a["c"] + i
                                v = cv[:, f * S + shift:(f + 1) * S]
                                ins = nc.vector.scalar_tensor_tensor(
                                    v, psum[:, use.bank, i * S:(i + 1) * S - shift],
                                    conv_c[:, tap * CONV + tile:tap * CONV + tile + 1], v, ALU.mult, ALU.add)
                                if tap == 1 or i == 0:
                                    m = mark(ins)
                            if tap == 1:
                                dve.wait_ge(dve_step, m)
                        ins.then_inc(psum_read[use.bank], 1)
                    wait_read(dve, a["uses"][0])
                    dve.wait_ge(dve_step, m)
                    dve.wait_ge(gelu_ready, a["cc"] + 1)
                    link(nc.vector.tensor_tensor(hfull, gg, cv[:, 0:2 * S], ALU.mult))
                    split_group(hi, lo, hfull)
                elif kind == "post":
                    norm = a["mode"] == "norm"
                    if norm:
                        dve.wait_ge(g_row_loaded, 16 * (a["row"] + 1))
                    for j in range(2 * TT):
                        half, t = j // TT, j % TT
                        use = a["uses"][2 * t + half]
                        cs = slice(half * BANK, (half + 1) * BANK)
                        if norm:
                            dve.wait_ge(squares_ready, a["st"]["squares"] + j + 1)
                        else:
                            wait_ready(dve, use)
                        rows = g_row[:, cs] if norm else gate_rows[:, a["gate"], cs]
                        nc.vector.tensor_tensor(scr[:, t, cs], psum[:, use.bank, :], rows, ALU.mult)\
                            .then_inc(psum_read[use.bank], 1)
                        if not norm and t == TT - 1:
                            for u in range(TT):
                                wait_read(dve, a["uses"][2 * u + half])
                                ins = nc.vector.tensor_tensor(X[:, u, cs], scr[:, u, cs], X[:, u, cs], ALU.add)
                                if u == 0:
                                    mark(ins)
                            ins.then_inc(x_ready, 1)
                    if norm:
                        st = a["st"]
                        ss, ss2 = stat[:, st["ss"][0]:st["ss"][1]], stat[:, st["ss2"][0]:st["ss2"][1]]
                        link(nc.vector.tensor_tensor(ss, ss, ss2, ALU.add))
                        rms(st, D, a["factor"])
                        for use in a["uses"]:
                            wait_read(dve, use)
                    for half in range(2 if norm else 0):
                        for t in range(TT):
                            cs = slice(half * BANK, (half + 1) * BANK)
                            ins = nc.vector.scalar_tensor_tensor(X[:, t, cs], scr[:, t, cs], col(a["st"], "r", t),
                                                                 X[:, t, cs], ALU.mult, ALU.add)
                            if t == 0:
                                mark(ins)
                        ins.then_inc(x_ready, 1)
                    x_v[0] += 2
                    dve.wait_ge(dve_step, n[0])
                    dve.wait_ge(x_ready, x_v[0])
                    if norm:
                        nc.vector.memset(top[:, 0:1], 0.0).then_inc(g_row_used, 1)
                elif kind == "finalnorm":
                    dve.wait_ge(g_row_loaded, 16 * (a["row"] + 1))
                    for half in range(2):
                        cs = slice(half * BANK, (half + 1) * BANK)
                        for t in range(TT):
                            ins = nc.vector.scalar_tensor_tensor(X[:, t, cs], X[:, t, cs], col(a["st"], "r", t),
                                                                 g_row[:, cs], ALU.mult, ALU.mult)
                            if t == 0:
                                mark(ins)
                        ins.then_inc(x_ready, 1)
                    x_v[0] += 2
                    dve.wait_ge(dve_step, n[0])
                    dve.wait_ge(x_ready, x_v[0])
                    nc.vector.memset(top[:, 0:1], 0.0).then_inc(g_row_used, 1)

        @block.tensor
        def _(pe):
            split_seen = [0]

            def need_group(g):
                if g + 1 > split_seen[0]:
                    pe.wait_ge(split_done, g + 1)
                    split_seen[0] = g + 1

            def need_unit(u):
                pe.wait_ge(hi_ready, u + 1)
                pe.wait_ge(lo_ready, u + 1)

            def product(o, a_hi, a_lo, b_hi, b_lo, start, stop):
                nc.tensor.matmul(o, a_hi, b_hi, start=start, stop=False)
                nc.tensor.matmul(o, a_hi, b_lo, start=False, stop=False)
                return nc.tensor.matmul(o, a_lo, b_hi, start=False, stop=stop)

            def chunk(a, k_tiles, k_base=0):
                s, k0, outs = a["unit"], a["k0"], a["uses"]
                if k0 == 0:
                    for use in outs:
                        wait_free(pe, use)
                need_unit(s)
                nk, w, _ = units[s]
                for k in range(nk):
                    kk = k_base + k0 + k
                    need_group(a["g0"] + kk // 2)
                    for t in range(TT):
                        sl = slice(t * P, (t + 1) * P)
                        b = slice(k * w, (k + 1) * w)
                        ins = product(psum[:, outs[t].bank, 0:w], hT_hi[:, kk, sl], hT_lo[:, kk, sl],
                                      w_hi[:, s % SPLIT, b], w_lo[:, s % SPLIT, b],
                                      k0 + k == 0, k0 + k == k_tiles - 1)
                ins.then_inc(unit_used, 1)

            for kind, a in steps:
                if kind == "condition":
                    pe.wait_ge(c_loaded, 16)
                    pe.wait_ge(ident_loaded, 16)
                    nc.tensor.transpose(psum[:, a["use"].bank, 0:KT], c_rows[:, :], ident[0:KT, 0:KT])\
                        .then_inc(psum_ready[a["use"].bank], 1)
                elif kind == "vectors":
                    pe.wait_ge(vectors_loaded, 16 * 7)
                    for i, (use, w) in enumerate(zip(a["uses"], (NV, 48, 88, 88))):
                        nc.tensor.transpose(psum[:, use.bank, 0:w], PR[0:w, i * P:(i + 1) * P], ident[0:w, 0:w])\
                            .then_inc(psum_ready[use.bank], 1)
                elif kind == "adasum":
                    use = a["use"]
                    acc = ada_acc[:, a["n"] % 2, :]
                    wait_free(pe, use)
                    if a["unit"] is not None:
                        what = ("a", a["unit"])
                        pe.wait_ge(weight_loaded[raw_slot[what]], landed[what])
                        pe.wait_ge(c_act_ready, 1)
                        w = raw[:, raw_slot[what], :]
                        for j in range(4):
                            for k in (2, 3):
                                nc.tensor.matmul(psum[:, use.bank, 4 + j:5 + j],
                                                 w[:, k * BANK + j * P:k * BANK + (j + 1) * P],
                                                 c_act[:, 4 + k:5 + k], start=k == 2, stop=k == 3)
                    pe.wait_ge(ada_used, a["done"])
                    pe.wait_ge(ones_ready, 1)
                    if a["gate"] is not None:
                        ins = nc.tensor.matmul(psum[:, use.bank, :], ones[:, :], acc, start=True, stop=True)
                    else:
                        for j in range(4):
                            ins = nc.tensor.matmul(psum[:, use.bank, j:j + 1], acc[:, j * P:(j + 1) * P],
                                                   ones[:, 0:1], start=True, stop=True)
                    ins.then_inc(psum_ready[use.bank], 1)
                elif kind == "turn":
                    use, src = a["use"], bufs[a["src"]]
                    wait_free(pe, use)
                    if a["after"] and a["after"][0] == "uses":
                        for u in a["after"][1]:
                            wait_read(pe, u)
                    elif a["after"]:
                        pe.wait_ge(named[a["after"][0]], a["after"][1])
                    for i in range(2):
                        for t in range(TT):
                            k = a["kt"] + i
                            ins = nc.tensor.transpose(psum[:, use.bank, i * S + t * P:i * S + (t + 1) * P],
                                                      src[:, t, k * P:(k + 1) * P], ident)
                    ins.then_inc(psum_ready[use.bank], 1)
                elif kind == "proj":
                    chunk(a, a["k_tiles"], a["k_base"])
                elif kind == "headturn":
                    use = a["use"]
                    wait_free(pe, use)
                    if a["after"][0] == "uses":
                        for u in a["after"][1]:
                            wait_read(pe, u)
                    else:
                        pe.wait_ge(rope_ready, a["after"][1])
                    for i in range(2):
                        for t in range(TT):
                            c0 = a["col"] + i * P
                            ins = nc.tensor.transpose(psum[:, use.bank, i * S + t * P:i * S + (t + 1) * P],
                                                      pr[:, t, c0:c0 + P], ident)
                    ins.then_inc(psum_ready[use.bank], 1)
                elif kind == "idxturn":
                    pe.wait_ge(rope_ready, a["after"][1])
                    use = a["uses"][0]
                    wait_free(pe, use)
                    for i in range(2):
                        for t in range(TT):
                            c0 = 6 * BANK + i * P
                            ins = nc.tensor.transpose(psum[:, use.bank, i * S + t * P:i * S + (t + 1) * P],
                                                      pr[:, t, c0:c0 + P], ident)
                    ins.then_inc(psum_ready[use.bank], 1)
                    use = a["uses"][1]
                    wait_free(pe, use)
                    for t in range(TT):
                        ins = nc.tensor.transpose(psum[:, use.bank, t * P:(t + 1) * P], work[:, t * P:(t + 1) * P], ident)
                    ins.then_inc(psum_ready[use.bank], 1)
                    for use in a["uses"]:
                        wait_read(pe, use)
                elif kind == "idx":
                    h, use = a["h"], a["use"]
                    wait_free(pe, use)
                    p0, b = IDX_DIM * (h % 4), h // 4
                    q, k = IT[p0:p0 + IDX_DIM, b, :], IT[p0:p0 + IDX_DIM, 2, :]
                    nc.tensor.matmul(psum[:, use.bank, 0:P], q[:, 0:P], k[:, 0:P], start=True, stop=True)
                    nc.tensor.matmul(psum[:, use.bank, P:SC], q[:, P:S], k[:, 0:S], start=True, stop=True)\
                        .then_inc(psum_ready[use.bank], 1)
                elif kind in ("qk", "sb_z"):
                    use = a["use"]
                    h, base = (a["h"], a["base"]) if kind == "qk" else (a["m"], 8)
                    for u in a["ready"]:
                        wait_read(pe, u)
                    wait_free(pe, use)
                    p0 = HD * (h % 2)
                    q, k = QK[p0:p0 + HD, base + h // 2, :], QK[p0:p0 + HD, base + 4 + h // 2, :]
                    if kind == "qk":
                        nc.tensor.matmul(psum[:, use.bank, 0:P], q[:, 0:P], k[:, 0:P], start=True, stop=True)
                        ins = nc.tensor.matmul(psum[:, use.bank, P:SC], q[:, P:S], k[:, 0:S], start=True, stop=True)
                    else:
                        nc.tensor.matmul(psum[:, use.bank, 0:S], k[:, 0:P], q[:, 0:S], start=True, stop=True)
                        ins = nc.tensor.matmul(psum[:, use.bank, S:SC], k[:, P:S], q[:, P:S], start=True, stop=True)
                    ins.then_inc(psum_ready[use.bank], 1)
                elif kind == "probturn":
                    n_, use = a["n"], a["use"]
                    wait_free(pe, use)
                    if a["diff"]:
                        pe.wait_ge(mixed_ready, (n_ - 7) // 2)
                        src = prob[:, (n_ - 1) % 4, :]
                    else:
                        pe.wait_ge(probs_ready, n_ + 1)
                        src = prob[:, n_ % 4, :]
                    for b in range(3):
                        ins = nc.tensor.transpose(psum[:, use.bank, b * P:(b + 1) * P], src[:, b * P:(b + 1) * P], ident)
                    ins.then_inc(psum_ready[use.bank], 1)
                elif kind in ("pv", "sb_pv"):
                    if kind == "pv":
                        if a["first"]:
                            for u in a["v_ready"]:
                                wait_read(pe, u)
                            for u in a["uses"]:
                                wait_free(pe, u)
                        wait_read(pe, a["turned"])
                        pT, w, o0, last = probT[:, a["k"] % 2, :], a["w"], a["slot"] * a["w"], a["last"]
                    else:
                        m = a["m"]
                        if m == 0:
                            for u in a["v_ready"]:
                                wait_read(pe, u)
                            for u in a["uses"]:
                                wait_free(pe, u)
                        pe.wait_ge(weight_masked, m + 1)
                        pT, w, o0, last = logit[:, m % 4, :], HD, m * HD, m == 7
                    vc = a["v"]
                    b0, b1 = a["uses"][0].bank, a["uses"][1].bank
                    ins = nc.tensor.matmul(psum[:, b0, o0:o0 + w], pT[:, 0:P], pr[:, 0, vc:vc + w], start=True, stop=True)
                    if last:
                        ins.then_inc(psum_ready[b0], 1)
                    nc.tensor.matmul(psum[:, b1, o0:o0 + w], pT[:, P:2 * P], pr[:, 0, vc:vc + w], start=True, stop=False)
                    ins = nc.tensor.matmul(psum[:, b1, o0:o0 + w], pT[:, 2 * P:SC], pr[:, 1, vc:vc + w], start=False,
                                           stop=True)
                    if last:
                        ins.then_inc(psum_ready[b1], 1)
                elif kind == "sb_cum":
                    m, use = a["m"], a["use"]
                    wait_free(pe, use)
                    pe.wait_ge(log_keep_ready, m + 1)
                    pe.wait_ge(consts_loaded, 16)
                    pe.wait_ge(ones_ready, 1)
                    lk, o = probT[:, m % 2, :], psum[:, use.bank, :]
                    nc.tensor.matmul(o[:, 0:S], later, lk[:, 0:S], start=True, stop=False)
                    nc.tensor.matmul(o[:, P:S], ones[:, :], lk[:, S:SC], start=False, stop=True)
                    nc.tensor.matmul(o[:, S:SC], later, lk[:, S:SC], start=True, stop=True)\
                        .then_inc(psum_ready[use.bank], 1)
                elif kind == "up":
                    chunk(a, KT)
                elif kind == "hturn":
                    for use in a["uses"]:
                        wait_free(pe, use)
                    for use in a["ups"]:
                        wait_read(pe, use)
                    src = (ub if a["conv"] else hid)[:, a["c"] % 2]
                    for i, use in enumerate(a["uses"]):
                        for f in range(2):
                            for t in range(TT):
                                c0 = (2 * i + f) * P
                                ins = nc.tensor.transpose(psum[:, use.bank, f * S + t * P:f * S + (t + 1) * P],
                                                          src[:, t, c0:c0 + P], ident)
                        ins.then_inc(psum_ready[use.bank], 1)
                elif kind == "down":
                    c_, u = a["c"], a["unit"]
                    need_unit(u)
                    need_group(a["g"])
                    if c_ == 0:
                        for use in a["uses"]:
                            wait_free(pe, use)
                    order = [(k, t, half) for k in range(2) for t in range(TT) for half in range(2)]
                    if c_ == NFC - 1:
                        order = [(k, t, half) for half in range(2) for k in range(2) for t in range(TT)]
                    for k, t, half in order[a["part"][0]:a["part"][1]]:
                        sl = slice(k * S + t * P, k * S + (t + 1) * P)
                        b = slice(k * D + half * BANK, k * D + (half + 1) * BANK)
                        use = a["uses"][2 * t + half]
                        ins = product(psum[:, use.bank, :], hc_hi[:, c_ % 2, sl], hc_lo[:, c_ % 2, sl],
                                      w_hi[:, u % SPLIT, b], w_lo[:, u % SPLIT, b],
                                      c_ == 0 and k == 0, c_ == NFC - 1 and k == 1)
                        if c_ == NFC - 1 and k == 1 and use.unit is None:
                            ins.then_inc(psum_ready[use.bank], 1)
                    if a["part"][1] == 8:
                        ins.then_inc(unit_used, 1)


_INS = ["x", "c", "w_ada", "b_ada", "g_mix", "w_in", "w_br_moba", "w_br_sb", "w_out", "rel_bias", "g_ffn", "w_up",
        "w_conv", "b_conv", "w_down", "g_final", "norm_g_2", "ffn_wg_2", "ffn_wu_2", "ffn_wd_2", "even_w_in_2",
        "even_w_out_2", "even_lambda_2", "even_subln_2", "odd_w_in_2", "odd_w_out_2", "odd_rel_bias_2"]


def kernel(**inputs):
    import concourse.bacc as bacc
    from concourse.bass_utils import run_bass_kernel_spmd

    nc = bacc.Bacc("TRN2", target_bir_lowering=False, num_devices=1)
    arrays, args = {}, []
    for name, a in [("consts", constants())] + [(name, inputs[name]) for name in _INS]:
        a = np.ascontiguousarray(a)
        arrays[f"in_{name}_dram"] = a
        args.append(nc.dram_tensor(f"in_{name}_dram", a.shape, mybir.dt.from_np(a.dtype), kind="ExternalInput").ap())
    args.append(nc.dram_tensor("distance_table", (8, BIAS_T), F32, kind="Internal").ap())
    args.append(nc.dram_tensor("out_0_dram", (1, S, D), F32, kind="ExternalOutput").ap())
    program(nc, *args)
    r = run_bass_kernel_spmd(nc, [arrays], core_ids=[0])
    return r.results[0]["out_0_dram"]
```
